# Optimizing a Trainium2 kernel written in Bass

```python
import jax
import jax.numpy as jnp
from jax import lax
import numpy as np

D_MODEL = 1024
BATCH = 1
SEQ = 512
DEPTH = 2

CTX_LEN = 256
GRID_W = 64

M_HEADS = 8
M_HEAD_DIM = 128
M_WIDTH = M_HEADS * M_HEAD_DIM
M_CHUNK = 128
M_CONV = 3
M_STAB_INIT = -1e30

S_GROUPS = 8
S_WIDTH = 1024
S_GROUP_DIM = S_WIDTH // S_GROUPS
S_CHUNK = 128

N_KEYS = 128
N_EXPERTS = N_KEYS * N_KEYS
PEER_HEADS = 8
PEER_TOPK = 16
PEER_QDIM = 256
PEER_HALF = PEER_QDIM // 2
PEER_BLOCK = 128

N_GATES = 4 * M_HEADS
IN_SPLITS = (2 * M_WIDTH, 3 * M_WIDTH, 4 * M_WIDTH, 4 * M_WIDTH + N_GATES,
             4 * M_WIDTH + N_GATES + S_WIDTH, 4 * M_WIDTH + N_GATES + 2 * S_WIDTH,
             4 * M_WIDTH + N_GATES + 2 * S_WIDTH + D_MODEL)
IN_WIDTH = IN_SPLITS[-1] + D_MODEL

DN_ALPHA = (2 * DEPTH) ** 0.25
DN_BETA = (8 * DEPTH) ** -0.25
LN_EPS = 1e-5

kernel_name = 'hybrid_mlstm_sgu_peer_dit'

def _standardize(a):
    af = a.astype(jnp.float32)
    mu = jnp.mean(af, axis=-1, keepdims=True)
    var = jnp.mean(jnp.square(af - mu), axis=-1, keepdims=True)
    return (af - mu) * lax.rsqrt(var + LN_EPS)

def layer_norm(a, w, b):
    return (_standardize(a) * w + b).astype(a.dtype)

def conv_grid(a, w, b, rows):
    B_, T, C = a.shape
    img = a.reshape(B_, rows, GRID_W, C)
    out = lax.conv_general_dilated(img, w[:, :, None, :], window_strides=(1, 1), padding='SAME',
                                   dimension_numbers=('NHWC', 'HWIO', 'NHWC'),
                                   feature_group_count=C)
    return out.reshape(B_, T, C) + b

def conv_seq(a, w_row, b):
    ap = jnp.pad(a, ((0, 0), (1, 1), (0, 0)))
    return ap[:, :-2] * w_row[0] + ap[:, 1:-1] * w_row[1] + ap[:, 2:] * w_row[2] + b

def zero_state(b):
    return (jnp.zeros((b, M_HEADS, M_HEAD_DIM, M_HEAD_DIM), jnp.float32),
            jnp.zeros((b, M_HEADS, M_HEAD_DIM), jnp.float32),
            jnp.full((b, M_HEADS), M_STAB_INIT, jnp.float32))

def mlstm_chunked(q, k, v, log_i, log_f, state):
    B_, H, T, dh = q.shape
    nc = T // M_CHUNK

    def to_chunks(a):
        a = a.reshape(B_, H, nc, M_CHUNK, *a.shape[3:])
        return jnp.moveaxis(a, 2, 0)

    xs = (to_chunks(q), to_chunks(k), to_chunks(v), to_chunks(log_i), to_chunks(log_f))
    tri = jnp.tril(jnp.ones((M_CHUNK, M_CHUNK), dtype=bool))

    def step(carry, inp):
        C, n, m = carry
        qc, kc, vc, ic, fc = inp
        b = jnp.cumsum(fc, axis=-1)
        d = jnp.where(tri, b[..., :, None] - b[..., None, :] + ic[..., None, :], -jnp.inf)
        inter = b + m[..., None]
        m_t = jnp.maximum(inter, jnp.max(d, axis=-1))
        a_t = jnp.exp(inter - m_t)
        s = jnp.einsum('bhtk,bhsk->bhts', qc, kc) * jnp.exp(d - m_t[..., None])
        num = a_t[..., None] * jnp.einsum('bhvk,bhtk->bhtv', C, qc) + jnp.einsum('bhts,bhsv->bhtv', s, vc)
        den = a_t * jnp.einsum('bhk,bhtk->bht', n, qc) + jnp.sum(s, axis=-1)
        h = num / jnp.maximum(jnp.abs(den), jnp.exp(-m_t))[..., None]
        g = b[..., -1]
        dl = g[..., None] - b + ic
        m_new = jnp.maximum(g + m, jnp.max(dl, axis=-1))
        wl = jnp.exp(dl - m_new[..., None])
        a_l = jnp.exp(g + m - m_new)
        C = a_l[..., None, None] * C + jnp.einsum('bhsv,bhsk->bhvk', vc * wl[..., None], kc)
        n = a_l[..., None] * n + jnp.einsum('bhs,bhsk->bhk', wl, kc)
        return (C, n, m_new), h

    final, hs = lax.scan(step, state, xs)
    return jnp.moveaxis(hs, 0, 2).reshape(B_, H, T, dh), final

def mlstm_prepare(qk, v, gates, gate_b):
    B_, T, _ = v.shape

    def heads(a):
        return a.reshape(B_, T, M_HEADS, M_HEAD_DIM).transpose(0, 2, 1, 3).astype(jnp.float32)

    q, k = jnp.split(qk, 2, axis=-1)
    g = (gates + gate_b).astype(jnp.float32).transpose(0, 2, 1)
    i_f, f_f, i_b, f_b = jnp.split(g, 4, axis=1)
    return (heads(q) * M_HEAD_DIM ** -0.5, heads(k), heads(v),
            (i_f, jax.nn.log_sigmoid(f_f)), (i_b, jax.nn.log_sigmoid(f_b)))

def mlstm_bidir(q, k, v, fwd, bwd, state_f, state_b):
    h_f, st_f = mlstm_chunked(q, k, v, fwd[0], fwd[1], state_f)
    rev = lambda a: jnp.flip(a, axis=2)
    h_b, st_b = mlstm_chunked(rev(q), rev(k), rev(v), rev(bwd[0]), rev(bwd[1]), state_b)
    return h_f + rev(h_b), st_f, st_b

def mlstm_readout(h, o, norm_w):
    B_, H, T, dh = h.shape
    hn = _standardize(h).transpose(0, 2, 1, 3).reshape(B_, T, M_WIDTH) * norm_w
    return (jax.nn.sigmoid(o.astype(jnp.float32)) * hn).astype(o.dtype)

def spatial_gating(u, vg, norm_w, w_s, b_s):
    B_, T, _ = u.shape
    zv = (_standardize(jax.nn.gelu(vg)) * norm_w).astype(vg.dtype)
    zv = zv.reshape(B_, T // S_CHUNK, S_CHUNK, S_GROUPS, S_GROUP_DIM)
    mixed = jnp.einsum('gpq,bnqgc->bnpgc', w_s, zv) + b_s.T[:, :, None]
    return jax.nn.gelu(u) * mixed.reshape(B_, T, S_WIDTH)

def branch_merge(h_a, h_b, ga, gb, branch_b, p_a, p_b, w_out):
    ba, bb = jnp.split(branch_b, 2)
    merged = jax.nn.sigmoid(ga + ba) * (h_a @ p_a) + jax.nn.sigmoid(gb + bb) * (h_b @ p_b)
    return merged @ w_out

def token_mixer(hc, hx, rows, w_in, qk_conv_w, qk_conv_b, gate_b, mlstm_norm_w, sgu_norm_w,
                sgu_w, sgu_b, branch_b, p_a, p_b, w_out, ctx_out):
    qk_c, v_c, o_c, gt_c, u_c, vg_c, ga_c, gb_c = jnp.split(hc @ w_in, IN_SPLITS, axis=-1)
    qk_x, v_x, o_x, gt_x, u_x, vg_x, ga_x, gb_x = jnp.split(hx @ w_in, IN_SPLITS, axis=-1)
    qk_c = jax.nn.silu(conv_seq(qk_c, qk_conv_w[M_CONV // 2], qk_conv_b))
    qk_x = jax.nn.silu(conv_grid(qk_x, qk_conv_w, qk_conv_b, rows))
    q_c, k_c, vh_c, fwd_c, bwd_c = mlstm_prepare(qk_c, v_c, gt_c, gate_b)
    q_x, k_x, vh_x, fwd_x, bwd_x = mlstm_prepare(qk_x, v_x, gt_x, gate_b)
    nb = hc.shape[0]
    h_mc, st_f, st_b = mlstm_bidir(q_c, k_c, vh_c, fwd_c, bwd_c, zero_state(nb), zero_state(nb))
    h_mx, _, _ = mlstm_bidir(q_x, k_x, vh_x, fwd_x, bwd_x, st_f, st_b)
    y_x = branch_merge(mlstm_readout(h_mx, o_x, mlstm_norm_w),
                       spatial_gating(u_x, vg_x, sgu_norm_w, sgu_w, sgu_b),
                       ga_x, gb_x, branch_b, p_a, p_b, w_out)
    if not ctx_out:
        return None, y_x
    y_c = branch_merge(mlstm_readout(h_mc, o_c, mlstm_norm_w),
                       spatial_gating(u_c, vg_c, sgu_norm_w, sgu_w, sgu_b),
                       ga_c, gb_c, branch_b, p_a, p_b, w_out)
    return y_c, y_x

def peer(h, w_q, sub_keys, expert_u, expert_v):
    B_, T, D = h.shape
    blocks = h.reshape(B_ * T // PEER_BLOCK, PEER_BLOCK, D)

    def retrieve(xb):
        qry = (xb @ w_q).reshape(PEER_BLOCK, PEER_HEADS, 2, PEER_HALF)
        scores = jnp.einsum('thpd,hpkd->thpk', qry, sub_keys)
        s_top, i_top = lax.top_k(scores, PEER_TOPK)
        cand_s = (s_top[:, :, 0, :, None] + s_top[:, :, 1, None, :]).reshape(
            PEER_BLOCK, PEER_HEADS, PEER_TOPK * PEER_TOPK)
        cand_i = (i_top[:, :, 0, :, None] * N_KEYS + i_top[:, :, 1, None, :]).reshape(
            PEER_BLOCK, PEER_HEADS, PEER_TOPK * PEER_TOPK)
        s_fin, pos = lax.top_k(cand_s, PEER_TOPK)
        idx = jnp.take_along_axis(cand_i, pos, axis=-1)
        gate = jax.nn.softmax(s_fin.astype(jnp.float32), axis=-1).astype(xb.dtype)
        act = jax.nn.gelu(jnp.einsum('thed,td->the', jnp.take(expert_u, idx, axis=0), xb))
        return jnp.einsum('the,thed->td', gate * act, jnp.take(expert_v, idx, axis=0))

    return lax.map(retrieve, blocks).reshape(B_, T, D)

def setup_inputs(seed: int = 0) -> dict:
    key = jax.random.key(seed)
    ks = jax.random.split(key, 24)

    def nrm(k, shape, s=1.0):
        return s * jax.random.normal(k, shape, jnp.float32)

    f_bias = jnp.linspace(3.0, 6.0, M_HEADS, dtype=jnp.float32)
    zeros_h = jnp.zeros((M_HEADS,), jnp.float32)
    gate_base = jnp.concatenate([zeros_h, f_bias, zeros_h, f_bias])
    return {
        'x': nrm(ks[0], (BATCH, SEQ, D_MODEL)),
        'c': nrm(ks[1], (BATCH, D_MODEL)),
        'ctx': nrm(ks[2], (BATCH, CTX_LEN, D_MODEL)),
        'c_ctx': nrm(ks[3], (D_MODEL,)),
        'w_mod': nrm(ks[4], (DEPTH, D_MODEL, 6 * D_MODEL), 0.5 * D_MODEL ** -0.5),
        'b_mod': nrm(ks[5], (DEPTH, 6 * D_MODEL), 0.02),
        'w_in': nrm(ks[6], (DEPTH, D_MODEL, IN_WIDTH), D_MODEL ** -0.5),
        'qk_conv_w': nrm(ks[7], (DEPTH, M_CONV, M_CONV, 2 * M_WIDTH), 1.0 / M_CONV),
        'qk_conv_b': nrm(ks[8], (DEPTH, 2 * M_WIDTH), 0.02),
        'gate_b': gate_base + nrm(ks[9], (DEPTH, N_GATES), 0.1),
        'mlstm_norm_w': 1.0 + nrm(ks[10], (DEPTH, M_WIDTH), 0.1),
        'sgu_norm_w': 1.0 + nrm(ks[11], (DEPTH, S_WIDTH), 0.1),
        'sgu_w': nrm(ks[12], (DEPTH, S_GROUPS, S_CHUNK, S_CHUNK), S_CHUNK ** -0.5),
        'sgu_b': 1.0 + nrm(ks[13], (DEPTH, S_GROUPS, S_CHUNK), 0.1),
        'branch_b': nrm(ks[14], (DEPTH, 2 * D_MODEL), 0.1),
        'p_a': nrm(ks[15], (DEPTH, M_WIDTH, D_MODEL), DN_BETA * M_WIDTH ** -0.5),
        'p_b': nrm(ks[16], (DEPTH, S_WIDTH, D_MODEL), DN_BETA * S_WIDTH ** -0.5),
        'w_out': nrm(ks[17], (DEPTH, D_MODEL, D_MODEL), DN_BETA * D_MODEL ** -0.5),
        'ln_w': 1.0 + nrm(ks[18], (DEPTH, 2, D_MODEL), 0.1),
        'ln_b': nrm(ks[19], (DEPTH, 2, D_MODEL), 0.02),
        'peer_wq': nrm(ks[20], (DEPTH, D_MODEL, PEER_HEADS * PEER_QDIM), D_MODEL ** -0.5),
        'peer_keys': nrm(ks[21], (DEPTH, PEER_HEADS, 2, N_KEYS, PEER_HALF), PEER_HALF ** -0.5),
        'expert_u': nrm(ks[22], (DEPTH, N_EXPERTS, D_MODEL), D_MODEL ** -0.5),
        'expert_v': nrm(ks[23], (DEPTH, N_EXPERTS, D_MODEL), DN_BETA),
    }

def reference(x, c, ctx, c_ctx, w_mod, b_mod, w_in, qk_conv_w, qk_conv_b, gate_b, mlstm_norm_w,
              sgu_norm_w, sgu_w, sgu_b, branch_b, p_a, p_b, w_out, ln_w, ln_b, peer_wq, peer_keys,
              expert_u, expert_v):
    rows = x.shape[1] // GRID_W
    cond_x = jax.nn.silu(c)
    cond_c = jax.nn.silu(c_ctx)
    zx, zc = x, ctx
    for l in range(DEPTH):
        ctx_live = l < DEPTH - 1
        mx = jnp.split((cond_x @ w_mod[l] + b_mod[l])[:, None, :], 6, axis=-1)
        mc = jnp.split(cond_c @ w_mod[l] + b_mod[l], 6, axis=-1)
        hx = zx * (1.0 + mx[1]) + mx[0]
        hc = zc * (1.0 + mc[1]) + mc[0]
        y_c, y_x = token_mixer(hc, hx, rows, w_in[l], qk_conv_w[l], qk_conv_b[l], gate_b[l],
                               mlstm_norm_w[l], sgu_norm_w[l], sgu_w[l], sgu_b[l], branch_b[l],
                               p_a[l], p_b[l], w_out[l], ctx_live)
        zx = layer_norm(DN_ALPHA * zx + mx[2] * y_x, ln_w[l, 0], ln_b[l, 0])
        hx = zx * (1.0 + mx[4]) + mx[3]
        zx = layer_norm(DN_ALPHA * zx + mx[5] * peer(hx, peer_wq[l], peer_keys[l], expert_u[l], expert_v[l]),
                        ln_w[l, 1], ln_b[l, 1])
        if ctx_live:
            zc = layer_norm(DN_ALPHA * zc + mc[2] * y_c, ln_w[l, 0], ln_b[l, 0])
            hc = zc * (1.0 + mc[4]) + mc[3]
            zc = layer_norm(DN_ALPHA * zc + mc[5] * peer(hc, peer_wq[l], peer_keys[l], expert_u[l], expert_v[l]),
                            ln_w[l, 1], ln_b[l, 1])
    return zx


_drawn_inputs = setup_inputs


def setup_inputs(seed=0):
    import zlib

    import numpy as np

    out = dict(_drawn_inputs(seed))
    spreads = {}
    factors = {'ctx': 8.0,
     'c_ctx': 8.0,
     'b_mod': 3.447,
     'qk_conv_w': 143.662,
     'qk_conv_b': 200.0,
     'gate_b': 3.218,
     'mlstm_norm_w': 21.376,
     'sgu_norm_w': 8.0,
     'sgu_b': 8.0,
     'branch_b': 8.0}
    for name, (base, spread) in spreads.items():
        noise = np.random.default_rng([zlib.crc32(name.encode()), seed]).standard_normal(out[name].shape)
        drawn = base * np.exp(spread * noise) if base else spread * noise
        out[name] = jnp.asarray(drawn.astype(out[name].dtype))
    for name, factor in factors.items():
        out[name] = (out[name] * factor).astype(out[name].dtype)
    return out
```

```python
from contextlib import ExitStack

import concourse.bass as bass
from concourse import mybir

F32 = mybir.dt.float32
BF16 = mybir.dt.bfloat16
U32 = mybir.dt.uint32
ALU = mybir.AluOpType
ACT = mybir.ActivationFunctionType
AX = mybir.AxisListType.X

P = 128
D = 1024
KD = D // P
DEPTH = 2
CTX, SEQ = 256, 512
T = CTX + SEQ
NT = T // P
CT = CTX // P
H = 8
GRID_W = 64
ROWS = SEQ // GRID_W
TAPS = 9
E_H = P + 1
BANK = 512
TOPK = 16
N_EXPERTS = P * P
NEG = -1e30
ALPHA = float((2 * DEPTH) ** 0.25)
EPS = 1e-5
QSCALE = float(P) ** -0.5
MODW = 6 * D
C_QK, C_V, C_O, C_G, C_U = 0, 2 * D, 3 * D, 4 * D, 4 * D + 32
C_VG, C_GA, C_GB = C_U + D, C_U + 2 * D, C_U + 3 * D
K_TAP, K_CB, K_BR, K_MN, K_SB, K_ALL = 0, 144, 160, 176, 184, 192
ORDER = [[0, 1, 2, 3, 4, 5], [1, 0, 5, 4, 3, 2]]
ROW0 = [0, 32]
GR = 40


def wcols(w, c0, n):
    return w[:, c0:c0 + n].rearrange("(k p) n -> p k n", p=P)


class Kernel:
    def __init__(self, nc, a, out):
        self.nc, self.a, self.out = nc, a, out
        self.count = 0

    def scope(self):
        ctx = ExitStack()
        self.count += 1
        tag = f"_{self.count}"

        def sb(name, shape, dt=F32):
            return ctx.enter_context(self.nc.sbuf_tensor(name + tag, shape, dt))

        sems = []

        def sem(name):
            sems.append(self.nc.alloc_semaphore(name + tag))
            return sems[-1]

        def clear():
            if sems:
                self.nc.clear_and_free_semaphores(sems)
                self.nc.all_engine_barrier()

        ctx.callback(clear)
        return ctx, sb, sem

    def setup(self):
        nc, a = self.nc, self.a
        ctx, sb, sem = self.scope()
        z, ident, identb, mask, cols, cond = self.z, self.ident, self.identb, self.mask, self.cols, self.cond
        with ctx:
            rows_a = sb("rows_a", [P, DEPTH, P])
            rows_b = sb("rows_b", [64, DEPTH, P])
            crow = sb("crow", [2 * KD, P])
            csil = sb("csil", [2 * KD, P])
            z_in, rows_in, c_in = sem("z_in"), sem("rows_in"), sem("c_in")
            zeroed, ident_ready, cond_silu = sem("zeroed"), sem("ident_ready"), sem("cond_silu")
            turned, copied, masks_ready = sem("turned"), sem("copied"), sem("masks_ready")
            block = ctx.enter_context(nc.Block())

            @block.sync
            def _(sp):
                sp.dma_start(crow[0:KD, :], a["c"].rearrange("a (k p) -> (a k) p", p=P)).then_inc(c_in, 16)
                sp.dma_start(crow[KD:2 * KD, :], a["c_ctx"].rearrange("(k p) -> k p", p=P)).then_inc(c_in, 16)
                for l in range(DEPTH):
                    taps = a["qk_conv_w"][l].rearrange("i j (c p) -> (i j c) p", p=P)
                    sp.dma_start(rows_a[:, l, :], taps[0:P]).then_inc(rows_in, 16)
                    sp.dma_start(rows_b[0:16, l, :], taps[P:144]).then_inc(rows_in, 16)
                    sp.dma_start(rows_b[16:32, l, :], a["qk_conv_b"][l].rearrange("(c p) -> c p", p=P)).then_inc(rows_in, 16)
                    sp.dma_start(rows_b[32:48, l, :], a["branch_b"][l].rearrange("(c p) -> c p", p=P)).then_inc(rows_in, 16)
                    sp.dma_start(rows_b[48:56, l, :], a["mlstm_norm_w"][l].rearrange("(c p) -> c p", p=P)).then_inc(rows_in, 16)
                    sp.dma_start(rows_b[56:64, l, :], a["sgu_b"][l]).then_inc(rows_in, 16)
                sp.dma_start(z[:, 0:CT, :], a["ctx"][0].rearrange("(t p) d -> p t d", p=P)).then_inc(z_in, 16)
                sp.dma_start(z[:, CT:NT, :], a["x"][0].rearrange("(t p) d -> p t d", p=P)).then_inc(z_in, 16)
                sp.wait_ge(z_in, 32)

            @block.gpsimd
            def _(gp):
                gp.memset(ident[:], 0.0).then_inc(zeroed, 1)
                gp.memset(mask[:], 0.0).then_inc(zeroed, 1)
                gp.memset(self.ones[:], 1.0).then_inc(zeroed, 1)
                gp.wait_ge(zeroed, 3)
                gp.affine_select(out=ident[:], in_=ident[:], compare_op=ALU.not_equal, fill=1.0, base=0,
                                 pattern=[[-1, P]], channel_multiplier=1).then_inc(ident_ready, 1)
                m0 = mask[:, 0, :].rearrange("p (b t) -> p b t", b=2)
                gp.affine_select(out=m0, in_=m0, compare_op=ALU.is_ge, fill=NEG, base=0,
                                 pattern=[[0, 2], [1, P]], channel_multiplier=-1).then_inc(masks_ready, 1)
                m1 = mask[:, 1, :].rearrange("p (b t) -> p b t", b=2)
                gp.affine_select(out=m1, in_=m1, compare_op=ALU.is_ge, fill=NEG, base=0,
                                 pattern=[[0, 2], [-1, P]], channel_multiplier=1).then_inc(masks_ready, 1)
                gp.wait_ge(ident_ready, 1)
                gp.tensor_scalar(self.negident[:], ident[:], -1.0, None, ALU.mult).then_inc(masks_ready, 1)

            @block.scalar
            def _(act):
                act.wait_ge(c_in, 32)
                act.activation(csil[:], crow[:], ACT.Silu).then_inc(cond_silu, 1)

            @block.tensor
            def _(pe):
                pe.wait_ge(ident_ready, 1)
                pe.wait_ge(cond_silu, 1)
                pe.transpose(self.ps[:, 0, 0:2 * KD], csil[:], ident[0:2 * KD, 0:2 * KD]).then_inc(turned, 1)
                pe.wait_ge(rows_in, 16 * 6 * DEPTH)
                for l in range(DEPTH):
                    pe.transpose(self.ps[:, 1 + l, 0:P], rows_a[:, l, :], ident[:])
                    pe.transpose(self.ps[:, 1 + l, P:P + 64], rows_b[:, l, :], ident[0:64, 0:64]).then_inc(turned, 1)

            @block.vector
            def _(ve):
                ve.wait_ge(ident_ready, 1)
                ve.tensor_copy(identb[:], ident[:]).then_inc(copied, 1)
                ve.wait_ge(turned, 1)
                ve.tensor_copy(cond[:], self.ps[:, 0, 0:2 * KD].rearrange("p (w k) -> p k w", w=2)).then_inc(copied, 1)
                ve.wait_ge(turned, 1 + DEPTH)
                for l in range(DEPTH):
                    ve.tensor_copy(cols[:, l, :], self.ps[:, 1 + l, 0:K_ALL]).then_inc(copied, 1)

    def modulation(self):
        nc, a, ps, cond = self.nc, self.a, self.ps, self.cond
        ctx, sb, sem = self.scope()
        W = BANK
        per_layer = MODW // W
        UN = 4
        with ctx:
            wt = sb("wt", [P, UN, KD, W])
            bias = sb("bias", [2, MODW])
            row = sb("row", [2, MODW])
            rows = sb("rows", [96, P])
            w_in = [sem(f"w_in{u}") for u in range(UN)]
            b_in, w_used, row_ready, stored, back = sem("b_in"), sem("w_used"), sem("row_ready"), sem("stored"), sem("back")
            turned, cols_ready = sem("turned"), sem("cols_ready")
            block = ctx.enter_context(nc.Block())

            @block.sync
            def _(sp):
                for l in range(DEPTH):
                    def load(g, u):
                        sp.dma_start(wt[:, u], wcols_dyn(a["w_mod"][l], g * W, W)).then_inc(w_in[u], 16)
                    if l == 0:
                        for u in range(UN):
                            load(u, u)
                    else:
                        for u in range(UN):
                            sp.wait_ge(w_used, per_layer * l - UN + u + 1)
                            load(u, u)
                    with sp.Fori(1, per_layer // UN) as i:
                        for u in range(UN):
                            sp.wait_ge(w_used, i * UN + (per_layer * l - UN + u + 1))
                            load(i * UN + u, u)
                    sp.wait_ge(row_ready, per_layer * (l + 1) + UN)
                    sp.dma_start(self.mod_dram[l], row[:]).then_inc(stored, 16)
                    sp.wait_ge(stored, 16 * (l + 1))
                    for w in range(2):
                        if l:
                            sp.wait_ge(turned, l)
                        sp.dma_start(rows[48 * w:48 * w + 48, :],
                                     self.mod_dram[l, w].rearrange("(r p) -> r p", p=P)).then_inc(back, 16)

            @block.tensor
            def _(pe):
                for l in range(DEPTH):
                    with pe.Fori(0, per_layer // UN) as i:
                        for u in range(UN):
                            pe.wait_ge(w_in[u], i * 16 + 16 * (l * (per_layer // UN) + 1))
                            pe.wait_ge(row_ready, i * UN + per_layer * l + u + 1)
                            for k in range(KD):
                                mm = pe.matmul(ps[0:2, u, :], cond[:, k, :], wt[:, u, k, :], start=(k == 0), stop=(k == KD - 1))
                            mm.then_inc(w_used, 1)
                    pe.wait_ge(back, 32 * (l + 1))
                    pe.transpose(ps[:, 4 + l, 0:96], rows[:], self.ident[0:96, 0:96]).then_inc(turned, 1)

            @block.scalar
            def _(act):
                for l in range(DEPTH):
                    if l:
                        act.wait_ge(row_ready, per_layer * l + UN)
                    act.dma_start(bias[:], a["b_mod"][l:l + 1, :].broadcast_to((2, MODW))).then_inc(b_in, 16)

            @block.vector
            def _(ve):
                ve.memset(row[:], 0.0).then_inc(row_ready, UN)
                ve.wait_ge(row_ready, UN)
                for l in range(DEPTH):
                    ve.wait_ge(b_in, 16 * (l + 1))
                    if l:
                        ve.wait_ge(stored, 16 * l)
                    with ve.Fori(0, per_layer // UN) as i:
                        for u in range(UN):
                            ve.wait_ge(w_used, i * UN + per_layer * l + u + 1)
                            at = bass.ds(i * (UN * W) + u * W, W)
                            ve.tensor_tensor(out=row[:, at], in0=ps[0:2, u, :], in1=bias[:, at], op=ALU.add).then_inc(row_ready, 1)
                    ve.wait_ge(turned, l + 1)
                    mc = self.modc[:, l]
                    ve.tensor_copy(mc, ps[:, 4 + l, 0:96].rearrange("p (w m k) -> p w m k", w=2, m=6)).then_inc(cols_ready, 1)
                    ve.wait_ge(cols_ready, 3 * l + 1)
                    for m in (1, 4):
                        ve.tensor_scalar(mc[:, :, m, :], mc[:, :, m, :], 1.0, None, ALU.add).then_inc(cols_ready, 1)

    def modulated_turn(self, l, m_shift, hT, t0):
        nc, ps = self.nc, self.ps
        ctx, sb, sem = self.scope()
        with ctx:
            turned, act_out, dve_out = sem("turned"), sem("act_out"), sem("dve_out")
            block = ctx.enter_context(nc.Block())
            tiles = list(range(t0, NT))

            def col(t, m, k):
                return self.modc[:, l, 1 if t < CT else 0, m, k:k + 1]

            @block.tensor
            def _(pe):
                for n, t in enumerate(tiles):
                    if n >= 4:
                        pe.wait_ge(act_out, 4 * (n - 3))
                        pe.wait_ge(dve_out, 4 * (n - 3))
                    for k in range(KD):
                        mm = pe.transpose(ps[:, 2 * (n % 4) + k // 4, (k % 4) * P:(k % 4) * P + P],
                                          self.z[:, t, k * P:(k + 1) * P], self.ident[:])
                    mm.then_inc(turned, 1)

            @block.scalar
            def _(act):
                for n, t in enumerate(tiles):
                    act.wait_ge(turned, n + 1)
                    for k in range(4):
                        act.activation(hT[:, k, t * P:(t + 1) * P], ps[:, 2 * (n % 4), k * P:(k + 1) * P], ACT.Identity,
                                       bias=col(t, m_shift, k), scale=col(t, m_shift + 1, k)).then_inc(act_out, 1)

            @block.vector
            def _(ve):
                for n, t in enumerate(tiles):
                    ve.wait_ge(turned, n + 1)
                    for k in range(4):
                        ve.tensor_scalar(hT[:, 4 + k, t * P:(t + 1) * P], ps[:, 2 * (n % 4) + 1, k * P:(k + 1) * P],
                                         col(t, m_shift + 1, 4 + k), col(t, m_shift, 4 + k), ALU.mult, ALU.add).then_inc(dve_out, 1)

    def project_qk(self, l, hT, qk):
        nc, a, ps, cols = self.nc, self.a, self.ps, self.cols
        ctx, sb, sem = self.scope()
        UN = 4
        NC = 2 * D // P
        RH, RW = ROWS + 2, GRID_W + 2
        w_l = a["w_in"][l]
        with ctx:
            wt = sb("wt", [P, UN, KD, P])
            raw_x = sb("raw_x", [P, 2, RH, RW])
            raw_c = sb("raw_c", [P, 2, CTX + 2])
            acc = sb("acc", [P, 2, T])
            w_in = [sem(f"w_in{u}") for u in range(UN)]
            w_used, raw_ready, zeroed, conv_step, silu_done = sem("w_used"), sem("raw_ready"), sem("zeroed"), sem("conv_step"), sem("silu_done")
            STEPS = TAPS + 3
            block = ctx.enter_context(nc.Block())

            @block.sync
            def _(sp):
                def load(n, u):
                    sp.dma_start(wt[:, u], wcols_dyn(w_l, n * P, P)).then_inc(w_in[u], 16)
                for u in range(UN):
                    load(u, u)
                with sp.Fori(1, NC // UN) as i:
                    for u in range(UN):
                        sp.wait_ge(w_used, i * UN + (u + 1 - UN))
                        load(i * UN + u, u)

            @block.tensor
            def _(pe):
                with pe.Fori(0, NC // UN) as i:
                    for u in range(UN):
                        b = 2 * (u % 4)
                        pe.wait_ge(w_in[u], i * 16 + 16)
                        pe.wait_ge(raw_ready, i * 8 + 2 * u + 2)
                        for k in range(KD):
                            pe.matmul(ps[:, b, :], wt[:, u, k, :], hT[:, k, CTX:T], start=(k == 0), stop=(k == KD - 1))
                        for k in range(KD):
                            mm = pe.matmul(ps[:, b + 1, 0:CTX], wt[:, u, k, :], hT[:, k, 0:CTX], start=(k == 0), stop=(k == KD - 1))
                        mm.then_inc(w_used, 1)

            @block.gpsimd
            def _(gp):
                gp.memset(raw_x[:], 0.0).then_inc(raw_ready, 4)
                gp.memset(raw_c[:], 0.0).then_inc(raw_ready, 4)

            @block.scalar
            def _(act):
                act.wait_ge(raw_ready, 8)
                with act.Fori(0, NC // UN) as i:
                    for u in range(UN):
                        s, b = u % 2, 2 * (u % 4)
                        act.wait_ge(w_used, i * UN + u + 1)
                        act.activation(raw_x[:, s, 1:1 + ROWS, 1:1 + GRID_W],
                                       ps[:, b, :].rearrange("p (r w) -> p r w", r=ROWS), ACT.Copy).then_inc(raw_ready, 1)
                        act.activation(raw_c[:, s, 1:1 + CTX], ps[:, b + 1, 0:CTX], ACT.Copy).then_inc(raw_ready, 1)
                        act.wait_ge(conv_step, i * (UN * STEPS) + STEPS * (u + 1))
                        act.activation(qk[:, bass.ds(i * UN + u, 1), :], acc[:, s:s + 1, :], ACT.Silu).then_inc(silu_done, 1)

            @block.vector
            def _(ve):
                with ve.Fori(0, NC // UN) as i:
                    for u in range(UN):
                        s = u % 2
                        ve.wait_ge(raw_ready, i * (2 * UN) + 8 + 2 * (u + 1))
                        def tap(j):
                            return cols[:, l, bass.ds(i * UN + (K_TAP + 16 * j + u), 1)]
                        cb = cols[:, l, bass.ds(i * UN + (K_CB + u), 1)]
                        done = 0
                        for j in range(TAPS):
                            src = raw_x[:, s, j // 3:j // 3 + ROWS, j % 3:j % 3 + GRID_W]
                            dst = acc[:, s, CTX:T].rearrange("p (r w) -> p r w", r=ROWS)
                            if j:
                                ve.wait_ge(conv_step, i * (UN * STEPS) + (STEPS * u + (2 * j - 1 if j < 4 else j + 3)))
                                ve.scalar_tensor_tensor(out=dst, in0=src, scalar=tap(j), in1=dst, op0=ALU.mult, op1=ALU.add).then_inc(conv_step, 1)
                            else:
                                ve.tensor_scalar(dst, src, tap(0), cb, ALU.mult, ALU.add).then_inc(conv_step, 1)
                            if j < 3:
                                src, dst = raw_c[:, s, j:j + CTX], acc[:, s, 0:CTX]
                                if j:
                                    ve.wait_ge(conv_step, i * (UN * STEPS) + (STEPS * u + 2 * j))
                                    ve.scalar_tensor_tensor(out=dst, in0=src, scalar=tap(3 + j), in1=dst, op0=ALU.mult, op1=ALU.add).then_inc(conv_step, 1)
                                else:
                                    ve.tensor_scalar(dst, src, tap(3), cb, ALU.mult, ALU.add).then_inc(conv_step, 1)

    def project_rows(self, sources, actT, tiles, evacuate, extra=None):
        nc, ps = self.nc, self.ps
        ctx, sb, sem = self.scope()
        NS = 2
        G = len(sources)
        with ctx:
            wt = sb("wt", [P, NS, KD, BANK])
            w_in = [sem(f"w_in{s}") for s in range(NS)]
            mm_done, evacuated = sem("mm_done"), sem("evacuated")
            block = ctx.enter_context(nc.Block())

            @block.sync
            def _(sp):
                for g, src in enumerate(sources):
                    if g >= NS:
                        sp.wait_ge(mm_done, (g - NS + 1) * len(tiles))
                    for half in range(2):
                        k0 = half * KD // 2
                        sp.dma_start(wt[:, g % NS, k0:k0 + KD // 2, :],
                                     src[k0 * P:(k0 + KD // 2) * P, :].rearrange("(k p) n -> p k n", p=P)).then_inc(w_in[g % NS], 16)

            @block.tensor
            def _(pe):
                n = 0
                for g in range(G):
                    pe.wait_ge(w_in[g % NS], 32 * (g // NS + 1))
                    for t in tiles:
                        if n >= 8:
                            pe.wait_ge(evacuated, n - 7)
                        for k in range(KD):
                            mm = pe.matmul(ps[:, n % 8, :], actT[:, k, t * P:(t + 1) * P], wt[:, g % NS, k, :],
                                           start=(k == 0), stop=(k == KD - 1))
                        mm.then_inc(mm_done, 1)
                        n += 1

            @block.scalar
            def _(act):
                n = 0
                for g in range(G):
                    for t in tiles:
                        act.wait_ge(mm_done, n + 1)
                        evacuate(act, g, t, ps[:, n % 8, :]).then_inc(evacuated, 1)
                        n += 1

    def gates(self, l, hT, tok, alast):
        nc, a, ps, ident = self.nc, self.a, self.ps, self.ident
        ctx, sb, sem = self.scope()
        w_l = a["w_in"][l]
        M = self.m_rows
        with ctx:
            wg = sb("wg", [P, KD, 2, GR])
            gb = sb("gb", [GR, 2])
            gi, gf, t1, t2, b_, c_ = (sb(n, [GR, T]) for n in ("gi", "gf", "t1", "t2", "b_", "c_"))
            one = sb("one", [GR, P])
            mprev = sb("mprev", [GR, NT])
            nlast = sb("nlast", [GR, NT])
            al = sb("al", [GR, NT])
            ald = sb("ald", [GR, NT, GR])
            av, ev, wv = (sb(n, [GR, T]) for n in ("av", "ev", "wv"))
            zeroed, w_in, g_mm, act_done, dve_done, turned, out_done = (
                sem(n) for n in ("zeroed", "w_in", "g_mm", "act_done", "dve_done", "turned", "out_done"))
            N_ABS = 5
            N_LF = N_ABS + 1
            N_M = N_LF + 2 * NT + 1 + (6 * NT - 2) + NT
            N_DVE = N_M + NT
            block = ctx.enter_context(nc.Block())

            @block.gpsimd
            def _(gp):
                gp.memset(wg[:], 0.0).then_inc(zeroed, 1)
                gp.memset(gb[:], 0.0).then_inc(zeroed, 1)
                gp.memset(one[:], 1.0).then_inc(zeroed, 1)
                for x in (mprev, nlast, al, b_, M):
                    gp.memset(x[:], 0.0).then_inc(zeroed, 1)
                gp.wait_ge(zeroed, 8)
                for d in range(2):
                    c = ORDER[d][0]
                    gp.memset(mprev[ROW0[d]:ROW0[d] + H, c:c + 1], NEG).then_inc(zeroed, 1)

            @block.sync
            def _(sp):
                sp.wait_ge(zeroed, 2)
                for d in range(2):
                    for kind in range(2):
                        c0 = C_G + 16 * d + 8 * kind
                        sp.dma_start(wg[:, :, kind, ROW0[d]:ROW0[d] + H],
                                     w_l[:, c0:c0 + H].rearrange("(k p) n -> p k n", p=P)).then_inc(w_in, 16)
                        g0 = 16 * d + 8 * kind
                        sp.dma_start(gb[ROW0[d]:ROW0[d] + H, kind:kind + 1],
                                     a["gate_b"][l, g0:g0 + H].rearrange("(n o) -> n o", o=1)).then_inc(w_in, 16)

            @block.tensor
            def _(pe):
                pe.wait_ge(w_in, 16 * 8)
                for kind in range(2):
                    for k in range(KD):
                        pe.matmul(ps[0:GR, 2 * kind, 0:BANK], wg[:, k, kind, :], hT[:, k, 0:BANK], start=(k == 0), stop=(k == KD - 1))
                    for k in range(KD):
                        mm = pe.matmul(ps[0:GR, 2 * kind + 1, 0:T - BANK], wg[:, k, kind, :], hT[:, k, BANK:T], start=(k == 0), stop=(k == KD - 1))
                    mm.then_inc(g_mm, 1)
                pe.wait_ge(act_done, 3 + 3 * NT)
                for c in range(NT):
                    for n, x in enumerate((av, ev, wv, c_)):
                        mm = pe.transpose(ps[:, c, n * GR:(n + 1) * GR], x[:, c * P:(c + 1) * P], ident[0:GR, 0:GR])
                    mm.then_inc(turned, 1)
                pe.wait_ge(dve_done, N_DVE)
                pe.matmul(ps[:, 6, 0:NT * GR], self.ones[0:GR, :], ald[:].rearrange("p c r -> p (c r)"), start=True, stop=True).then_inc(turned, 1)

            @block.scalar
            def _(act):
                act.wait_ge(dve_done, N_ABS)
                act.activation(t1[:], t1[:], ACT.Exp, scale=-1.0).then_inc(act_done, 1)
                act.wait_ge(act_done, 1)
                act.activation(t2[:], t1[:], ACT.Ln, bias=1.0).then_inc(act_done, 1)
                act.wait_ge(dve_done, N_M)
                act.activation(ev[:], t1[:], ACT.Exp, scale=-1.0).then_inc(act_done, 1)
                for c in range(NT):
                    cs = slice(c * P, (c + 1) * P)
                    act.activation(av[:, cs], M[:, cs], ACT.Exp, bias=mprev[:, c:c + 1], scale=-1.0).then_inc(act_done, 1)
                    act.activation(wv[:, cs], c_[:, cs], ACT.Exp, bias=nlast[:, c:c + 1]).then_inc(act_done, 1)
                    act.activation(al[:, c:c + 1], nlast[:, c:c + 1], ACT.Exp, bias=mprev[:, c:c + 1]).then_inc(act_done, 1)

            @block.vector
            def _(ve):
                n = 0

                def after(ins):
                    nonlocal n
                    n += 1
                    ins.then_inc(dve_done, 1)
                    ve.wait_ge(dve_done, n)

                def take(ins):
                    nonlocal n
                    n += 1
                    ins.then_inc(dve_done, 1)

                ve.wait_ge(zeroed, 10)
                ve.wait_ge(g_mm, 2)
                i2 = gi
                take(ve.tensor_scalar(i2[:, 0:BANK], ps[0:GR, 0, :], gb[:, 0:1], None, ALU.add))
                take(ve.tensor_scalar(i2[:, BANK:T], ps[0:GR, 1, 0:T - BANK], gb[:, 0:1], None, ALU.add))
                take(ve.tensor_scalar(gf[:, 0:BANK], ps[0:GR, 2, :], gb[:, 1:2], None, ALU.add))
                after(ve.tensor_scalar(gf[:, BANK:T], ps[0:GR, 3, 0:T - BANK], gb[:, 1:2], None, ALU.add))
                after(ve.scalar_tensor_tensor(out=t1[:], in0=gf[:], scalar=-1.0, in1=gf[:], op0=ALU.mult, op1=ALU.max))
                assert n == N_ABS
                ve.wait_ge(act_done, 2)
                after(ve.scalar_tensor_tensor(out=gf[:], in0=gf[:], scalar=0.0, in1=t2[:], op0=ALU.min, op1=ALU.subtract))
                for d in range(2):
                    r = slice(ROW0[d], ROW0[d] + H)
                    for c in range(NT):
                        cs = chunk_slice(c, d)
                        take(ve.tensor_tensor_scan(b_[r, cs], one[r, :], gf[r, cs], 0.0, ALU.mult, ALU.add))
                ve.wait_ge(dve_done, n)
                after(ve.tensor_tensor(out=c_[:], in0=gi[:], in1=b_[:], op=ALU.subtract))
                for pos in range(NT):
                    for d in range(2):
                        c = ORDER[d][pos]
                        r = slice(ROW0[d], ROW0[d] + H)
                        last = c * P + (P - 1 if d == 0 else 0)
                        cs = chunk_slice(c, d)
                        after(ve.tensor_tensor_scan(M[r, cs], c_[r, cs], c_[r, cs], mprev[r, c:c + 1], ALU.max, ALU.max))
                        take(ve.tensor_scalar(nlast[r, c:c + 1], M[r, last:last + 1], -1.0, None, ALU.mult))
                        if pos < NT - 1:
                            nx = ORDER[d][pos + 1]
                            take(ve.tensor_tensor(out=mprev[r, nx:nx + 1], in0=M[r, last:last + 1], in1=b_[r, last:last + 1], op=ALU.add))
                        ve.wait_ge(dve_done, n)
                for c in range(NT):
                    cs = slice(c * P, (c + 1) * P)
                    take(ve.tensor_tensor(out=t1[:, cs], in0=M[:, cs], in1=b_[:, cs], op=ALU.add))
                ve.wait_ge(act_done, 3 + 3 * NT)
                for c in range(NT):
                    take(ve.tensor_scalar(ald[:, c, :], ident[0:GR, 0:GR], al[:, c:c + 1], None, ALU.mult))
                assert n == N_DVE, (n, N_DVE)
                for c in range(NT):
                    ve.wait_ge(turned, c + 1)
                    ve.tensor_copy(tok[:, c], ps[:, c, 0:4 * GR].rearrange("p (n r) -> p n r", n=4)).then_inc(out_done, 1)
                ve.wait_ge(turned, NT + 1)
                ve.tensor_copy(alast[:], ps[:, 6, 0:NT * GR].rearrange("p (c r) -> p c r", c=NT)).then_inc(out_done, 1)
                ve.wait_ge(out_done, NT)
                ve.tensor_scalar(tok[:, :, 0, :], tok[:, :, 0, :], QSCALE, None, ALU.mult).then_inc(out_done, 1)

    def mlstm(self, t0, qk, v, tok, alast, hsum):
        nc, ps = self.nc, self.ps
        ctx, sb, sem = self.scope()
        M = self.m_rows
        steps = [(d, ORDER[d][pos], ORDER[d][pos] >= t0, pos < NT - 1) for pos in range(NT) for d in range(2)]
        NP_ = H // 2
        hu = []
        uu = []
        for s, (d, c, has_h, has_u) in enumerate(steps):
            for p in range(NP_):
                if has_h:
                    hu.append((s, p))
                if has_u:
                    uu.append((s, p))
        h_at = {x: n for n, x in enumerate(hu)}
        u_at = {x: n for n, x in enumerate(uu)}
        slots = [(s, p) for s in range(len(steps)) for p in range(NP_)]
        h_steps = [s for s in range(len(steps)) if steps[s][2]]
        u_steps = [s for s in range(len(steps)) if steps[s][3]]
        seen = set()
        first_visit = {}
        for s in h_steps:
            first_visit[s] = steps[s][1] not in seen
            seen.add(steps[s][1])
        fin_len = {s: 4 if first_visit[s] else 5 for s in h_steps}
        fin_upto = {}
        total = 0
        for s in h_steps:
            total += fin_len[s]
            fin_upto[s] = total

        def ct_needed(s, p):
            d = steps[s][0]
            before = [x for x in u_steps if x < s and steps[x][0] == d]
            return u_at[(before[-1], p)] + 1 if before else 0

        def after_unit(slot, units_at):
            return units_at.get(slot)

        with ctx:
            state = sb("state", [P, 2, H, E_H])
            ktok = sb("ktok", [P, 2, D])
            vw = sb("vw", [P, 2, H, E_H])
            ex = sb("ex", [P, 2, 2, P])
            pt = sb("pt", [P, 2, 2, P])
            iv = sb("iv", [P, 2, 2, E_H])
            num = sb("num", [P, 2, H, E_H])
            den = sb("den", [P, 3, H])
            hb = sb("hb", [P, H, P])
            zeroed, sb_done, exp_done, p_ready, ii_done, iv_ready, num_ready, upd_done, ct_ready = (
                sem(n) for n in ("zeroed", "sb_done", "exp_done", "p_ready", "ii_done", "iv_ready", "num_ready", "upd_done", "ct_ready"))
            ktr_done, ktok_ready, vw_ready, fin = sem("ktr_done"), sem("ktok_ready"), sem("vw_ready"), sem("fin")
            block = ctx.enter_context(nc.Block())

            @block.gpsimd
            def _(gp):
                for d in range(2):
                    gp.memset(state[:, d], 0.0).then_inc(zeroed, 1)
                for n, s in enumerate(u_steps):
                    d, c = steps[s][:2]
                    if n >= 2:
                        gp.wait_ge(upd_done, NP_ * (n - 1))
                    wl = tok[:, c, 2, ROW0[d]:ROW0[d] + H]
                    gp.tensor_tensor(out=vw[:, n % 2], in0=v[:, c], in1=wl.unsqueeze(2).broadcast_to((P, H, E_H)), op=ALU.mult).then_inc(vw_ready, 1)

            @block.tensor
            def _(pe):
                pe.wait_ge(zeroed, 2)

                def scores(s, p):
                    n = h_at[(s, p)]
                    d, c = steps[s][:2]
                    cs = slice(c * P, (c + 1) * P)
                    if n >= 2:
                        pe.wait_ge(p_ready, n - 1)
                    for j in range(2):
                        h = 2 * p + j
                        pe.matmul(ps[:, n % 2, j * P:(j + 1) * P], qk[:, H + h, cs], qk[:, h, cs], start=True, stop=True)
                    pe.matmul(ps[:, n % 2, 2 * P:4 * P], self.identb[:], self.mask[:, d, :], start=True, stop=False, skip_group_check=True)
                    for j in range(2):
                        r = ROW0[d] + 2 * p + j
                        mm = pe.matmul(ps[:, n % 2, (2 + j) * P:(3 + j) * P], self.negident[0:GR, r:r + 1].broadcast_to((GR, P)),
                                       M[:, cs], start=False, stop=True, skip_group_check=True)
                    mm.then_inc(sb_done, 1)

                def outputs(s, p):
                    n = h_at[(s, p)]
                    d, c = steps[s][:2]
                    cs = slice(c * P, (c + 1) * P)
                    if n >= 2:
                        pe.wait_ge(num_ready, n - 1)
                    need = ct_needed(s, p)
                    if need:
                        pe.wait_ge(ct_ready, 2 * need)
                    for j in range(2):
                        h = 2 * p + j
                        pe.matmul(ps[:, 4 + n % 2, j * E_H:(j + 1) * E_H], qk[:, h, cs], state[:, d, h, :], start=True, stop=True)
                    pe.wait_ge(p_ready, n + 1)
                    for j in range(2):
                        mm = pe.matmul(ps[:, 2 + n % 2, j * E_H:(j + 1) * E_H], pt[:, n % 2, j, :], v[:, c, 2 * p + j, :], start=True, stop=True)
                    mm.then_inc(ii_done, 1)

                def k_rows(s):
                    n = u_steps.index(s)
                    c = steps[s][1]
                    cs = slice(c * P, (c + 1) * P)
                    for half in range(2):
                        if 2 * n + half >= 1:
                            pe.wait_ge(ktok_ready, 2 * n + half)
                        for j in range(4):
                            mm = pe.transpose(ps[:, 7, j * P:(j + 1) * P], qk[:, H + 4 * half + j, cs], self.ident[:])
                        mm.then_inc(ktr_done, 1)

                def update(s, p):
                    n = u_at[(s, p)]
                    us = u_steps.index(s)
                    if n >= 1:
                        pe.wait_ge(ct_ready, 2 * n)
                    pe.wait_ge(ktok_ready, 2 * us + p // 2 + 1)
                    pe.wait_ge(vw_ready, us + 1)
                    for j in range(2):
                        h = 2 * p + j
                        mm = pe.matmul(ps[:, 6, j * E_H:(j + 1) * E_H], ktok[:, us % 2, h * P:(h + 1) * P], vw[:, us % 2, h, :], start=True, stop=True)
                    mm.then_inc(upd_done, 1)

                nxt = {slots[i]: slots[i + 1] for i in range(len(slots) - 1)}
                if slots[0] in h_at:
                    scores(*slots[0])
                for slot in slots:
                    s, p = slot
                    if p == 0 and s in u_steps:
                        k_rows(s)
                    if nxt.get(slot) in h_at:
                        scores(*nxt[slot])
                    if slot in h_at:
                        outputs(s, p)
                    if slot in u_at:
                        update(s, p)

            @block.scalar
            def _(act):
                def exps(s, p):
                    n = h_at[(s, p)]
                    d, c = steps[s][:2]
                    act.wait_ge(sb_done, n + 1)
                    if n >= 2:
                        act.wait_ge(p_ready, n - 1)
                    for j in range(2):
                        r = ROW0[d] + 2 * p + j
                        act.activation(ex[:, n % 2, j, :], ps[:, n % 2, (2 + j) * P:(3 + j) * P], ACT.Exp,
                                       bias=tok[:, c, 3, r:r + 1]).then_inc(exp_done, 1)

                def inter(s, p):
                    n = h_at[(s, p)]
                    d, c = steps[s][:2]
                    act.wait_ge(ii_done, n + 1)
                    if n >= 2:
                        act.wait_ge(num_ready, n - 1)
                    for j in range(2):
                        r = ROW0[d] + 2 * p + j
                        act.activation(iv[:, n % 2, j, :], ps[:, 4 + n % 2, j * E_H:(j + 1) * E_H], ACT.Copy,
                                       scale=tok[:, c, 0, r:r + 1]).then_inc(iv_ready, 1)

                nxt = {slots[i]: slots[i + 1] for i in range(len(slots) - 1)}
                if slots[0] in h_at:
                    exps(*slots[0])
                for slot in slots:
                    s, p = slot
                    if p == 0 and s in u_steps:
                        us = u_steps.index(s)
                        if us >= 2:
                            act.wait_ge(upd_done, NP_ * (us - 1))
                        for half in range(2):
                            act.wait_ge(ktr_done, 2 * us + half + 1)
                            act.activation(ktok[:, us % 2, half * BANK:(half + 1) * BANK], ps[:, 7, :], ACT.Copy).then_inc(ktok_ready, 1)
                    if nxt.get(slot) in h_at:
                        exps(*nxt[slot])
                    if slot in h_at:
                        inter(s, p)

            @block.vector
            def _(ve):
                ve.wait_ge(zeroed, 2)

                def weights(s, p):
                    n = h_at[(s, p)]
                    ve.wait_ge(exp_done, 2 * (n + 1))
                    if n >= 2:
                        ve.wait_ge(ii_done, n - 1)
                    ve.scalar_tensor_tensor(out=pt[:, n % 2], in0=ps[:, n % 2, 0:2 * P].rearrange("p (j t) -> p j t", j=2), scalar=QSCALE,
                                            in1=ex[:, n % 2], op0=ALU.mult, op1=ALU.mult).then_inc(p_ready, 1)

                def sums(s, p):
                    n = h_at[(s, p)]
                    hs = h_steps.index(s)
                    if hs >= 2 and p == 0:
                        ve.wait_ge(fin, fin_upto[h_steps[hs - 2]])
                    ve.wait_ge(iv_ready, 2 * (n + 1))
                    ve.tensor_tensor(out=num[:, hs % 2, 2 * p:2 * p + 2, :], in0=ps[:, 2 + n % 2, 0:2 * E_H].rearrange("p (j t) -> p j t", j=2),
                                     in1=iv[:, n % 2], op=ALU.add).then_inc(num_ready, 1)

                def new_state(s, p):
                    n = u_at[(s, p)]
                    d, c = steps[s][:2]
                    ve.wait_ge(upd_done, n + 1)
                    if (s, p) in h_at:
                        ve.wait_ge(ii_done, h_at[(s, p)] + 1)
                    if ct_needed(s, p):
                        ve.wait_ge(ct_ready, 2 * ct_needed(s, p))
                    for j in range(2):
                        h = 2 * p + j
                        r = ROW0[d] + h
                        ve.scalar_tensor_tensor(out=state[:, d, h, :], in0=state[:, d, h, :], scalar=alast[:, c, r:r + 1],
                                                in1=ps[:, 6, j * E_H:(j + 1) * E_H], op0=ALU.mult, op1=ALU.add).then_inc(ct_ready, 1)

                def finish(s):
                    d, c = steps[s][:2]
                    hs = h_steps.index(s)
                    base = fin_upto[s] - fin_len[s]
                    nb = num[:, hs % 2]
                    ve.wait_ge(num_ready, NP_ * (hs + 1))
                    if base:
                        ve.wait_ge(fin, base)
                    ve.scalar_tensor_tensor(out=den[:, 0], in0=nb[:, :, P], scalar=-1.0, in1=nb[:, :, P], op0=ALU.mult, op1=ALU.max).then_inc(fin, 1)
                    ve.wait_ge(fin, base + 1)
                    ve.tensor_tensor(out=den[:, 1], in0=den[:, 0], in1=tok[:, c, 1, ROW0[d]:ROW0[d] + H], op=ALU.max).then_inc(fin, 1)
                    ve.wait_ge(fin, base + 2)
                    ve.reciprocal(den[:, 2], den[:, 1]).then_inc(fin, 1)
                    ve.wait_ge(fin, base + 3)
                    dst = hsum[:, c].rearrange("p (h e) -> p h e", h=H)
                    first = first_visit[s]
                    ve.tensor_tensor(out=dst if first else hb[:], in0=nb[:, :, 0:P], in1=den[:, 2].unsqueeze(2).broadcast_to((P, H, P)),
                                     op=ALU.mult).then_inc(fin, 1)
                    if not first:
                        ve.wait_ge(fin, base + 4)
                        ve.tensor_tensor(out=dst, in0=dst, in1=hb[:], op=ALU.add).then_inc(fin, 1)

                nxt = {slots[i]: slots[i + 1] for i in range(len(slots) - 1)}
                if slots[0] in h_at:
                    weights(*slots[0])
                for slot in slots:
                    s, p = slot
                    if nxt.get(slot) in h_at:
                        weights(*nxt[slot])
                    if slot in h_at:
                        sums(s, p)
                    if slot in u_at:
                        new_state(s, p)
                    if p == NP_ - 1 and s in h_steps:
                        finish(s)

    def standardize(self, x, tiles, groups, width):
        nc = self.nc
        ctx, sb, sem = self.scope()
        parts = max(1, width // BANK)
        w = width // parts
        with ctx:
            stats = sb("stats", [P, NT, groups, parts, 6])
            mv = sb("mv", [P, NT, groups, 2])
            sd = sb("sd", [P, NT, groups])
            rs = sb("rs", [P, NT, groups])
            stat_done, rooted, scaled = sem("stat_done"), sem("rooted"), sem("scaled")
            block = ctx.enter_context(nc.Block())
            ns = groups * parts

            @block.vector
            def _(ve):
                for n, t in enumerate(tiles):
                    base = n * (ns + groups)
                    for g in range(groups):
                        for q in range(parts):
                            c0 = g * width + q * w
                            ve.bn_stats(stats[:, t, g, q, :], x[:, t, c0:c0 + w]).then_inc(stat_done, 1)
                    ve.wait_ge(stat_done, base + ns)
                    for g in range(groups):
                        ve.bn_aggr(mv[:, t, g, :], stats[:, t, g]).then_inc(stat_done, 1)
                for n, t in enumerate(tiles):
                    ve.wait_ge(rooted, n + 1)
                    ve.reciprocal(rs[:, t], sd[:, t]).then_inc(scaled, 1)
                    ve.wait_ge(scaled, n * (groups + 1) + 1)
                    for g in range(groups):
                        xs = x[:, t, g * width:(g + 1) * width]
                        ve.tensor_scalar(xs, xs, mv[:, t, g, 0:1], rs[:, t, g:g + 1], ALU.subtract, ALU.mult).then_inc(scaled, 1)

            @block.scalar
            def _(act):
                for n, t in enumerate(tiles):
                    act.wait_ge(stat_done, (n + 1) * (ns + groups))
                    act.activation(sd[:, t], mv[:, t, :, 1], ACT.Sqrt, bias=self.eps[:, 0:1]).then_inc(rooted, 1)

    def turn(self, src, dst, tiles, scale=None):
        nc, ps = self.nc, self.ps
        ctx, sb, sem = self.scope()
        with ctx:
            turned, act_out, dve_out = sem("turned"), sem("act_out"), sem("dve_out")
            block = ctx.enter_context(nc.Block())

            @block.tensor
            def _(pe):
                for n, t in enumerate(tiles):
                    if n >= 4:
                        pe.wait_ge(act_out, 4 * (n - 3))
                        pe.wait_ge(dve_out, 4 * (n - 3))
                    for k in range(KD):
                        mm = pe.transpose(ps[:, 2 * (n % 4) + k // 4, (k % 4) * P:(k % 4) * P + P], src[:, t, k * P:(k + 1) * P], self.ident[:])
                    mm.then_inc(turned, 1)

            @block.scalar
            def _(act):
                for n, t in enumerate(tiles):
                    act.wait_ge(turned, n + 1)
                    for k in range(4):
                        act.activation(dst[:, k, t * P:(t + 1) * P], ps[:, 2 * (n % 4), k * P:(k + 1) * P], ACT.Copy,
                                       scale=scale[:, k:k + 1] if scale is not None else 1.0).then_inc(act_out, 1)

            @block.vector
            def _(ve):
                for n, t in enumerate(tiles):
                    ve.wait_ge(turned, n + 1)
                    for k in range(4):
                        ve.tensor_scalar(dst[:, 4 + k, t * P:(t + 1) * P], ps[:, 2 * (n % 4) + 1, k * P:(k + 1) * P],
                                         scale[:, 4 + k:5 + k] if scale is not None else 1.0, None, ALU.mult).then_inc(dve_out, 1)

    def merge_branch(self, l, w_p, c_gate, k_bias, hT, brT, merged, t0, add):
        nc, a, ps = self.nc, self.a, self.ps
        ctx, sb, sem = self.scope()
        UN = 2
        w_l = a["w_in"][l]
        pieces = [(0, CTX), (CTX, T)] if t0 == 0 else [(CTX, T)]
        npc = len(pieces)
        with ctx:
            wp = sb("wp", [P, UN, KD, P])
            wg = sb("wg", [P, UN, KD, P])
            sg = sb("sg", [P, UN, T])
            pr = sb("pr", [P, UN, T])
            w_in = [sem(f"w_in{u}") for u in range(UN)]
            g_done, w_used, gated, merged_up, spare = sem("g_done"), sem("w_used"), sem("gated"), sem("merged_up"), sem("spare")
            PER = npc * (2 if add else 1)
            block = ctx.enter_context(nc.Block())

            @block.sync
            def _(sp):
                def load(n, u):
                    sp.dma_start(wg[:, u], wcols_dyn(w_l, n * P + c_gate, P)).then_inc(w_in[u], 16)
                    sp.dma_start(wp[:, u], wcols_dyn(w_p, n * P, P)).then_inc(w_in[u], 16)
                for u in range(UN):
                    load(u, u)
                with sp.Fori(1, KD // UN) as i:
                    for u in range(UN):
                        sp.wait_ge(w_used, i * UN + (u + 1 - UN))
                        load(i * UN + u, u)

            @block.gpsimd
            def _(gp):
                gp.memset(pr[:], 0.0).then_inc(merged_up, UN * PER)

            @block.tensor
            def _(pe):
                with pe.Fori(0, KD // UN) as i:
                    for u in range(UN):
                        pe.wait_ge(w_in[u], i * 32 + 32)
                        pe.wait_ge(merged_up, i * (UN * PER) + (u + 1) * PER)
                        for w, br, o, done in ((wg, hT, 0, g_done), (wp, brT, 2, w_used)):
                            for q, (c0, c1) in enumerate(pieces):
                                for k in range(KD):
                                    mm = pe.matmul(ps[:, 4 * u + o + q, 0:c1 - c0], w[:, u, k, :], br[:, k, c0:c1],
                                                   start=(k == 0), stop=(k == KD - 1))
                            mm.then_inc(done, 1)

            @block.scalar
            def _(act):
                with act.Fori(0, KD // UN) as i:
                    for u in range(UN):
                        act.wait_ge(g_done, i * UN + u + 1)
                        act.wait_ge(merged_up, i * (UN * PER) + (u + 1) * PER)
                        for q, (c0, c1) in enumerate(pieces):
                            act.activation(sg[:, u, c0:c1], ps[:, 4 * u + q, 0:c1 - c0], ACT.Sigmoid,
                                           bias=self.cols[:, l, bass.ds(i * UN + (k_bias + u), 1)]).then_inc(gated, 1)

            @block.vector
            def _(ve):
                with ve.Fori(0, KD // UN) as i:
                    for u in range(UN):
                        ve.wait_ge(w_used, i * UN + u + 1)
                        ve.wait_ge(gated, i * (UN * npc) + npc * (u + 1))
                        ve.wait_ge(merged_up, i * (UN * PER) + (u + UN) * PER)
                        for q, (c0, c1) in enumerate(pieces):
                            g, p = sg[:, u, c0:c1].unsqueeze(1), ps[:, 4 * u + 2 + q, 0:c1 - c0].unsqueeze(1)
                            dst = merged[:, bass.ds(i * UN + u, 1), c0:c1]
                            if add:
                                ve.tensor_tensor(out=pr[:, u, c0:c1].unsqueeze(1), in0=p, in1=g, op=ALU.mult).then_inc(merged_up, 1)
                            else:
                                ve.tensor_tensor(out=dst, in0=p, in1=g, op=ALU.mult).then_inc(merged_up, 1)
                        if add:
                            ve.wait_ge(merged_up, i * (UN * PER) + (UN * PER + u * PER + npc))
                            for q, (c0, c1) in enumerate(pieces):
                                dst = merged[:, bass.ds(i * UN + u, 1), c0:c1]
                                ve.tensor_tensor(out=dst, in0=dst, in1=pr[:, u, c0:c1].unsqueeze(1), op=ALU.add).then_inc(merged_up, 1)

    def times(self, x, y, tiles, bcast=None):
        nc = self.nc
        ctx, sb, sem = self.scope()
        with ctx:
            done, row_in = sem("done"), sem("row_in")
            row = sb("row", [P, D]) if bcast is not None else None
            block = ctx.enter_context(nc.Block())
            if bcast is not None:
                @block.sync
                def _(sp):
                    sp.dma_start(row[:], bcast.broadcast_to((P, D))).then_inc(row_in, 16)

            @block.vector
            def _(ve):
                if bcast is not None:
                    ve.wait_ge(row_in, 16)
                for t in tiles:
                    ve.tensor_tensor(out=x[:, t, :], in0=x[:, t, :], in1=y[:, t, :] if bcast is None else row[:], op=ALU.mult).then_inc(done, 1)

    def spatial(self, l, zv, gu, tiles):
        nc, a, ps = self.nc, self.a, self.ps
        ctx, sb, sem = self.scope()
        with ctx:
            ws = sb("ws", [P, H, P])
            wsT = sb("wsT", [P, H, P])
            w_in, turned, copied, mixed, gated = (sem(n) for n in ("w_in", "turned", "copied", "mixed", "gated"))
            block = ctx.enter_context(nc.Block())
            pieces = [[t for t in tiles if t < CT], [t for t in tiles if t >= CT]]
            pieces = [p for p in pieces if p]

            @block.sync
            def _(sp):
                sp.dma_start(ws[:], a["sgu_w"][l].rearrange("g p q -> p g q")).then_inc(w_in, 16)

            @block.tensor
            def _(pe):
                pe.wait_ge(w_in, 16)
                for g in range(H):
                    mm = pe.transpose(ps[:, g // 4, (g % 4) * P:(g % 4 + 1) * P], ws[:, g, :], self.ident[:])
                mm.then_inc(turned, 1)
                pe.wait_ge(copied, 2)
                n = 0
                for g in range(H):
                    for p in pieces:
                        if n >= 6:
                            pe.wait_ge(gated, n - 5)
                        t0, t1 = p[0], p[-1] + 1
                        pe.matmul(ps[:, 2 + n % 6, 0:(t1 - t0) * P].rearrange("p (t c) -> p t c", c=P), wsT[:, g, :],
                                  zv[:, t0:t1, g * P:(g + 1) * P], start=True, stop=True).then_inc(mixed, 1)
                        n += 1

            @block.vector
            def _(ve):
                ve.wait_ge(turned, 1)
                for j in range(2):
                    ve.tensor_copy(wsT[:, 4 * j:4 * j + 4, :], ps[:, j, :].rearrange("p (g q) -> p g q", g=4)).then_inc(copied, 1)
                n = 0
                for g in range(H):
                    for p in pieces:
                        ve.wait_ge(mixed, n + 1)
                        t0, t1 = p[0], p[-1] + 1
                        dst = gu[:, t0:t1, g * P:(g + 1) * P]
                        ve.scalar_tensor_tensor(out=dst, in0=ps[:, 2 + n % 6, 0:(t1 - t0) * P].rearrange("p (t c) -> p t c", c=P),
                                                scalar=self.cols[:, l, K_SB + g:K_SB + g + 1], in1=dst, op0=ALU.add, op1=ALU.mult).then_inc(gated, 1)
                        n += 1

    def residual_norm(self, l, which, m_gate, y, tiles):
        nc, a, z = self.nc, self.a, self.z
        ctx, sb, sem = self.scope()
        with ctx:
            gate = sb("gate", [P, 2, D])
            lw = sb("lw", [P, D])
            lb = sb("lb", [P, D])
            stats = sb("stats", [P, 2, 2, 6])
            mv = sb("mv", [P, NT, 2])
            sd = sb("sd", [P, NT])
            rs = sb("rs", [P, NT])
            rows_in, gp_done, dve_done, rooted, scaled, z_ready = (
                sem(n) for n in ("rows_in", "gp_done", "dve_done", "rooted", "scaled", "z_ready"))
            block = ctx.enter_context(nc.Block())

            @block.sync
            def _(sp):
                for w in range(2):
                    sp.dma_start(gate[:, w, :], self.mod_dram[l, w:w + 1, m_gate * D:(m_gate + 1) * D].broadcast_to((P, D))).then_inc(rows_in, 16)
                sp.dma_start(lw[:], a["ln_w"][l, which:which + 1, :].broadcast_to((P, D))).then_inc(rows_in, 16)
                sp.dma_start(lb[:], a["ln_b"][l, which:which + 1, :].broadcast_to((P, D))).then_inc(rows_in, 16)

            @block.gpsimd
            def _(gp):
                gp.wait_ge(rows_in, 64)
                for n, t in enumerate(tiles):
                    gp.wait_ge(scaled, 2 * (n + 1))
                    gp.tensor_tensor(out=z[:, t, :], in0=z[:, t, :], in1=lw[:], op=ALU.mult).then_inc(z_ready, 1)
                    gp.wait_ge(z_ready, 2 * n + 1)
                    gp.tensor_tensor(out=z[:, t, :], in0=z[:, t, :], in1=lb[:], op=ALU.add).then_inc(z_ready, 1)

            @block.scalar
            def _(act):
                for n, t in enumerate(tiles):
                    act.wait_ge(dve_done, 5 * (n + 1))
                    act.activation(sd[:, t:t + 1], mv[:, t, 1:2], ACT.Sqrt, bias=self.eps[:, 0:1]).then_inc(rooted, 1)

            @block.vector
            def _(ve):
                ve.wait_ge(rows_in, 64)

                def scale(n):
                    t = tiles[n]
                    ve.wait_ge(rooted, n + 1)
                    ve.reciprocal(rs[:, t:t + 1], sd[:, t:t + 1]).then_inc(scaled, 1)
                    ve.wait_ge(scaled, 2 * n + 1)
                    ve.tensor_scalar(z[:, t, :], z[:, t, :], mv[:, t, 0:1], rs[:, t:t + 1], ALU.subtract, ALU.mult).then_inc(scaled, 1)

                for n, t in enumerate(tiles):
                    base = 5 * n
                    ve.tensor_tensor(out=y[:, t, :], in0=y[:, t, :], in1=gate[:, 1 if t < CT else 0, :], op=ALU.mult).then_inc(dve_done, 1)
                    ve.wait_ge(dve_done, base + 1)
                    ve.scalar_tensor_tensor(out=z[:, t, :], in0=z[:, t, :], scalar=ALPHA, in1=y[:, t, :], op0=ALU.mult, op1=ALU.add).then_inc(dve_done, 1)
                    ve.wait_ge(dve_done, base + 2)
                    for q in range(2):
                        ve.bn_stats(stats[:, n % 2, q, :], z[:, t, q * BANK:(q + 1) * BANK]).then_inc(dve_done, 1)
                    ve.wait_ge(dve_done, base + 4)
                    ve.bn_aggr(mv[:, t, :], stats[:, n % 2]).then_inc(dve_done, 1)
                    if n:
                        scale(n - 1)
                scale(len(tiles) - 1)

    def queries(self, l, hT, qT, kT, t0):
        nc, a, ps = self.nc, self.a, self.ps
        ctx, sb, sem = self.scope()
        UN = 4
        NG = 2 * H
        pieces = [(0, CTX), (CTX, T)] if t0 == 0 else [(CTX, T)]
        npc = len(pieces)
        with ctx:
            wt = sb("wt", [P, UN, KD, P])
            keys = sb("keys", [P, NG, P])
            w_in = [sem(f"w_in{u}") for u in range(UN)]
            k_in, k_turned, w_used, q_out = sem("k_in"), sem("k_turned"), sem("w_used"), sem("q_out")
            k_out = sem("k_out")
            block = ctx.enter_context(nc.Block())

            @block.sync
            def _(sp):
                sp.dma_start(keys[:], a["peer_keys"][l].rearrange("h t k d -> k (h t) d")).then_inc(k_in, 16)

                def load(n, u):
                    sp.dma_start(wt[:, u], wcols_dyn(a["peer_wq"][l], n * P, P)).then_inc(w_in[u], 16)
                for u in range(UN):
                    load(u, u)
                with sp.Fori(1, NG // UN) as i:
                    for u in range(UN):
                        sp.wait_ge(w_used, i * UN + (u + 1 - UN))
                        load(i * UN + u, u)

            @block.tensor
            def _(pe):
                pe.wait_ge(k_in, 16)
                for g in range(NG):
                    mm = pe.transpose(ps[:, g // 4, (g % 4) * P:(g % 4 + 1) * P], keys[:, g, :], self.ident[:])
                    if g % 4 == 3:
                        mm.then_inc(k_turned, 1)
                pe.wait_ge(k_out, 4)
                with pe.Fori(0, NG // UN) as i:
                    for u in range(UN):
                        pe.wait_ge(w_in[u], i * 16 + 16)
                        pe.wait_ge(q_out, i * (UN * npc) + npc * (u + 1))
                        for q, (c0, c1) in enumerate(pieces):
                            for k in range(KD):
                                mm = pe.matmul(ps[:, 2 * u + q, 0:c1 - c0], wt[:, u, k, :], hT[:, k, c0:c1], start=(k == 0), stop=(k == KD - 1))
                        mm.then_inc(w_used, 1)

            @block.scalar
            def _(act):
                for j in range(4):
                    act.wait_ge(k_turned, j + 1)
                    act.activation(kT[:, 4 * j:4 * j + 4, :], ps[:, j, :].rearrange("p (g q) -> p g q", g=4), ACT.Copy).then_inc(k_out, 1)
                act.wait_ge(k_out, 4)
                act.activation(keys[:, 0, :], kT[:, 0, :], ACT.Copy).then_inc(q_out, UN * npc)
                with act.Fori(0, NG // UN) as i:
                    for u in range(UN):
                        act.wait_ge(w_used, i * UN + u + 1)
                        for q, (c0, c1) in enumerate(pieces):
                            act.activation(qT[:, bass.ds(i * UN + u, 1), c0:c1], ps[:, 2 * u + q, 0:c1 - c0].unsqueeze(1), ACT.Copy).then_inc(q_out, 1)

    def select_experts(self, l, t0, qT, kT, idx, gate):
        nc, ps = self.nc, self.ps
        ctx, sb, sem = self.scope()
        NG = 2 * H
        NB = NT - t0
        HC = H * TOPK
        with ctx:
            qb = sb("qb", [P, NG, P])
            sc = sb("sc", [P, NG, P])
            sc2 = sb("sc2", [P, NG, P])
            s16 = sb("s16", [P, NG, TOPK])
            i16 = sb("i16", [P, NG, TOPK], U32)
            i16f = sb("i16f", [P, NG, TOPK])
            cand = sb("cand", [P, H, TOPK * TOPK])
            cand2 = sb("cand2", [P, H, TOPK * TOPK])
            sf = sb("sf", [P, H, TOPK])
            pf = sb("pf", [P, H, TOPK], U32)
            pij = sb("pij", [P, 2, HC], U32)
            pijf = sb("pijf", [P, 2, HC])
            hot = sb("hot", [P, 2, HC, TOPK])
            ids = sb("ids", [P, 2, HC])
            idf = sb("idf", [P, HC])
            iota = sb("iota", [P, TOPK])
            sm = sb("sm", [P, 2, H])
            ex = sb("ex", [P, HC])
            mark = sb("mark", [P, 1])
            iota_ready, q_ready, scored, picked, exped, step = (sem(n) for n in ("iota_ready", "q_ready", "scored", "picked", "exped", "step"))
            block = ctx.enter_context(nc.Block())
            N_STEPS = self.n_select_steps

            @block.gpsimd
            def _(gp):
                gp.iota(iota[:], pattern=[[1, TOPK]], base=0, channel_multiplier=0, allow_small_or_imprecise_dtypes=True).then_inc(iota_ready, 1)

            @block.scalar
            def _(act):
                act.wait_ge(iota_ready, 1)
                with act.Fori(0, NB) as b:
                    act.wait_ge(picked, b + 1)
                    act.activation(qb[:], qT[:, :, bass.ds(b * P + t0 * P, P)], ACT.Copy).then_inc(q_ready, 1)
                    act.wait_ge(step, b * N_STEPS + self.select_exp_step)
                    act.activation(ex[:], idf[:], ACT.Exp).then_inc(exped, 1)

            @block.tensor
            def _(pe):
                with pe.Fori(0, NB) as b:
                    pe.wait_ge(q_ready, b + 1)
                    pe.wait_ge(picked, b + 1)
                    for g in range(NG):
                        mm = pe.matmul(ps[:, g // 4, (g % 4) * P:(g % 4 + 1) * P], qb[:, g, :], kT[:, g, :], start=True, stop=True)
                    mm.then_inc(scored, 1)

            @block.vector
            def _(ve):
                ve.memset(mark[:], 0.0).then_inc(picked, 1)
                ve.wait_ge(picked, 1)
                with ve.Fori(0, NB) as b:
                    n = 0

                    def put(ins):
                        nonlocal n
                        n += 1
                        ins.then_inc(step, 1)

                    def upto():
                        nonlocal n
                        ve.wait_ge(step, b * N_STEPS + n)

                    def hold():
                        upto()
                        put(ve.memset(mark[:], 0.0))

                    ve.wait_ge(scored, b + 1)
                    for j in range(3):
                        put(ve.tensor_copy(sc[:, 4 * j:4 * j + 4, :], ps[:, j, :].rearrange("p (g k) -> p g k", g=4)))
                    put(ve.tensor_copy(sc[:, 12:16, :], ps[:, 3, :].rearrange("p (g k) -> p g k", g=4)))
                    upto()
                    ve.memset(mark[:], 0.0).then_inc(picked, 1)
                    ve.wait_ge(picked, b + 2)
                    put(ve.memset(mark[:], 0.0))
                    for g in range(NG):
                        put(ve.max(s16[:, g, 0:8], sc[:, g, :]))
                    hold()
                    for g in range(NG):
                        put(ve.max_index(i16[:, g, 0:8], s16[:, g, 0:8], sc[:, g, :]))
                        put(ve.match_replace(sc2[:, g, :], s16[:, g, 0:8], sc[:, g, :], -3.0e38))
                    hold()
                    for g in range(NG):
                        put(ve.max(s16[:, g, 8:16], sc2[:, g, :]))
                    hold()
                    for g in range(NG):
                        put(ve.max_index(i16[:, g, 8:16], s16[:, g, 8:16], sc2[:, g, :]))
                    upto()
                    put(ve.tensor_copy(i16f[:], i16[:]))
                    v4 = s16[:].rearrange("p (h t) e -> p h t e", t=2)
                    put(ve.tensor_tensor(out=cand[:].rearrange("p h (i j) -> p h i j", i=TOPK),
                                         in0=v4[:, :, 0, :].unsqueeze(3).broadcast_to((P, H, TOPK, TOPK)),
                                         in1=v4[:, :, 1, :].unsqueeze(2).broadcast_to((P, H, TOPK, TOPK)), op=ALU.add))
                    hold()
                    for h in range(H):
                        put(ve.max(sf[:, h, 0:8], cand[:, h, :]))
                    hold()
                    for h in range(H):
                        put(ve.max_index(pf[:, h, 0:8], sf[:, h, 0:8], cand[:, h, :]))
                        put(ve.match_replace(cand2[:, h, :], sf[:, h, 0:8], cand[:, h, :], -3.0e38))
                    hold()
                    for h in range(H):
                        put(ve.max(sf[:, h, 8:16], cand2[:, h, :]))
                    hold()
                    for h in range(H):
                        put(ve.max_index(pf[:, h, 8:16], sf[:, h, 8:16], cand2[:, h, :]))
                    upto()
                    put(ve.tensor_tensor(out=idf[:].rearrange("p (h e) -> p h e", h=H), in0=sf[:], in1=sf[:, :, 0:1].broadcast_to((P, H, TOPK)), op=ALU.subtract))
                    self.select_exp_step_found = n
                    pflat = pf[:].rearrange("p h e -> p (h e)")
                    put(ve.tensor_single_scalar(pij[:, 0, :], pflat, 4, ALU.logical_shift_right))
                    put(ve.tensor_single_scalar(pij[:, 1, :], pflat, TOPK - 1, ALU.bitwise_and))
                    upto()
                    put(ve.tensor_copy(pijf[:], pij[:]))
                    upto()
                    for t in range(2):
                        put(ve.tensor_tensor(out=hot[:, t], in0=pijf[:, t, :].unsqueeze(2).broadcast_to((P, HC, TOPK)),
                                             in1=iota[:].unsqueeze(1).broadcast_to((P, HC, TOPK)), op=ALU.is_equal))
                    upto()
                    tab = i16f[:].rearrange("p (h t) e -> p h t e", t=2)
                    for t in range(2):
                        ht = hot[:, t].rearrange("p (h e) k -> p h e k", h=H)
                        put(ve.tensor_tensor(out=ht, in0=ht, in1=tab[:, :, t, :].unsqueeze(2).broadcast_to((P, H, TOPK, TOPK)), op=ALU.mult))
                    upto()
                    for t in range(2):
                        put(ve.tensor_reduce(ids[:, t, :], hot[:, t], AX, ALU.add))
                    ve.wait_ge(exped, b + 1)
                    e3 = ex[:].rearrange("p (h e) -> p h e", h=H)
                    put(ve.tensor_reduce(sm[:, 0, :], e3, AX, ALU.add))
                    upto()
                    put(ve.scalar_tensor_tensor(out=idf[:], in0=ids[:, 0, :], scalar=float(P), in1=ids[:, 1, :], op0=ALU.mult, op1=ALU.add))
                    put(ve.reciprocal(sm[:, 1, :], sm[:, 0, :]))
                    upto()
                    put(ve.tensor_scalar(idx[:, bass.ds(b * HC, HC)], idf[:], float(l * N_EXPERTS), None, ALU.add))
                    put(ve.tensor_tensor(out=gate[:, bass.ds(b * HC, HC)].rearrange("p (h e) -> p h e", h=H), in0=e3,
                                         in1=sm[:, 1, :].unsqueeze(2).broadcast_to((P, H, TOPK)), op=ALU.mult))
                    self.n_select_steps_found = n
            assert self.n_select_steps_found == N_STEPS, self.n_select_steps_found
            assert self.select_exp_step_found == self.select_exp_step, self.select_exp_step_found

    def modulate_rows(self, l, hx, tiles):
        nc, z = self.nc, self.z
        ctx, sb, sem = self.scope()
        with ctx:
            sh = sb("sh", [P, 2, D])
            sc = sb("sc", [P, 2, D])
            rows_in, done = sem("rows_in"), sem("done")
            block = ctx.enter_context(nc.Block())

            @block.sync
            def _(sp):
                for w in range(2):
                    sp.dma_start(sh[:, w, :], self.mod_dram[l, w:w + 1, 3 * D:4 * D].broadcast_to((P, D))).then_inc(rows_in, 16)
                    sp.dma_start(sc[:, w, :], self.mod_dram[l, w:w + 1, 4 * D:5 * D].broadcast_to((P, D))).then_inc(rows_in, 16)

            @block.vector
            def _(ve):
                ve.wait_ge(rows_in, 64)
                for n, t in enumerate(tiles):
                    w = 1 if t < CT else 0
                    ve.scalar_tensor_tensor(out=hx[:, t, :], in0=sc[:, w, :], scalar=1.0, in1=z[:, t, :], op0=ALU.add, op1=ALU.mult).then_inc(done, 1)
                    ve.wait_ge(done, 2 * n + 1)
                    ve.tensor_tensor(out=hx[:, t, :], in0=hx[:, t, :], in1=sh[:, w, :], op=ALU.add).then_inc(done, 1)

    def experts(self, l, t0, idx, gate, hx, y):
        nc, a, ps = self.nc, self.a, self.ps
        ctx, sb, sem = self.scope()
        NS = (NT - t0) * H
        R = 8
        tab_u, tab_v = (a[n].rearrange("l e d -> (l e) d") for n in ("expert_u", "expert_v"))
        with ctx:
            ur = sb("ur", [P, R, D])
            vr = sb("vr", [P, R, D])
            junk = sb("junk", [P, 2, D])
            dots = sb("dots", [P, 2, TOPK])
            gl = sb("gl", [P, 2, TOPK])
            wt = sb("wt", [P, 2, TOPK])
            dg = sb("dg", [P, R, P])
            icu = sb("icu", [P, 2, TOPK], U32)
            icv = sb("icv", [P, 2, TOPK], U32)
            u_in = [sem(f"u_in{r}") for r in range(R)]
            v_in = [sem(f"v_in{r}") for r in range(R)]
            dot_done, icu_ready, icv_ready, gelu_done, w_ready, dg_ready, v_used, y_done = (
                sem(n) for n in ("dot_done", "icu_ready", "icv_ready", "gelu_done", "w_ready", "dg_ready", "v_used", "y_done"))
            block = ctx.enter_context(nc.Block())
            gathers = sem("gathers")

            @block.gpsimd
            def _(gp):
                gp.memset(icv[:], 0).then_inc(icv_ready, 1)
                gp.memset(wt[:], 0.0).then_inc(w_ready, 1)
                gp.memset(dg[:], 0.0).then_inc(v_used, TOPK)
                gp.wait_ge(icv_ready, 1)

                def rows_v(n, u, j):
                    gp.wait_ge(v_used, n * TOPK + (j + 1 + TOPK - R))
                    gp.sem_inc(gathers, 1)
                    gp.indirect_dma_start(vr[:, j % R, :], None, tab_v, bass.IndirectOffsetOnAxis(ap=icv[:, (u + 1) % 2, j:j + 1], axis=0)).then_inc(v_in[j % R], 16)

                with gp.Fori(0, NS // 2) as i:
                    for u in range(2):
                        n = i * 2 + u
                        for j in range(TOPK):
                            if j == 0:
                                gp.wait_ge(icu_ready, n + 1)
                            gp.wait_ge(dot_done, n * TOPK + (j + 1))
                            gp.sem_inc(gathers, 1)
                            gp.indirect_dma_start(ur[:, j % R, :], None, tab_u, bass.IndirectOffsetOnAxis(ap=icu[:, u, j:j + 1], axis=0)).then_inc(u_in[j % R], 16)
                            if j == 0:
                                gp.wait_ge(icv_ready, n + 1)
                            rows_v(n, u, j)
                gp.wait_ge(icv_ready, NS + 1)
                for j in range(TOPK):
                    rows_v(NS, 0, j)

            @block.vector
            def _(ve):
                for u in range(2):
                    ve.tensor_copy(icu[:, u, :], idx[:, u * TOPK:(u + 1) * TOPK]).then_inc(icu_ready, 1)
                ve.memset(y[:, 0:2], 0.0).then_inc(dot_done, R)
                ve.memset(y[:, 2:NT + 1], 0.0).then_inc(y_done, 4)
                with ve.Fori(0, NS // 2) as i:
                    for u in range(2):
                        n = i * 2 + u
                        for j in range(TOPK):
                            ve.wait_ge(u_in[j % R], n * (16 * (TOPK // R)) + 16 * (j // R + 1))
                            ve.wait_ge(dot_done, n * TOPK + (R + j - 1))
                            if j == 0:
                                ve.wait_ge(gelu_done, n + 1)
                            ve.scalar_tensor_tensor(out=junk[:, j % 2, :].unsqueeze(1), in0=ur[:, j % R, :].unsqueeze(1), scalar=1.0,
                                                    in1=hx[:, bass.ds(n // H + t0, 1), :], op0=ALU.mult, op1=ALU.mult,
                                                    accum_out=dots[:, u, j:j + 1]).then_inc(dot_done, 1)
                        ve.wait_ge(dot_done, n * TOPK + (R + TOPK))
                        ve.wait_ge(v_used, n * TOPK + TOPK)
                        ve.tensor_copy(icv[:, u, :], idx[:, bass.ds(n * TOPK, TOPK)]).then_inc(icv_ready, 1)
                        ve.tensor_copy(icu[:, u, :], idx[:, bass.ds(n * TOPK + 2 * TOPK, TOPK)]).then_inc(icu_ready, 1)
                        ve.wait_ge(gelu_done, n + 3)
                        ve.wait_ge(dg_ready, n * TOPK + TOPK)
                        ve.tensor_tensor(out=wt[:, u, :], in0=gl[:, u, :], in1=gate[:, bass.ds(n * TOPK, TOPK)], op=ALU.mult).then_inc(w_ready, 1)
                        ve.wait_ge(v_used, n * TOPK + 2 * TOPK)
                        ve.wait_ge(y_done, n * 2 + 4)
                        for q in range(2):
                            dst = y[:, bass.ds((n + (H - 1)) // H + t0, 1), q * BANK:(q + 1) * BANK]
                            ve.tensor_tensor(out=dst, in0=ps[:, 2 * ((u + 1) % 2) + q, :].unsqueeze(1), in1=dst, op=ALU.add).then_inc(y_done, 1)
                ve.wait_ge(v_used, (NS + 2) * TOPK)
                ve.wait_ge(y_done, 2 * NS + 4)
                for q in range(2):
                    dst = y[:, NT, q * BANK:(q + 1) * BANK]
                    ve.tensor_tensor(out=dst, in0=ps[:, 2 + q, :], in1=dst, op=ALU.add).then_inc(y_done, 1)

            @block.scalar
            def _(act):
                act.activation(gl[:, 0, :], self.ones[:, 0:TOPK], ACT.Copy).then_inc(gelu_done, 1)
                act.activation(gl[:, 1, :], self.ones[:, 0:TOPK], ACT.Copy).then_inc(gelu_done, 1)
                act.wait_ge(v_used, TOPK)
                act.wait_ge(gelu_done, 2)

                def diagonals(n, par):
                    act.wait_ge(w_ready, n + 1)
                    for j in range(TOPK):
                        act.wait_ge(v_used, n * TOPK + (j + 1 + TOPK - R))
                        act.activation(dg[:, j % R, :], self.ident[:], ACT.Copy, scale=wt[:, par, j:j + 1]).then_inc(dg_ready, 1)

                with act.Fori(0, NS // 2) as i:
                    for u in range(2):
                        n = i * 2 + u
                        diagonals(n, (u + 1) % 2)
                        act.wait_ge(dot_done, n * TOPK + (R + TOPK))
                        act.activation(gl[:, u, :], dots[:, u, :], ACT.Gelu_apprx_tanh).then_inc(gelu_done, 1)
                diagonals(NS, 1)

            @block.tensor
            def _(pe):
                def head(n, b):
                    pe.wait_ge(y_done, n * 2 + 2)
                    for j in range(TOPK):
                        pe.wait_ge(dg_ready, n * TOPK + (j + 1))
                        pe.wait_ge(v_in[j % R], n * (16 * (TOPK // R)) + 16 * (j // R + 1))
                        for q in range(2):
                            mm = pe.matmul(ps[:, 2 * b + q, :], dg[:, j % R, :], vr[:, j % R, q * BANK:(q + 1) * BANK],
                                           start=(j == 0), stop=(j == TOPK - 1))
                        mm.then_inc(v_used, 1)

                with pe.Fori(0, NS // 2) as i:
                    for u in range(2):
                        head(i * 2 + u, (u + 1) % 2)
                head(NS, 1)

    def build(self):
        nc, a = self.nc, self.a
        ctx = ExitStack()
        with ctx:
            def sb(name, shape, dt=F32):
                return ctx.enter_context(nc.sbuf_tensor(name, shape, dt))

            self.ps = ctx.enter_context(nc.psum_tensor("ps", [P, 8, BANK], F32))
            self.mod_dram = nc.dram_tensor("mod_scratch", (DEPTH, 2, MODW), F32, kind="Internal").ap()
            self.z = sb("z", [P, NT, D])
            self.ident = sb("ident", [P, P])
            self.negident = sb("negident", [P, P])
            self.identb = sb("identb", [P, P], BF16)
            self.mask = sb("mask", [P, 2, 2 * P], BF16)
            self.ones = sb("ones", [P, P])
            self.eps = sb("eps", [P, 1])
            self.cols = sb("cols", [P, DEPTH, K_ALL])
            self.cond = sb("cond", [P, KD, 2])
            self.modc = sb("modc", [P, DEPTH, 2, 6, KD])
            self.setup()
            self.modulation()
            for l in range(DEPTH):
                self.layer(l)
            self.finish_out()

    def layer(self, l):
        nc, a = self.nc, self.a
        t0 = 0 if l < DEPTH - 1 else CT
        tiles = list(range(t0, NT))
        w_l = a["w_in"][l]
        mix, sb, _ = self.scope()
        with mix:
            hT = sb("hT", [P, KD, T])
            hs = sb("hs", [P, NT, D])
            self.modulated_turn(l, 0, hT, 0)
            inner, sb2, _ = self.scope()
            with inner:
                qk = sb2("qk", [P, 2 * KD, T])
                self.project_qk(l, hT, qk)
                v = sb2("v", [P, NT, H, E_H])
                tok = sb2("tok", [P, NT, 4, GR])
                alast = sb2("alast", [P, NT, GR])
                self.m_rows = sb2("m_rows", [GR, T])
                self.ones_column(v)

                def put_v(act, g, t, bank):
                    return act.activation(v[:, t, 4 * g:4 * g + 4, 0:P], bank.rearrange("p (h e) -> p h e", h=4), ACT.Copy)

                self.project_rows([w_l[:, C_V + g * BANK:C_V + (g + 1) * BANK] for g in range(2)], hT, list(range(NT)), put_v)
                self.gates(l, hT, tok, alast)
                self.mlstm(t0, qk, v, tok, alast, hs)
            merged = sb("merged", [P, KD, T])
            brT = sb("brT", [P, KD, T])
            other = sb("other", [P, NT, D])
            self.standardize(hs, tiles, H, P)

            def sig(act, g, t, bank):
                return act.activation(other[:, t, g * BANK:(g + 1) * BANK], bank, ACT.Sigmoid)

            self.project_rows([w_l[:, C_O + g * BANK:C_O + (g + 1) * BANK] for g in range(2)], hT, tiles, sig)
            self.times(hs, other, tiles)
            self.turn(hs, brT, tiles, self.cols[:, l, K_MN:K_MN + KD])
            self.merge_branch(l, a["p_a"][l], C_GA, K_BR, hT, brT, merged, t0, False)

            def gelu_pair(act, g, t, bank):
                dst = hs if g < 2 else other
                return act.activation(dst[:, t, (g % 2) * BANK:(g % 2 + 1) * BANK], bank, ACT.Gelu_apprx_tanh)

            self.project_rows([w_l[:, c0 + g * BANK:c0 + (g + 1) * BANK] for c0 in (C_VG, C_U) for g in range(2)], hT, tiles, gelu_pair)
            self.standardize(hs, tiles, 1, D)
            self.times(hs, None, tiles, a["sgu_norm_w"][l:l + 1, :])
            self.spatial(l, hs, other, tiles)
            self.turn(other, brT, tiles)
            self.merge_branch(l, a["p_b"][l], C_GB, K_BR + KD, hT, brT, merged, t0, True)

            def put_y(act, g, t, bank):
                return act.activation(hs[:, t, g * BANK:(g + 1) * BANK], bank, ACT.Copy)

            self.project_rows([a["w_out"][l][:, g * BANK:(g + 1) * BANK] for g in range(2)], merged, tiles, put_y)
            self.residual_norm(l, 0, 2, hs, tiles)
        peer, sb, _ = self.scope()
        NB = NT - t0
        with peer:
            idx = sb("idx", [P, (NB * H + 2) * TOPK], U32)
            gate = sb("gate", [P, NB * H * TOPK])
            inner, sb2, _ = self.scope()
            with inner:
                hT = sb2("hT", [P, KD, T])
                qT = sb2("qT", [P, 2 * H, T])
                kT = sb2("kT", [P, 2 * H, P])
                self.modulated_turn(l, 3, hT, t0)
                self.queries(l, hT, qT, kT, t0)
                self.zero_tail(idx, NB * H * TOPK)
                self.select_experts(l, t0, qT, kT, idx, gate)
            hx = sb("hx", [P, NT, D])
            y = sb("y", [P, NT + 1, D])
            self.modulate_rows(l, hx, tiles)
            self.experts(l, t0, idx, gate, hx, y)
            self.residual_norm(l, 1, 5, y[:, 1:NT + 1, :], tiles)

    n_select_steps = 149
    select_exp_step = 135
    n_select_steps_found = 0
    select_exp_step_found = 0

    def ones_column(self, v):
        nc = self.nc
        ctx, sb, sem = self.scope()
        with ctx:
            done = sem("done")
            block = ctx.enter_context(nc.Block())

            @block.gpsimd
            def _(gp):
                gp.memset(v[:, :, :, P:E_H], 1.0).then_inc(done, 1)
                gp.memset(self.eps[:], EPS).then_inc(done, 1)

    def zero_tail(self, idx, at):
        nc = self.nc
        ctx, sb, sem = self.scope()
        with ctx:
            done = sem("done")
            block = ctx.enter_context(nc.Block())

            @block.gpsimd
            def _(gp):
                gp.memset(idx[:, at:at + 2 * TOPK], 0).then_inc(done, 1)

    def finish_out(self):
        nc = self.nc
        ctx, sb, sem = self.scope()
        with ctx:
            stored = sem("stored")
            block = ctx.enter_context(nc.Block())

            @block.sync
            def _(sp):
                sp.dma_start(self.out[0].rearrange("(t p) d -> p t d", p=P), self.z[:, CT:NT, :]).then_inc(stored, 16)
                sp.wait_ge(stored, 16)


def chunk_slice(c, d):
    if d == 0:
        return slice(c * P, (c + 1) * P)
    stop = c * P - 1
    return slice((c + 1) * P - 1, stop if stop >= 0 else None, -1)


def wcols_dyn(w, c0, n):
    return w[:, bass.ds(c0, n)].rearrange("(k p) n -> p k n", p=P)


_INS = ['x', 'c', 'ctx', 'c_ctx', 'w_mod', 'b_mod', 'w_in', 'qk_conv_w', 'qk_conv_b', 'gate_b', 'mlstm_norm_w',
        'sgu_norm_w', 'sgu_w', 'sgu_b', 'branch_b', 'p_a', 'p_b', 'w_out', 'ln_w', 'ln_b', 'peer_wq', 'peer_keys',
        'expert_u', 'expert_v']
_OUTS = [((1, SEQ, D), 'float32')]


def kernel(**inputs):
    import numpy as _np
    import concourse.bacc as _bacc
    from concourse import mybir as _mybir
    from concourse.bass_utils import run_bass_kernel_spmd as _run

    nc = _bacc.Bacc("TRN2", target_bir_lowering=False, num_devices=1)
    arrays, args = {}, {}
    for name in _INS:
        a = _np.ascontiguousarray(inputs[name])
        arrays[f"in_{name}_dram"] = a
        args[name] = nc.dram_tensor(f"in_{name}_dram", a.shape, _mybir.dt.from_np(a.dtype), kind="ExternalInput").ap()
    out = nc.dram_tensor("out_0_dram", _OUTS[0][0], _mybir.dt.from_np(_np.dtype(_OUTS[0][1])), kind="ExternalOutput").ap()
    Kernel(nc, args, out).build()
    r = _run(nc, [arrays], core_ids=[0])
    return r.results[0]["out_0_dram"]
```

```python
from contextlib import ExitStack

import concourse.bass as bass
from concourse import mybir

F32 = mybir.dt.float32
BF16 = mybir.dt.bfloat16
U32 = mybir.dt.uint32
ALU = mybir.AluOpType
ACT = mybir.ActivationFunctionType
AX = mybir.AxisListType.X

P = 128
D = 1024
KD = D // P
DEPTH = 2
CTX, SEQ = 256, 512
T = CTX + SEQ
NT = T // P
CT = CTX // P
H = 8
GRID_W = 64
ROWS = SEQ // GRID_W
TAPS = 9
E_H = P + 1
BANK = 512
TOPK = 16
N_EXPERTS = P * P
NEG = -1e30
ALPHA = float((2 * DEPTH) ** 0.25)
EPS = 1e-5
QSCALE = float(P) ** -0.5
MODW = 6 * D
C_QK, C_V, C_O, C_G, C_U = 0, 2 * D, 3 * D, 4 * D, 4 * D + 32
C_VG, C_GA, C_GB = C_U + D, C_U + 2 * D, C_U + 3 * D
K_TAP, K_CB, K_BR, K_MN, K_SB, K_ALL = 0, 144, 160, 176, 184, 192
ORDER = [[0, 1, 2, 3, 4, 5], [1, 0, 5, 4, 3, 2]]
ROW0 = [0, 32]
GR = 40


def wcols(w, c0, n):
    return w[:, c0:c0 + n].rearrange("(k p) n -> p k n", p=P)


class Kernel:
    def __init__(self, nc, a, out):
        self.nc, self.a, self.out = nc, a, out
        self.count = 0

    def scope(self):
        ctx = ExitStack()
        self.count += 1
        tag = f"_{self.count}"

        def sb(name, shape, dt=F32):
            return ctx.enter_context(self.nc.sbuf_tensor(name + tag, shape, dt))

        sems = []

        def sem(name):
            sems.append(self.nc.alloc_semaphore(name + tag))
            return sems[-1]

        def clear():
            if sems:
                self.nc.clear_and_free_semaphores(sems)
                self.nc.all_engine_barrier()

        ctx.callback(clear)
        return ctx, sb, sem

    def setup(self):
        nc, a = self.nc, self.a
        ctx, sb, sem = self.scope()
        z, ident, identb, mask, cols, cond = self.z, self.ident, self.identb, self.mask, self.cols, self.cond
        with ctx:
            rows_a = sb("rows_a", [P, DEPTH, P])
            rows_b = sb("rows_b", [64, DEPTH, P])
            crow = sb("crow", [2 * KD, P])
            csil = sb("csil", [2 * KD, P])
            z_in, rows_in, c_in = sem("z_in"), sem("rows_in"), sem("c_in")
            zeroed, ident_ready, cond_silu = sem("zeroed"), sem("ident_ready"), sem("cond_silu")
            turned, copied, masks_ready = sem("turned"), sem("copied"), sem("masks_ready")
            block = ctx.enter_context(nc.Block())

            @block.sync
            def _(sp):
                sp.dma_start(crow[0:KD, :], a["c"].rearrange("a (k p) -> (a k) p", p=P)).then_inc(c_in, 16)
                sp.dma_start(crow[KD:2 * KD, :], a["c_ctx"].rearrange("(k p) -> k p", p=P)).then_inc(c_in, 16)
                for l in range(DEPTH):
                    taps = a["qk_conv_w"][l].rearrange("i j (c p) -> (i j c) p", p=P)
                    sp.dma_start(rows_a[:, l, :], taps[0:P]).then_inc(rows_in, 16)
                    sp.dma_start(rows_b[0:16, l, :], taps[P:144]).then_inc(rows_in, 16)
                    sp.dma_start(rows_b[16:32, l, :], a["qk_conv_b"][l].rearrange("(c p) -> c p", p=P)).then_inc(rows_in, 16)
                    sp.dma_start(rows_b[32:48, l, :], a["branch_b"][l].rearrange("(c p) -> c p", p=P)).then_inc(rows_in, 16)
                    sp.dma_start(rows_b[48:56, l, :], a["mlstm_norm_w"][l].rearrange("(c p) -> c p", p=P)).then_inc(rows_in, 16)
                    sp.dma_start(rows_b[56:64, l, :], a["sgu_b"][l]).then_inc(rows_in, 16)
                sp.dma_start(z[:, 0:CT, :], a["ctx"][0].rearrange("(t p) d -> p t d", p=P)).then_inc(z_in, 16)
                sp.dma_start(z[:, CT:NT, :], a["x"][0].rearrange("(t p) d -> p t d", p=P)).then_inc(z_in, 16)
                sp.wait_ge(z_in, 32)

            @block.gpsimd
            def _(gp):
                gp.memset(ident[:], 0.0).then_inc(zeroed, 1)
                gp.memset(mask[:], 0.0).then_inc(zeroed, 1)
                gp.memset(self.ones[:], 1.0).then_inc(zeroed, 1)
                gp.wait_ge(zeroed, 3)
                gp.affine_select(out=ident[:], in_=ident[:], compare_op=ALU.not_equal, fill=1.0, base=0,
                                 pattern=[[-1, P]], channel_multiplier=1).then_inc(ident_ready, 1)
                m0 = mask[:, 0, :].rearrange("p (b t) -> p b t", b=2)
                gp.affine_select(out=m0, in_=m0, compare_op=ALU.is_ge, fill=NEG, base=0,
                                 pattern=[[0, 2], [1, P]], channel_multiplier=-1).then_inc(masks_ready, 1)
                m1 = mask[:, 1, :].rearrange("p (b t) -> p b t", b=2)
                gp.affine_select(out=m1, in_=m1, compare_op=ALU.is_ge, fill=NEG, base=0,
                                 pattern=[[0, 2], [-1, P]], channel_multiplier=1).then_inc(masks_ready, 1)
                gp.wait_ge(ident_ready, 1)
                gp.tensor_scalar(self.negident[:], ident[:], -1.0, None, ALU.mult).then_inc(masks_ready, 1)

            @block.scalar
            def _(act):
                act.wait_ge(c_in, 32)
                act.activation(csil[:], crow[:], ACT.Silu).then_inc(cond_silu, 1)

            @block.tensor
            def _(pe):
                pe.wait_ge(ident_ready, 1)
                pe.wait_ge(cond_silu, 1)
                pe.transpose(self.ps[:, 0, 0:2 * KD], csil[:], ident[0:2 * KD, 0:2 * KD]).then_inc(turned, 1)
                pe.wait_ge(rows_in, 16 * 6 * DEPTH)
                for l in range(DEPTH):
                    pe.transpose(self.ps[:, 1 + l, 0:P], rows_a[:, l, :], ident[:])
                    pe.transpose(self.ps[:, 1 + l, P:P + 64], rows_b[:, l, :], ident[0:64, 0:64]).then_inc(turned, 1)

            @block.vector
            def _(ve):
                ve.wait_ge(ident_ready, 1)
                ve.tensor_copy(identb[:], ident[:]).then_inc(copied, 1)
                ve.wait_ge(turned, 1)
                ve.tensor_copy(cond[:], self.ps[:, 0, 0:2 * KD].rearrange("p (w k) -> p k w", w=2)).then_inc(copied, 1)
                ve.wait_ge(turned, 1 + DEPTH)
                for l in range(DEPTH):
                    ve.tensor_copy(cols[:, l, :], self.ps[:, 1 + l, 0:K_ALL]).then_inc(copied, 1)

    def modulation(self):
        nc, a, ps, cond = self.nc, self.a, self.ps, self.cond
        ctx, sb, sem = self.scope()
        W = BANK
        per_layer = MODW // W
        UN = 4
        with ctx:
            wt = sb("wt", [P, UN, KD, W])
            bias = sb("bias", [2, MODW])
            row = sb("row", [2, MODW])
            rows = sb("rows", [96, P])
            w_in = [sem(f"w_in{u}") for u in range(UN)]
            b_in, w_used, row_ready, stored, back = sem("b_in"), sem("w_used"), sem("row_ready"), sem("stored"), sem("back")
            turned, cols_ready = sem("turned"), sem("cols_ready")
            block = ctx.enter_context(nc.Block())

            @block.sync
            def _(sp):
                for l in range(DEPTH):
                    def load(g, u):
                        sp.dma_start(wt[:, u], wcols_dyn(a["w_mod"][l], g * W, W)).then_inc(w_in[u], 16)
                    if l == 0:
                        for u in range(UN):
                            load(u, u)
                    else:
                        for u in range(UN):
                            sp.wait_ge(w_used, per_layer * l - UN + u + 1)
                            load(u, u)
                    with sp.Fori(1, per_layer // UN) as i:
                        for u in range(UN):
                            sp.wait_ge(w_used, i * UN + (per_layer * l - UN + u + 1))
                            load(i * UN + u, u)
                    sp.wait_ge(row_ready, per_layer * (l + 1) + UN)
                    sp.dma_start(self.mod_dram[l], row[:]).then_inc(stored, 16)
                    sp.wait_ge(stored, 16 * (l + 1))
                    for w in range(2):
                        if l:
                            sp.wait_ge(turned, l)
                        sp.dma_start(rows[48 * w:48 * w + 48, :],
                                     self.mod_dram[l, w].rearrange("(r p) -> r p", p=P)).then_inc(back, 16)

            @block.tensor
            def _(pe):
                for l in range(DEPTH):
                    with pe.Fori(0, per_layer // UN) as i:
                        for u in range(UN):
                            pe.wait_ge(w_in[u], i * 16 + 16 * (l * (per_layer // UN) + 1))
                            pe.wait_ge(row_ready, i * UN + per_layer * l + u + 1)
                            for k in range(KD):
                                mm = pe.matmul(ps[0:2, u, :], cond[:, k, :], wt[:, u, k, :], start=(k == 0), stop=(k == KD - 1))
                            mm.then_inc(w_used, 1)
                    pe.wait_ge(back, 32 * (l + 1))
                    pe.transpose(ps[:, 4 + l, 0:96], rows[:], self.ident[0:96, 0:96]).then_inc(turned, 1)

            @block.scalar
            def _(act):
                for l in range(DEPTH):
                    if l:
                        act.wait_ge(row_ready, per_layer * l + UN)
                    act.dma_start(bias[:], a["b_mod"][l:l + 1, :].broadcast_to((2, MODW))).then_inc(b_in, 16)

            @block.vector
            def _(ve):
                ve.memset(row[:], 0.0).then_inc(row_ready, UN)
                ve.wait_ge(row_ready, UN)
                for l in range(DEPTH):
                    ve.wait_ge(b_in, 16 * (l + 1))
                    if l:
                        ve.wait_ge(stored, 16 * l)
                    with ve.Fori(0, per_layer // UN) as i:
                        for u in range(UN):
                            ve.wait_ge(w_used, i * UN + per_layer * l + u + 1)
                            at = bass.ds(i * (UN * W) + u * W, W)
                            ve.tensor_tensor(out=row[:, at], in0=ps[0:2, u, :], in1=bias[:, at], op=ALU.add).then_inc(row_ready, 1)
                    ve.wait_ge(turned, l + 1)
                    mc = self.modc[:, l]
                    ve.tensor_copy(mc, ps[:, 4 + l, 0:96].rearrange("p (w m k) -> p w m k", w=2, m=6)).then_inc(cols_ready, 1)
                    ve.wait_ge(cols_ready, 3 * l + 1)
                    for m in (1, 4):
                        ve.tensor_scalar(mc[:, :, m, :], mc[:, :, m, :], 1.0, None, ALU.add).then_inc(cols_ready, 1)

    def modulated_turn(self, l, m_shift, hT, t0):
        nc, ps = self.nc, self.ps
        ctx, sb, sem = self.scope()
        with ctx:
            turned, act_out, dve_out = sem("turned"), sem("act_out"), sem("dve_out")
            block = ctx.enter_context(nc.Block())
            tiles = list(range(t0, NT))

            def col(t, m, k):
                return self.modc[:, l, 1 if t < CT else 0, m, k:k + 1]

            @block.tensor
            def _(pe):
                for n, t in enumerate(tiles):
                    if n >= 4:
                        pe.wait_ge(act_out, 4 * (n - 3))
                        pe.wait_ge(dve_out, 4 * (n - 3))
                    for k in range(KD):
                        mm = pe.transpose(ps[:, 2 * (n % 4) + k // 4, (k % 4) * P:(k % 4) * P + P],
                                          self.z[:, t, k * P:(k + 1) * P], self.ident[:])
                    mm.then_inc(turned, 1)

            @block.scalar
            def _(act):
                for n, t in enumerate(tiles):
                    act.wait_ge(turned, n + 1)
                    for k in range(4):
                        act.activation(hT[:, k, t * P:(t + 1) * P], ps[:, 2 * (n % 4), k * P:(k + 1) * P], ACT.Identity,
                                       bias=col(t, m_shift, k), scale=col(t, m_shift + 1, k)).then_inc(act_out, 1)

            @block.vector
            def _(ve):
                for n, t in enumerate(tiles):
                    ve.wait_ge(turned, n + 1)
                    for k in range(4):
                        ve.tensor_scalar(hT[:, 4 + k, t * P:(t + 1) * P], ps[:, 2 * (n % 4) + 1, k * P:(k + 1) * P],
                                         col(t, m_shift + 1, 4 + k), col(t, m_shift, 4 + k), ALU.mult, ALU.add).then_inc(dve_out, 1)

    def project_qk(self, l, hT, qk):
        nc, a, ps, cols = self.nc, self.a, self.ps, self.cols
        ctx, sb, sem = self.scope()
        UN = 4
        NC = 2 * D // P
        RH, RW = ROWS + 2, GRID_W + 2
        w_l = a["w_in"][l]
        with ctx:
            wt = sb("wt", [P, UN, KD, P])
            raw_x = sb("raw_x", [P, 2, RH, RW])
            raw_c = sb("raw_c", [P, 2, CTX + 2])
            acc = sb("acc", [P, 2, T])
            w_in = [sem(f"w_in{u}") for u in range(UN)]
            w_used, raw_ready, zeroed, conv_step, silu_done = sem("w_used"), sem("raw_ready"), sem("zeroed"), sem("conv_step"), sem("silu_done")
            STEPS = TAPS + 3
            block = ctx.enter_context(nc.Block())

            @block.sync
            def _(sp):
                def load(n, u):
                    sp.dma_start(wt[:, u], wcols_dyn(w_l, n * P, P)).then_inc(w_in[u], 16)
                for u in range(UN):
                    load(u, u)
                with sp.Fori(1, NC // UN) as i:
                    for u in range(UN):
                        sp.wait_ge(w_used, i * UN + (u + 1 - UN))
                        load(i * UN + u, u)

            @block.tensor
            def _(pe):
                with pe.Fori(0, NC // UN) as i:
                    for u in range(UN):
                        b = 2 * (u % 4)
                        pe.wait_ge(w_in[u], i * 16 + 16)
                        pe.wait_ge(raw_ready, i * 8 + 2 * u + 2)
                        for k in range(KD):
                            pe.matmul(ps[:, b, :], wt[:, u, k, :], hT[:, k, CTX:T], start=(k == 0), stop=(k == KD - 1))
                        for k in range(KD):
                            mm = pe.matmul(ps[:, b + 1, 0:CTX], wt[:, u, k, :], hT[:, k, 0:CTX], start=(k == 0), stop=(k == KD - 1))
                        mm.then_inc(w_used, 1)

            @block.gpsimd
            def _(gp):
                gp.memset(raw_x[:], 0.0).then_inc(raw_ready, 4)
                gp.memset(raw_c[:], 0.0).then_inc(raw_ready, 4)

            @block.scalar
            def _(act):
                act.wait_ge(raw_ready, 8)
                with act.Fori(0, NC // UN) as i:
                    for u in range(UN):
                        s, b = u % 2, 2 * (u % 4)
                        act.wait_ge(w_used, i * UN + u + 1)
                        act.activation(raw_x[:, s, 1:1 + ROWS, 1:1 + GRID_W],
                                       ps[:, b, :].rearrange("p (r w) -> p r w", r=ROWS), ACT.Copy).then_inc(raw_ready, 1)
                        act.activation(raw_c[:, s, 1:1 + CTX], ps[:, b + 1, 0:CTX], ACT.Copy).then_inc(raw_ready, 1)
                        act.wait_ge(conv_step, i * (UN * STEPS) + STEPS * (u + 1))
                        act.activation(qk[:, bass.ds(i * UN + u, 1), :], acc[:, s:s + 1, :], ACT.Silu).then_inc(silu_done, 1)

            @block.vector
            def _(ve):
                with ve.Fori(0, NC // UN) as i:
                    for u in range(UN):
                        s = u % 2
                        ve.wait_ge(raw_ready, i * (2 * UN) + 8 + 2 * (u + 1))
                        def tap(j):
                            return cols[:, l, bass.ds(i * UN + (K_TAP + 16 * j + u), 1)]
                        cb = cols[:, l, bass.ds(i * UN + (K_CB + u), 1)]
                        done = 0
                        for j in range(TAPS):
                            src = raw_x[:, s, j // 3:j // 3 + ROWS, j % 3:j % 3 + GRID_W]
                            dst = acc[:, s, CTX:T].rearrange("p (r w) -> p r w", r=ROWS)
                            if j:
                                ve.wait_ge(conv_step, i * (UN * STEPS) + (STEPS * u + (2 * j - 1 if j < 4 else j + 3)))
                                ve.scalar_tensor_tensor(out=dst, in0=src, scalar=tap(j), in1=dst, op0=ALU.mult, op1=ALU.add).then_inc(conv_step, 1)
                            else:
                                ve.tensor_scalar(dst, src, tap(0), cb, ALU.mult, ALU.add).then_inc(conv_step, 1)
                            if j < 3:
                                src, dst = raw_c[:, s, j:j + CTX], acc[:, s, 0:CTX]
                                if j:
                                    ve.wait_ge(conv_step, i * (UN * STEPS) + (STEPS * u + 2 * j))
                                    ve.scalar_tensor_tensor(out=dst, in0=src, scalar=tap(3 + j), in1=dst, op0=ALU.mult, op1=ALU.add).then_inc(conv_step, 1)
                                else:
                                    ve.tensor_scalar(dst, src, tap(3), cb, ALU.mult, ALU.add).then_inc(conv_step, 1)

    def project_rows(self, sources, actT, tiles, evacuate, extra=None):
        nc, ps = self.nc, self.ps
        ctx, sb, sem = self.scope()
        NS = 2
        G = len(sources)
        with ctx:
            wt = sb("wt", [P, NS, KD, BANK])
            w_in = [sem(f"w_in{s}") for s in range(NS)]
            mm_done, evacuated = sem("mm_done"), sem("evacuated")
            block = ctx.enter_context(nc.Block())

            @block.sync
            def _(sp):
                for g, src in enumerate(sources):
                    if g >= NS:
                        sp.wait_ge(mm_done, (g - NS + 1) * len(tiles))
                    for half in range(2):
                        k0 = half * KD // 2
                        sp.dma_start(wt[:, g % NS, k0:k0 + KD // 2, :],
                                     src[k0 * P:(k0 + KD // 2) * P, :].rearrange("(k p) n -> p k n", p=P)).then_inc(w_in[g % NS], 16)

            @block.tensor
            def _(pe):
                n = 0
                for g in range(G):
                    pe.wait_ge(w_in[g % NS], 32 * (g // NS + 1))
                    for t in tiles:
                        if n >= 8:
                            pe.wait_ge(evacuated, n - 7)
                        for k in range(KD):
                            mm = pe.matmul(ps[:, n % 8, :], actT[:, k, t * P:(t + 1) * P], wt[:, g % NS, k, :],
                                           start=(k == 0), stop=(k == KD - 1))
                        mm.then_inc(mm_done, 1)
                        n += 1

            @block.scalar
            def _(act):
                n = 0
                for g in range(G):
                    for t in tiles:
                        act.wait_ge(mm_done, n + 1)
                        evacuate(act, g, t, ps[:, n % 8, :]).then_inc(evacuated, 1)
                        n += 1

    def gates(self, l, hT, tok, alast):
        nc, a, ps, ident = self.nc, self.a, self.ps, self.ident
        ctx, sb, sem = self.scope()
        w_l = a["w_in"][l]
        M = self.m_rows
        with ctx:
            wg = sb("wg", [P, KD, 2, GR])
            gb = sb("gb", [GR, 2])
            gi, gf, t1, t2, b_, c_ = (sb(n, [GR, T]) for n in ("gi", "gf", "t1", "t2", "b_", "c_"))
            one = sb("one", [GR, P])
            mprev = sb("mprev", [GR, NT])
            nlast = sb("nlast", [GR, NT])
            al = sb("al", [GR, NT])
            ald = sb("ald", [GR, NT, GR])
            av, ev, wv = (sb(n, [GR, T]) for n in ("av", "ev", "wv"))
            zeroed, w_in, g_mm, act_done, dve_done, turned, out_done = (
                sem(n) for n in ("zeroed", "w_in", "g_mm", "act_done", "dve_done", "turned", "out_done"))
            N_ABS = 5
            N_LF = N_ABS + 1
            N_M = N_LF + 2 * NT + 1 + (6 * NT - 2) + NT
            N_DVE = N_M + NT
            block = ctx.enter_context(nc.Block())

            @block.gpsimd
            def _(gp):
                gp.memset(wg[:], 0.0).then_inc(zeroed, 1)
                gp.memset(gb[:], 0.0).then_inc(zeroed, 1)
                gp.memset(one[:], 1.0).then_inc(zeroed, 1)
                for x in (mprev, nlast, al, b_, M):
                    gp.memset(x[:], 0.0).then_inc(zeroed, 1)
                gp.wait_ge(zeroed, 8)
                for d in range(2):
                    c = ORDER[d][0]
                    gp.memset(mprev[ROW0[d]:ROW0[d] + H, c:c + 1], NEG).then_inc(zeroed, 1)

            @block.sync
            def _(sp):
                sp.wait_ge(zeroed, 2)
                for d in range(2):
                    for kind in range(2):
                        c0 = C_G + 16 * d + 8 * kind
                        sp.dma_start(wg[:, :, kind, ROW0[d]:ROW0[d] + H],
                                     w_l[:, c0:c0 + H].rearrange("(k p) n -> p k n", p=P)).then_inc(w_in, 16)
                        g0 = 16 * d + 8 * kind
                        sp.dma_start(gb[ROW0[d]:ROW0[d] + H, kind:kind + 1],
                                     a["gate_b"][l, g0:g0 + H].rearrange("(n o) -> n o", o=1)).then_inc(w_in, 16)

            @block.tensor
            def _(pe):
                pe.wait_ge(w_in, 16 * 8)
                for kind in range(2):
                    for k in range(KD):
                        pe.matmul(ps[0:GR, 2 * kind, 0:BANK], wg[:, k, kind, :], hT[:, k, 0:BANK], start=(k == 0), stop=(k == KD - 1))
                    for k in range(KD):
                        mm = pe.matmul(ps[0:GR, 2 * kind + 1, 0:T - BANK], wg[:, k, kind, :], hT[:, k, BANK:T], start=(k == 0), stop=(k == KD - 1))
                    mm.then_inc(g_mm, 1)
                pe.wait_ge(act_done, 3 + 3 * NT)
                for c in range(NT):
                    for n, x in enumerate((av, ev, wv, c_)):
                        mm = pe.transpose(ps[:, c, n * GR:(n + 1) * GR], x[:, c * P:(c + 1) * P], ident[0:GR, 0:GR])
                    mm.then_inc(turned, 1)
                pe.wait_ge(dve_done, N_DVE)
                pe.matmul(ps[:, 6, 0:NT * GR], self.ones[0:GR, :], ald[:].rearrange("p c r -> p (c r)"), start=True, stop=True).then_inc(turned, 1)

            @block.scalar
            def _(act):
                act.wait_ge(dve_done, N_ABS)
                act.activation(t1[:], t1[:], ACT.Exp, scale=-1.0).then_inc(act_done, 1)
                act.wait_ge(act_done, 1)
                act.activation(t2[:], t1[:], ACT.Ln, bias=1.0).then_inc(act_done, 1)
                act.wait_ge(dve_done, N_M)
                act.activation(ev[:], t1[:], ACT.Exp, scale=-1.0).then_inc(act_done, 1)
                for c in range(NT):
                    cs = slice(c * P, (c + 1) * P)
                    act.activation(av[:, cs], M[:, cs], ACT.Exp, bias=mprev[:, c:c + 1], scale=-1.0).then_inc(act_done, 1)
                    act.activation(wv[:, cs], c_[:, cs], ACT.Exp, bias=nlast[:, c:c + 1]).then_inc(act_done, 1)
                    act.activation(al[:, c:c + 1], nlast[:, c:c + 1], ACT.Exp, bias=mprev[:, c:c + 1]).then_inc(act_done, 1)

            @block.vector
            def _(ve):
                n = 0

                def after(ins):
                    nonlocal n
                    n += 1
                    ins.then_inc(dve_done, 1)
                    ve.wait_ge(dve_done, n)

                def take(ins):
                    nonlocal n
                    n += 1
                    ins.then_inc(dve_done, 1)

                ve.wait_ge(zeroed, 10)
                ve.wait_ge(g_mm, 2)
                i2 = gi
                take(ve.tensor_scalar(i2[:, 0:BANK], ps[0:GR, 0, :], gb[:, 0:1], None, ALU.add))
                take(ve.tensor_scalar(i2[:, BANK:T], ps[0:GR, 1, 0:T - BANK], gb[:, 0:1], None, ALU.add))
                take(ve.tensor_scalar(gf[:, 0:BANK], ps[0:GR, 2, :], gb[:, 1:2], None, ALU.add))
                after(ve.tensor_scalar(gf[:, BANK:T], ps[0:GR, 3, 0:T - BANK], gb[:, 1:2], None, ALU.add))
                after(ve.scalar_tensor_tensor(out=t1[:], in0=gf[:], scalar=-1.0, in1=gf[:], op0=ALU.mult, op1=ALU.max))
                assert n == N_ABS
                ve.wait_ge(act_done, 2)
                after(ve.scalar_tensor_tensor(out=gf[:], in0=gf[:], scalar=0.0, in1=t2[:], op0=ALU.min, op1=ALU.subtract))
                for d in range(2):
                    r = slice(ROW0[d], ROW0[d] + H)
                    for c in range(NT):
                        cs = chunk_slice(c, d)
                        take(ve.tensor_tensor_scan(b_[r, cs], one[r, :], gf[r, cs], 0.0, ALU.mult, ALU.add))
                ve.wait_ge(dve_done, n)
                after(ve.tensor_tensor(out=c_[:], in0=gi[:], in1=b_[:], op=ALU.subtract))
                for pos in range(NT):
                    for d in range(2):
                        c = ORDER[d][pos]
                        r = slice(ROW0[d], ROW0[d] + H)
                        last = c * P + (P - 1 if d == 0 else 0)
                        cs = chunk_slice(c, d)
                        after(ve.tensor_tensor_scan(M[r, cs], c_[r, cs], c_[r, cs], mprev[r, c:c + 1], ALU.max, ALU.max))
                        take(ve.tensor_scalar(nlast[r, c:c + 1], M[r, last:last + 1], -1.0, None, ALU.mult))
                        if pos < NT - 1:
                            nx = ORDER[d][pos + 1]
                            take(ve.tensor_tensor(out=mprev[r, nx:nx + 1], in0=M[r, last:last + 1], in1=b_[r, last:last + 1], op=ALU.add))
                        ve.wait_ge(dve_done, n)
                for c in range(NT):
                    cs = slice(c * P, (c + 1) * P)
                    take(ve.tensor_tensor(out=t1[:, cs], in0=M[:, cs], in1=b_[:, cs], op=ALU.add))
                ve.wait_ge(act_done, 3 + 3 * NT)
                for c in range(NT):
                    take(ve.tensor_scalar(ald[:, c, :], ident[0:GR, 0:GR], al[:, c:c + 1], None, ALU.mult))
                assert n == N_DVE, (n, N_DVE)
                for c in range(NT):
                    ve.wait_ge(turned, c + 1)
                    ve.tensor_copy(tok[:, c], ps[:, c, 0:4 * GR].rearrange("p (n r) -> p n r", n=4)).then_inc(out_done, 1)
                ve.wait_ge(turned, NT + 1)
                ve.tensor_copy(alast[:], ps[:, 6, 0:NT * GR].rearrange("p (c r) -> p c r", c=NT)).then_inc(out_done, 1)
                ve.wait_ge(out_done, NT)
                ve.tensor_scalar(tok[:, :, 0, :], tok[:, :, 0, :], QSCALE, None, ALU.mult).then_inc(out_done, 1)

    def mlstm(self, t0, qk, v, tok, alast, hsum):
        nc, ps = self.nc, self.ps
        ctx, sb, sem = self.scope()
        M = self.m_rows
        steps = [(d, ORDER[d][pos], ORDER[d][pos] >= t0, pos < NT - 1) for pos in range(NT) for d in range(2)]
        NP_ = H // 2
        hu = []
        uu = []
        for s, (d, c, has_h, has_u) in enumerate(steps):
            for p in range(NP_):
                if has_h:
                    hu.append((s, p))
                if has_u:
                    uu.append((s, p))
        h_at = {x: n for n, x in enumerate(hu)}
        u_at = {x: n for n, x in enumerate(uu)}
        slots = [(s, p) for s in range(len(steps)) for p in range(NP_)]
        h_steps = [s for s in range(len(steps)) if steps[s][2]]
        u_steps = [s for s in range(len(steps)) if steps[s][3]]
        seen = set()
        first_visit = {}
        for s in h_steps:
            first_visit[s] = steps[s][1] not in seen
            seen.add(steps[s][1])
        fin_len = {s: 4 if first_visit[s] else 5 for s in h_steps}
        fin_upto = {}
        total = 0
        for s in h_steps:
            total += fin_len[s]
            fin_upto[s] = total

        def ct_needed(s, p):
            d = steps[s][0]
            before = [x for x in u_steps if x < s and steps[x][0] == d]
            return u_at[(before[-1], p)] + 1 if before else 0

        def after_unit(slot, units_at):
            return units_at.get(slot)

        with ctx:
            state = sb("state", [P, 2, H, E_H])
            ktok = sb("ktok", [P, 2, D])
            vw = sb("vw", [P, 2, H, E_H])
            ex = sb("ex", [P, 2, 2, P])
            pt = sb("pt", [P, 2, 2, P])
            iv = sb("iv", [P, 2, 2, E_H])
            num = sb("num", [P, 2, H, E_H])
            den = sb("den", [P, 3, H])
            hb = sb("hb", [P, H, P])
            zeroed, sb_done, exp_done, p_ready, ii_done, iv_ready, num_ready, upd_done, ct_ready = (
                sem(n) for n in ("zeroed", "sb_done", "exp_done", "p_ready", "ii_done", "iv_ready", "num_ready", "upd_done", "ct_ready"))
            ktr_done, ktok_ready, vw_ready, fin = sem("ktr_done"), sem("ktok_ready"), sem("vw_ready"), sem("fin")
            block = ctx.enter_context(nc.Block())

            @block.gpsimd
            def _(gp):
                for d in range(2):
                    gp.memset(state[:, d], 0.0).then_inc(zeroed, 1)
                for n, s in enumerate(u_steps):
                    d, c = steps[s][:2]
                    if n >= 2:
                        gp.wait_ge(upd_done, NP_ * (n - 1))
                    wl = tok[:, c, 2, ROW0[d]:ROW0[d] + H]
                    gp.tensor_tensor(out=vw[:, n % 2], in0=v[:, c], in1=wl.unsqueeze(2).broadcast_to((P, H, E_H)), op=ALU.mult).then_inc(vw_ready, 1)

            @block.tensor
            def _(pe):
                pe.wait_ge(zeroed, 2)

                def scores(s, p):
                    n = h_at[(s, p)]
                    d, c = steps[s][:2]
                    cs = slice(c * P, (c + 1) * P)
                    if n >= 2:
                        pe.wait_ge(p_ready, n - 1)
                    for j in range(2):
                        h = 2 * p + j
                        pe.matmul(ps[:, n % 2, j * P:(j + 1) * P], qk[:, H + h, cs], qk[:, h, cs], start=True, stop=True)
                    pe.matmul(ps[:, n % 2, 2 * P:4 * P], self.identb[:], self.mask[:, d, :], start=True, stop=False, skip_group_check=True)
                    for j in range(2):
                        r = ROW0[d] + 2 * p + j
                        mm = pe.matmul(ps[:, n % 2, (2 + j) * P:(3 + j) * P], self.negident[0:GR, r:r + 1].broadcast_to((GR, P)),
                                       M[:, cs], start=False, stop=True, skip_group_check=True)
                    mm.then_inc(sb_done, 1)

                def outputs(s, p):
                    n = h_at[(s, p)]
                    d, c = steps[s][:2]
                    cs = slice(c * P, (c + 1) * P)
                    if n >= 2:
                        pe.wait_ge(num_ready, n - 1)
                    need = ct_needed(s, p)
                    if need:
                        pe.wait_ge(ct_ready, 2 * need)
                    for j in range(2):
                        h = 2 * p + j
                        pe.matmul(ps[:, 4 + n % 2, j * E_H:(j + 1) * E_H], qk[:, h, cs], state[:, d, h, :], start=True, stop=True)
                    pe.wait_ge(p_ready, n + 1)
                    for j in range(2):
                        mm = pe.matmul(ps[:, 2 + n % 2, j * E_H:(j + 1) * E_H], pt[:, n % 2, j, :], v[:, c, 2 * p + j, :], start=True, stop=True)
                    mm.then_inc(ii_done, 1)

                def k_rows(s):
                    n = u_steps.index(s)
                    c = steps[s][1]
                    cs = slice(c * P, (c + 1) * P)
                    for half in range(2):
                        if 2 * n + half >= 1:
                            pe.wait_ge(ktok_ready, 2 * n + half)
                        for j in range(4):
                            mm = pe.transpose(ps[:, 7, j * P:(j + 1) * P], qk[:, H + 4 * half + j, cs], self.ident[:])
                        mm.then_inc(ktr_done, 1)

                def update(s, p):
                    n = u_at[(s, p)]
                    us = u_steps.index(s)
                    if n >= 1:
                        pe.wait_ge(ct_ready, 2 * n)
                    pe.wait_ge(ktok_ready, 2 * us + p // 2 + 1)
                    pe.wait_ge(vw_ready, us + 1)
                    for j in range(2):
                        h = 2 * p + j
                        mm = pe.matmul(ps[:, 6, j * E_H:(j + 1) * E_H], ktok[:, us % 2, h * P:(h + 1) * P], vw[:, us % 2, h, :], start=True, stop=True)
                    mm.then_inc(upd_done, 1)

                nxt = {slots[i]: slots[i + 1] for i in range(len(slots) - 1)}
                if slots[0] in h_at:
                    scores(*slots[0])
                for slot in slots:
                    s, p = slot
                    if p == 0 and s in u_steps:
                        k_rows(s)
                    if nxt.get(slot) in h_at:
                        scores(*nxt[slot])
                    if slot in h_at:
                        outputs(s, p)
                    if slot in u_at:
                        update(s, p)

            @block.scalar
            def _(act):
                def exps(s, p):
                    n = h_at[(s, p)]
                    d, c = steps[s][:2]
                    act.wait_ge(sb_done, n + 1)
                    if n >= 2:
                        act.wait_ge(p_ready, n - 1)
                    for j in range(2):
                        r = ROW0[d] + 2 * p + j
                        act.activation(ex[:, n % 2, j, :], ps[:, n % 2, (2 + j) * P:(3 + j) * P], ACT.Exp,
                                       bias=tok[:, c, 3, r:r + 1]).then_inc(exp_done, 1)

                def inter(s, p):
                    n = h_at[(s, p)]
                    d, c = steps[s][:2]
                    act.wait_ge(ii_done, n + 1)
                    if n >= 2:
                        act.wait_ge(num_ready, n - 1)
                    for j in range(2):
                        r = ROW0[d] + 2 * p + j
                        act.activation(iv[:, n % 2, j, :], ps[:, 4 + n % 2, j * E_H:(j + 1) * E_H], ACT.Copy,
                                       scale=tok[:, c, 0, r:r + 1]).then_inc(iv_ready, 1)

                nxt = {slots[i]: slots[i + 1] for i in range(len(slots) - 1)}
                if slots[0] in h_at:
                    exps(*slots[0])
                for slot in slots:
                    s, p = slot
                    if p == 0 and s in u_steps:
                        us = u_steps.index(s)
                        if us >= 2:
                            act.wait_ge(upd_done, NP_ * (us - 1))
                        for half in range(2):
                            act.wait_ge(ktr_done, 2 * us + half + 1)
                            act.activation(ktok[:, us % 2, half * BANK:(half + 1) * BANK], ps[:, 7, :], ACT.Copy).then_inc(ktok_ready, 1)
                    if nxt.get(slot) in h_at:
                        exps(*nxt[slot])
                    if slot in h_at:
                        inter(s, p)

            @block.vector
            def _(ve):
                ve.wait_ge(zeroed, 2)

                def weights(s, p):
                    n = h_at[(s, p)]
                    ve.wait_ge(exp_done, 2 * (n + 1))
                    if n >= 2:
                        ve.wait_ge(ii_done, n - 1)
                    ve.scalar_tensor_tensor(out=pt[:, n % 2], in0=ps[:, n % 2, 0:2 * P].rearrange("p (j t) -> p j t", j=2), scalar=QSCALE,
                                            in1=ex[:, n % 2], op0=ALU.mult, op1=ALU.mult).then_inc(p_ready, 1)

                def sums(s, p):
                    n = h_at[(s, p)]
                    hs = h_steps.index(s)
                    if hs >= 2 and p == 0:
                        ve.wait_ge(fin, fin_upto[h_steps[hs - 2]])
                    ve.wait_ge(iv_ready, 2 * (n + 1))
                    ve.tensor_tensor(out=num[:, hs % 2, 2 * p:2 * p + 2, :], in0=ps[:, 2 + n % 2, 0:2 * E_H].rearrange("p (j t) -> p j t", j=2),
                                     in1=iv[:, n % 2], op=ALU.add).then_inc(num_ready, 1)

                def new_state(s, p):
                    n = u_at[(s, p)]
                    d, c = steps[s][:2]
                    ve.wait_ge(upd_done, n + 1)
                    if (s, p) in h_at:
                        ve.wait_ge(ii_done, h_at[(s, p)] + 1)
                    if ct_needed(s, p):
                        ve.wait_ge(ct_ready, 2 * ct_needed(s, p))
                    for j in range(2):
                        h = 2 * p + j
                        r = ROW0[d] + h
                        ve.scalar_tensor_tensor(out=state[:, d, h, :], in0=state[:, d, h, :], scalar=alast[:, c, r:r + 1],
                                                in1=ps[:, 6, j * E_H:(j + 1) * E_H], op0=ALU.mult, op1=ALU.add).then_inc(ct_ready, 1)

                def finish(s):
                    d, c = steps[s][:2]
                    hs = h_steps.index(s)
                    base = fin_upto[s] - fin_len[s]
                    nb = num[:, hs % 2]
                    ve.wait_ge(num_ready, NP_ * (hs + 1))
                    if base:
                        ve.wait_ge(fin, base)
                    ve.scalar_tensor_tensor(out=den[:, 0], in0=nb[:, :, P], scalar=-1.0, in1=nb[:, :, P], op0=ALU.mult, op1=ALU.max).then_inc(fin, 1)
                    ve.wait_ge(fin, base + 1)
                    ve.tensor_tensor(out=den[:, 1], in0=den[:, 0], in1=tok[:, c, 1, ROW0[d]:ROW0[d] + H], op=ALU.max).then_inc(fin, 1)
                    ve.wait_ge(fin, base + 2)
                    ve.reciprocal(den[:, 2], den[:, 1]).then_inc(fin, 1)
                    ve.wait_ge(fin, base + 3)
                    dst = hsum[:, c].rearrange("p (h e) -> p h e", h=H)
                    first = first_visit[s]
                    ve.tensor_tensor(out=dst if first else hb[:], in0=nb[:, :, 0:P], in1=den[:, 2].unsqueeze(2).broadcast_to((P, H, P)),
                                     op=ALU.mult).then_inc(fin, 1)
                    if not first:
                        ve.wait_ge(fin, base + 4)
                        ve.tensor_tensor(out=dst, in0=dst, in1=hb[:], op=ALU.add).then_inc(fin, 1)

                nxt = {slots[i]: slots[i + 1] for i in range(len(slots) - 1)}
                if slots[0] in h_at:
                    weights(*slots[0])
                for slot in slots:
                    s, p = slot
                    if nxt.get(slot) in h_at:
                        weights(*nxt[slot])
                    if slot in h_at:
                        sums(s, p)
                    if slot in u_at:
                        new_state(s, p)
                    if p == NP_ - 1 and s in h_steps:
                        finish(s)

    def standardize(self, x, tiles, groups, width):
        nc = self.nc
        ctx, sb, sem = self.scope()
        parts = max(1, width // BANK)
        w = width // parts
        with ctx:
            stats = sb("stats", [P, NT, groups, parts, 6])
            mv = sb("mv", [P, NT, groups, 2])
            sd = sb("sd", [P, NT, groups])
            rs = sb("rs", [P, NT, groups])
            stat_done, rooted, scaled = sem("stat_done"), sem("rooted"), sem("scaled")
            block = ctx.enter_context(nc.Block())
            ns = groups * parts

            @block.vector
            def _(ve):
                for n, t in enumerate(tiles):
                    base = n * (ns + groups)
                    for g in range(groups):
                        for q in range(parts):
                            c0 = g * width + q * w
                            ve.bn_stats(stats[:, t, g, q, :], x[:, t, c0:c0 + w]).then_inc(stat_done, 1)
                    ve.wait_ge(stat_done, base + ns)
                    for g in range(groups):
                        ve.bn_aggr(mv[:, t, g, :], stats[:, t, g]).then_inc(stat_done, 1)
                for n, t in enumerate(tiles):
                    ve.wait_ge(rooted, n + 1)
                    ve.reciprocal(rs[:, t], sd[:, t]).then_inc(scaled, 1)
                    ve.wait_ge(scaled, n * (groups + 1) + 1)
                    for g in range(groups):
                        xs = x[:, t, g * width:(g + 1) * width]
                        ve.tensor_scalar(xs, xs, mv[:, t, g, 0:1], rs[:, t, g:g + 1], ALU.subtract, ALU.mult).then_inc(scaled, 1)

            @block.scalar
            def _(act):
                for n, t in enumerate(tiles):
                    act.wait_ge(stat_done, (n + 1) * (ns + groups))
                    act.activation(sd[:, t], mv[:, t, :, 1], ACT.Sqrt, bias=self.eps[:, 0:1]).then_inc(rooted, 1)

    def turn(self, src, dst, tiles, scale=None):
        nc, ps = self.nc, self.ps
        ctx, sb, sem = self.scope()
        with ctx:
            turned, act_out, dve_out = sem("turned"), sem("act_out"), sem("dve_out")
            block = ctx.enter_context(nc.Block())

            @block.tensor
            def _(pe):
                for n, t in enumerate(tiles):
                    if n >= 4:
                        pe.wait_ge(act_out, 4 * (n - 3))
                        pe.wait_ge(dve_out, 4 * (n - 3))
                    for k in range(KD):
                        mm = pe.transpose(ps[:, 2 * (n % 4) + k // 4, (k % 4) * P:(k % 4) * P + P], src[:, t, k * P:(k + 1) * P], self.ident[:])
                    mm.then_inc(turned, 1)

            @block.scalar
            def _(act):
                for n, t in enumerate(tiles):
                    act.wait_ge(turned, n + 1)
                    for k in range(4):
                        act.activation(dst[:, k, t * P:(t + 1) * P], ps[:, 2 * (n % 4), k * P:(k + 1) * P], ACT.Copy,
                                       scale=scale[:, k:k + 1] if scale is not None else 1.0).then_inc(act_out, 1)

            @block.vector
            def _(ve):
                for n, t in enumerate(tiles):
                    ve.wait_ge(turned, n + 1)
                    for k in range(4):
                        ve.tensor_scalar(dst[:, 4 + k, t * P:(t + 1) * P], ps[:, 2 * (n % 4) + 1, k * P:(k + 1) * P],
                                         scale[:, 4 + k:5 + k] if scale is not None else 1.0, None, ALU.mult).then_inc(dve_out, 1)

    def merge_branch(self, l, w_p, c_gate, k_bias, hT, brT, merged, t0, add):
        nc, a, ps = self.nc, self.a, self.ps
        ctx, sb, sem = self.scope()
        UN = 2
        w_l = a["w_in"][l]
        pieces = [(0, CTX), (CTX, T)] if t0 == 0 else [(CTX, T)]
        npc = len(pieces)
        with ctx:
            wp = sb("wp", [P, UN, KD, P])
            wg = sb("wg", [P, UN, KD, P])
            sg = sb("sg", [P, UN, T])
            pr = sb("pr", [P, UN, T])
            w_in = [sem(f"w_in{u}") for u in range(UN)]
            g_done, w_used, gated, merged_up, spare = sem("g_done"), sem("w_used"), sem("gated"), sem("merged_up"), sem("spare")
            PER = npc * (2 if add else 1)
            block = ctx.enter_context(nc.Block())

            @block.sync
            def _(sp):
                def load(n, u):
                    sp.dma_start(wg[:, u], wcols_dyn(w_l, n * P + c_gate, P)).then_inc(w_in[u], 16)
                    sp.dma_start(wp[:, u], wcols_dyn(w_p, n * P, P)).then_inc(w_in[u], 16)
                for u in range(UN):
                    load(u, u)
                with sp.Fori(1, KD // UN) as i:
                    for u in range(UN):
                        sp.wait_ge(w_used, i * UN + (u + 1 - UN))
                        load(i * UN + u, u)

            @block.gpsimd
            def _(gp):
                gp.memset(pr[:], 0.0).then_inc(merged_up, UN * PER)

            @block.tensor
            def _(pe):
                with pe.Fori(0, KD // UN) as i:
                    for u in range(UN):
                        pe.wait_ge(w_in[u], i * 32 + 32)
                        pe.wait_ge(merged_up, i * (UN * PER) + (u + 1) * PER)
                        for w, br, o, done in ((wg, hT, 0, g_done), (wp, brT, 2, w_used)):
                            for q, (c0, c1) in enumerate(pieces):
                                for k in range(KD):
                                    mm = pe.matmul(ps[:, 4 * u + o + q, 0:c1 - c0], w[:, u, k, :], br[:, k, c0:c1],
                                                   start=(k == 0), stop=(k == KD - 1))
                            mm.then_inc(done, 1)

            @block.scalar
            def _(act):
                with act.Fori(0, KD // UN) as i:
                    for u in range(UN):
                        act.wait_ge(g_done, i * UN + u + 1)
                        act.wait_ge(merged_up, i * (UN * PER) + (u + 1) * PER)
                        for q, (c0, c1) in enumerate(pieces):
                            act.activation(sg[:, u, c0:c1], ps[:, 4 * u + q, 0:c1 - c0], ACT.Sigmoid,
                                           bias=self.cols[:, l, bass.ds(i * UN + (k_bias + u), 1)]).then_inc(gated, 1)

            @block.vector
            def _(ve):
                with ve.Fori(0, KD // UN) as i:
                    for u in range(UN):
                        ve.wait_ge(w_used, i * UN + u + 1)
                        ve.wait_ge(gated, i * (UN * npc) + npc * (u + 1))
                        ve.wait_ge(merged_up, i * (UN * PER) + (u + UN) * PER)
                        for q, (c0, c1) in enumerate(pieces):
                            g, p = sg[:, u, c0:c1].unsqueeze(1), ps[:, 4 * u + 2 + q, 0:c1 - c0].unsqueeze(1)
                            dst = merged[:, bass.ds(i * UN + u, 1), c0:c1]
                            if add:
                                ve.tensor_tensor(out=pr[:, u, c0:c1].unsqueeze(1), in0=p, in1=g, op=ALU.mult).then_inc(merged_up, 1)
                            else:
                                ve.tensor_tensor(out=dst, in0=p, in1=g, op=ALU.mult).then_inc(merged_up, 1)
                        if add:
                            ve.wait_ge(merged_up, i * (UN * PER) + (UN * PER + u * PER + npc))
                            for q, (c0, c1) in enumerate(pieces):
                                dst = merged[:, bass.ds(i * UN + u, 1), c0:c1]
                                ve.tensor_tensor(out=dst, in0=dst, in1=pr[:, u, c0:c1].unsqueeze(1), op=ALU.add).then_inc(merged_up, 1)

    def times(self, x, y, tiles, bcast=None):
        nc = self.nc
        ctx, sb, sem = self.scope()
        with ctx:
            done, row_in = sem("done"), sem("row_in")
            row = sb("row", [P, D]) if bcast is not None else None
            block = ctx.enter_context(nc.Block())
            if bcast is not None:
                @block.sync
                def _(sp):
                    sp.dma_start(row[:], bcast.broadcast_to((P, D))).then_inc(row_in, 16)

            @block.vector
            def _(ve):
                if bcast is not None:
                    ve.wait_ge(row_in, 16)
                for t in tiles:
                    ve.tensor_tensor(out=x[:, t, :], in0=x[:, t, :], in1=y[:, t, :] if bcast is None else row[:], op=ALU.mult).then_inc(done, 1)

    def spatial(self, l, zv, gu, tiles):
        nc, a, ps = self.nc, self.a, self.ps
        ctx, sb, sem = self.scope()
        with ctx:
            ws = sb("ws", [P, H, P])
            wsT = sb("wsT", [P, H, P])
            w_in, turned, copied, mixed, gated = (sem(n) for n in ("w_in", "turned", "copied", "mixed", "gated"))
            block = ctx.enter_context(nc.Block())
            pieces = [[t for t in tiles if t < CT], [t for t in tiles if t >= CT]]
            pieces = [p for p in pieces if p]

            @block.sync
            def _(sp):
                sp.dma_start(ws[:], a["sgu_w"][l].rearrange("g p q -> p g q")).then_inc(w_in, 16)

            @block.tensor
            def _(pe):
                pe.wait_ge(w_in, 16)
                for g in range(H):
                    mm = pe.transpose(ps[:, g // 4, (g % 4) * P:(g % 4 + 1) * P], ws[:, g, :], self.ident[:])
                mm.then_inc(turned, 1)
                pe.wait_ge(copied, 2)
                n = 0
                for g in range(H):
                    for p in pieces:
                        if n >= 6:
                            pe.wait_ge(gated, n - 5)
                        t0, t1 = p[0], p[-1] + 1
                        pe.matmul(ps[:, 2 + n % 6, 0:(t1 - t0) * P].rearrange("p (t c) -> p t c", c=P), wsT[:, g, :],
                                  zv[:, t0:t1, g * P:(g + 1) * P], start=True, stop=True).then_inc(mixed, 1)
                        n += 1

            @block.vector
            def _(ve):
                ve.wait_ge(turned, 1)
                for j in range(2):
                    ve.tensor_copy(wsT[:, 4 * j:4 * j + 4, :], ps[:, j, :].rearrange("p (g q) -> p g q", g=4)).then_inc(copied, 1)
                n = 0
                for g in range(H):
                    for p in pieces:
                        ve.wait_ge(mixed, n + 1)
                        t0, t1 = p[0], p[-1] + 1
                        dst = gu[:, t0:t1, g * P:(g + 1) * P]
                        ve.scalar_tensor_tensor(out=dst, in0=ps[:, 2 + n % 6, 0:(t1 - t0) * P].rearrange("p (t c) -> p t c", c=P),
                                                scalar=self.cols[:, l, K_SB + g:K_SB + g + 1], in1=dst, op0=ALU.add, op1=ALU.mult).then_inc(gated, 1)
                        n += 1

    def residual_norm(self, l, which, m_gate, y, tiles):
        nc, a, z = self.nc, self.a, self.z
        ctx, sb, sem = self.scope()
        with ctx:
            gate = sb("gate", [P, 2, D])
            lw = sb("lw", [P, D])
            lb = sb("lb", [P, D])
            stats = sb("stats", [P, 2, 2, 6])
            mv = sb("mv", [P, NT, 2])
            sd = sb("sd", [P, NT])
            rs = sb("rs", [P, NT])
            rows_in, gp_done, dve_done, rooted, scaled, z_ready = (
                sem(n) for n in ("rows_in", "gp_done", "dve_done", "rooted", "scaled", "z_ready"))
            block = ctx.enter_context(nc.Block())

            @block.sync
            def _(sp):
                for w in range(2):
                    sp.dma_start(gate[:, w, :], self.mod_dram[l, w:w + 1, m_gate * D:(m_gate + 1) * D].broadcast_to((P, D))).then_inc(rows_in, 16)
                sp.dma_start(lw[:], a["ln_w"][l, which:which + 1, :].broadcast_to((P, D))).then_inc(rows_in, 16)
                sp.dma_start(lb[:], a["ln_b"][l, which:which + 1, :].broadcast_to((P, D))).then_inc(rows_in, 16)

            @block.gpsimd
            def _(gp):
                gp.wait_ge(rows_in, 64)
                for n, t in enumerate(tiles):
                    gp.wait_ge(scaled, 2 * (n + 1))
                    gp.tensor_tensor(out=z[:, t, :], in0=z[:, t, :], in1=lw[:], op=ALU.mult).then_inc(z_ready, 1)
                    gp.wait_ge(z_ready, 2 * n + 1)
                    gp.tensor_tensor(out=z[:, t, :], in0=z[:, t, :], in1=lb[:], op=ALU.add).then_inc(z_ready, 1)

            @block.scalar
            def _(act):
                for n, t in enumerate(tiles):
                    act.wait_ge(dve_done, 5 * (n + 1))
                    act.activation(sd[:, t:t + 1], mv[:, t, 1:2], ACT.Sqrt, bias=self.eps[:, 0:1]).then_inc(rooted, 1)

            @block.vector
            def _(ve):
                ve.wait_ge(rows_in, 64)

                def scale(n):
                    t = tiles[n]
                    ve.wait_ge(rooted, n + 1)
                    ve.reciprocal(rs[:, t:t + 1], sd[:, t:t + 1]).then_inc(scaled, 1)
                    ve.wait_ge(scaled, 2 * n + 1)
                    ve.tensor_scalar(z[:, t, :], z[:, t, :], mv[:, t, 0:1], rs[:, t:t + 1], ALU.subtract, ALU.mult).then_inc(scaled, 1)

                for n, t in enumerate(tiles):
                    base = 5 * n
                    ve.tensor_tensor(out=y[:, t, :], in0=y[:, t, :], in1=gate[:, 1 if t < CT else 0, :], op=ALU.mult).then_inc(dve_done, 1)
                    ve.wait_ge(dve_done, base + 1)
                    ve.scalar_tensor_tensor(out=z[:, t, :], in0=z[:, t, :], scalar=ALPHA, in1=y[:, t, :], op0=ALU.mult, op1=ALU.add).then_inc(dve_done, 1)
                    ve.wait_ge(dve_done, base + 2)
                    for q in range(2):
                        ve.bn_stats(stats[:, n % 2, q, :], z[:, t, q * BANK:(q + 1) * BANK]).then_inc(dve_done, 1)
                    ve.wait_ge(dve_done, base + 4)
                    ve.bn_aggr(mv[:, t, :], stats[:, n % 2]).then_inc(dve_done, 1)
                    if n:
                        scale(n - 1)
                scale(len(tiles) - 1)

    def queries(self, l, hT, qT, kT, t0):
        nc, a, ps = self.nc, self.a, self.ps
        ctx, sb, sem = self.scope()
        UN = 4
        NG = 2 * H
        pieces = [(0, CTX), (CTX, T)] if t0 == 0 else [(CTX, T)]
        npc = len(pieces)
        with ctx:
            wt = sb("wt", [P, UN, KD, P])
            keys = sb("keys", [P, NG, P])
            w_in = [sem(f"w_in{u}") for u in range(UN)]
            k_in, k_turned, w_used, q_out = sem("k_in"), sem("k_turned"), sem("w_used"), sem("q_out")
            k_out = sem("k_out")
            block = ctx.enter_context(nc.Block())

            @block.sync
            def _(sp):
                sp.dma_start(keys[:], a["peer_keys"][l].rearrange("h t k d -> k (h t) d")).then_inc(k_in, 16)

                def load(n, u):
                    sp.dma_start(wt[:, u], wcols_dyn(a["peer_wq"][l], n * P, P)).then_inc(w_in[u], 16)
                for u in range(UN):
                    load(u, u)
                with sp.Fori(1, NG // UN) as i:
                    for u in range(UN):
                        sp.wait_ge(w_used, i * UN + (u + 1 - UN))
                        load(i * UN + u, u)

            @block.tensor
            def _(pe):
                pe.wait_ge(k_in, 16)
                for g in range(NG):
                    mm = pe.transpose(ps[:, g // 4, (g % 4) * P:(g % 4 + 1) * P], keys[:, g, :], self.ident[:])
                    if g % 4 == 3:
                        mm.then_inc(k_turned, 1)
                pe.wait_ge(k_out, 4)
                with pe.Fori(0, NG // UN) as i:
                    for u in range(UN):
                        pe.wait_ge(w_in[u], i * 16 + 16)
                        pe.wait_ge(q_out, i * (UN * npc) + npc * (u + 1))
                        for q, (c0, c1) in enumerate(pieces):
                            for k in range(KD):
                                mm = pe.matmul(ps[:, 2 * u + q, 0:c1 - c0], wt[:, u, k, :], hT[:, k, c0:c1], start=(k == 0), stop=(k == KD - 1))
                        mm.then_inc(w_used, 1)

            @block.scalar
            def _(act):
                for j in range(4):
                    act.wait_ge(k_turned, j + 1)
                    act.activation(kT[:, 4 * j:4 * j + 4, :], ps[:, j, :].rearrange("p (g q) -> p g q", g=4), ACT.Copy).then_inc(k_out, 1)
                act.wait_ge(k_out, 4)
                act.activation(keys[:, 0, :], kT[:, 0, :], ACT.Copy).then_inc(q_out, UN * npc)
                with act.Fori(0, NG // UN) as i:
                    for u in range(UN):
                        act.wait_ge(w_used, i * UN + u + 1)
                        for q, (c0, c1) in enumerate(pieces):
                            act.activation(qT[:, bass.ds(i * UN + u, 1), c0:c1], ps[:, 2 * u + q, 0:c1 - c0].unsqueeze(1), ACT.Copy).then_inc(q_out, 1)

    def modulate_rows(self, l, hx, tiles):
        nc, z = self.nc, self.z
        ctx, sb, sem = self.scope()
        with ctx:
            sh = sb("sh", [P, 2, D])
            sc = sb("sc", [P, 2, D])
            rows_in, done = sem("rows_in"), sem("done")
            block = ctx.enter_context(nc.Block())

            @block.sync
            def _(sp):
                for w in range(2):
                    sp.dma_start(sh[:, w, :], self.mod_dram[l, w:w + 1, 3 * D:4 * D].broadcast_to((P, D))).then_inc(rows_in, 16)
                    sp.dma_start(sc[:, w, :], self.mod_dram[l, w:w + 1, 4 * D:5 * D].broadcast_to((P, D))).then_inc(rows_in, 16)

            @block.vector
            def _(ve):
                ve.wait_ge(rows_in, 64)
                for n, t in enumerate(tiles):
                    w = 1 if t < CT else 0
                    ve.scalar_tensor_tensor(out=hx[:, t, :], in0=sc[:, w, :], scalar=1.0, in1=z[:, t, :], op0=ALU.add, op1=ALU.mult).then_inc(done, 1)
                    ve.wait_ge(done, 2 * n + 1)
                    ve.tensor_tensor(out=hx[:, t, :], in0=hx[:, t, :], in1=sh[:, w, :], op=ALU.add).then_inc(done, 1)

    def experts(self, l, t0, qT, kT, hx, y):
        nc, a, ps = self.nc, self.a, self.ps
        ctx, sb, sem = self.scope()
        NS = (NT - t0) * H
        AHEAD = 4
        RU, RV = 8, 4
        RD = 8
        N_STEPS = 38
        N_TO_EXP = 27
        tab_u, tab_v = (a[n].rearrange("l e d -> (l e) d") for n in ("expert_u", "expert_v"))
        with ctx:
            ur = sb("ur", [P, RU, D])
            vr = sb("vr", [P, RV, D])
            dots = sb("dots", [P, 2, TOPK])
            gl = sb("gl", [P, 2, TOPK])
            wt = sb("wt", [P, 2, TOPK])
            dg = sb("dg", [P, RD, P])
            icu = sb("icu", [P, 2, TOPK], U32)
            icv = sb("icv", [P, 2, TOPK], U32)
            idx = sb("idx", [P, (NS + 2) * TOPK], U32)
            gate = sb("gate", [P, NS * TOPK])
            qb = sb("qb", [P, 2, P])
            sc = sb("sc", [P, 2, P])
            sc2 = sb("sc2", [P, 2, P])
            s16 = sb("s16", [P, 2, TOPK])
            i16 = sb("i16", [P, 2, TOPK], U32)
            i16f = sb("i16f", [P, 2, TOPK])
            cand = sb("cand", [P, TOPK * TOPK])
            cand2 = sb("cand2", [P, TOPK * TOPK])
            sf = sb("sf", [P, TOPK])
            pf = sb("pf", [P, TOPK], U32)
            pij = sb("pij", [P, 2, TOPK], U32)
            pijf = sb("pijf", [P, 2, TOPK])
            hot = sb("hot", [P, 2, TOPK, TOPK])
            ids = sb("ids", [P, 2, TOPK])
            df = sb("df", [P, TOPK])
            idf = sb("idf", [P, TOPK])
            iota = sb("iota", [P, TOPK])
            sm = sb("sm", [P, 2])
            ex = sb("ex", [P, TOPK])
            mark = sb("mark", [P, 1])
            u_in = [sem(f"u_in{r}") for r in range(RU)]
            v_in = [sem(f"v_in{r}") for r in range(RV)]
            dot_done, icu_ready, icv_ready, gelu_done, w_ready, dg_ready, v_used, y_done = (
                sem(n) for n in ("dot_done", "icu_ready", "icv_ready", "gelu_done", "w_ready", "dg_ready", "v_used", "y_done"))
            set_up, q_ready, scored, picked, exped, step = (sem(n) for n in ("set_up", "q_ready", "scored", "picked", "exped", "step"))
            gathers = sem("gathers")
            block = ctx.enter_context(nc.Block())
            SEL = (NS - AHEAD) // 2

            def steps(eng, body):
                with eng.Fori(0, SEL) as i:
                    for u in range(2):
                        body(i * 2 + u, u, True)
                with eng.Fori(SEL, NS // 2) as i:
                    for u in range(2):
                        body(i * 2 + u, u, False)

            @block.gpsimd
            def _(gp):
                gp.iota(iota[:], pattern=[[1, TOPK]], base=0, channel_multiplier=0, allow_small_or_imprecise_dtypes=True).then_inc(set_up, 1)
                gp.memset(idx[:, NS * TOPK:(NS + 2) * TOPK], 0).then_inc(set_up, 1)
                gp.memset(icv[:], 0).then_inc(icv_ready, 1)
                gp.memset(wt[:], 0.0).then_inc(w_ready, 1)
                gp.memset(dg[:], 0.0).then_inc(v_used, TOPK)
                gp.wait_ge(icv_ready, 1)

                def rows_v(n, par, j):
                    gp.wait_ge(v_used, n * TOPK + (j + 1 + TOPK - RV))
                    gp.sem_inc(gathers, 1)
                    gp.indirect_dma_start(vr[:, j % RV, :], None, tab_v, bass.IndirectOffsetOnAxis(ap=icv[:, par, j:j + 1], axis=0)).then_inc(v_in[j % RV], 16)

                def body(n, u, _):
                    for j in range(TOPK):
                        if j == 0:
                            gp.wait_ge(icu_ready, n + 1)
                        gp.wait_ge(dot_done, n * TOPK + (j + 1))
                        gp.sem_inc(gathers, 1)
                        gp.indirect_dma_start(ur[:, j % RU, :], None, tab_u, bass.IndirectOffsetOnAxis(ap=icu[:, u, j:j + 1], axis=0)).then_inc(u_in[j % RU], 16)
                        if j == 0:
                            gp.wait_ge(icv_ready, n + 1)
                        rows_v(n, 1 - u, j)

                steps(gp, body)
                gp.wait_ge(icv_ready, NS + 1)
                for j in range(TOPK):
                    rows_v(NS, 1, j)

            @block.vector
            def _(ve):
                def stages(r):
                    n = 0

                    def put(ins):
                        nonlocal n
                        n += 1
                        ins.then_inc(step, 1)

                    def upto():
                        ve.wait_ge(step, r * N_STEPS + (n + 1))

                    def hold():
                        upto()
                        put(ve.memset(mark[:], 0.0))

                    def take_scores():
                        ve.wait_ge(scored, r + 1)
                        upto()
                        put(ve.tensor_copy(sc[:], ps[:, 4, 0:2 * P].rearrange("p (g k) -> p g k", g=2)))

                    def best_keys():
                        upto()
                        ve.memset(mark[:], 0.0).then_inc(picked, 1)
                        ve.wait_ge(picked, r + 2)
                        put(ve.memset(mark[:], 0.0))
                        for g in range(2):
                            put(ve.max(s16[:, g, 0:8], sc[:, g, :]))

                    def their_places():
                        hold()
                        for g in range(2):
                            put(ve.max_index(i16[:, g, 0:8], s16[:, g, 0:8], sc[:, g, :]))
                            put(ve.match_replace(sc2[:, g, :], s16[:, g, 0:8], sc[:, g, :], -3.0e38))

                    def next_keys():
                        hold()
                        for g in range(2):
                            put(ve.max(s16[:, g, 8:16], sc2[:, g, :]))

                    def next_places():
                        hold()
                        for g in range(2):
                            put(ve.max_index(i16[:, g, 8:16], s16[:, g, 8:16], sc2[:, g, :]))

                    def sums_of_halves():
                        upto()
                        put(ve.tensor_copy(i16f[:], i16[:]))
                        put(ve.tensor_tensor(out=cand[:].rearrange("p (i j) -> p i j", i=TOPK),
                                             in0=s16[:, 0, :].unsqueeze(2).broadcast_to((P, TOPK, TOPK)),
                                             in1=s16[:, 1, :].unsqueeze(1).broadcast_to((P, TOPK, TOPK)), op=ALU.add))

                    def best_pairs():
                        hold()
                        put(ve.max(sf[:, 0:8], cand[:]))

                    def their_positions():
                        hold()
                        put(ve.max_index(pf[:, 0:8], sf[:, 0:8], cand[:]))
                        put(ve.match_replace(cand2[:], sf[:, 0:8], cand[:], -3.0e38))

                    def next_pairs():
                        hold()
                        put(ve.max(sf[:, 8:16], cand2[:]))

                    def next_positions():
                        hold()
                        put(ve.max_index(pf[:, 8:16], sf[:, 8:16], cand2[:]))

                    def split_positions():
                        upto()
                        put(ve.tensor_tensor(out=df[:], in0=sf[:], in1=sf[:, 0:1].broadcast_to((P, TOPK)), op=ALU.subtract))
                        assert n == N_TO_EXP, n
                        put(ve.tensor_single_scalar(pij[:, 0, :], pf[:], 4, ALU.logical_shift_right))
                        put(ve.tensor_single_scalar(pij[:, 1, :], pf[:], TOPK - 1, ALU.bitwise_and))

                    def positions_as_floats():
                        upto()
                        put(ve.tensor_copy(pijf[:], pij[:]))

                    def one_hot():
                        upto()
                        put(ve.tensor_tensor(out=hot[:], in0=pijf[:].unsqueeze(3).broadcast_to((P, 2, TOPK, TOPK)),
                                             in1=iota[:].unsqueeze(1).unsqueeze(1).broadcast_to((P, 2, TOPK, TOPK)), op=ALU.is_equal))

                    def keys_there():
                        upto()
                        put(ve.tensor_tensor(out=hot[:], in0=hot[:], in1=i16f[:].unsqueeze(2).broadcast_to((P, 2, TOPK, TOPK)), op=ALU.mult))

                    def keys_summed():
                        upto()
                        put(ve.tensor_reduce(ids[:], hot[:], AX, ALU.add))

                    def expert_numbers():
                        upto()
                        put(ve.scalar_tensor_tensor(out=idf[:], in0=ids[:, 0, :], scalar=float(P), in1=ids[:, 1, :], op0=ALU.mult, op1=ALU.add))

                    def numbers_kept():
                        upto()
                        put(ve.tensor_scalar(idx[:, bass.ds(r * TOPK, TOPK)], idf[:], float(l * N_EXPERTS), None, ALU.add))

                    def softmax():
                        ve.wait_ge(exped, r + 1)
                        put(ve.tensor_reduce(sm[:, 0:1], ex[:], AX, ALU.add))
                        upto()
                        put(ve.reciprocal(sm[:, 1:2], sm[:, 0:1]))
                        upto()
                        put(ve.tensor_scalar(gate[:, bass.ds(r * TOPK, TOPK)], ex[:], sm[:, 1:2], None, ALU.mult))
                        assert n == N_STEPS, n

                    return [take_scores, best_keys, their_places, next_keys, next_places, sums_of_halves, best_pairs,
                            their_positions, next_pairs, next_positions, split_positions, positions_as_floats, one_hot,
                            keys_there, keys_summed, expert_numbers, numbers_kept], softmax

                ve.memset(mark[:], 0.0).then_inc(step, 1)
                ve.wait_ge(step, 1)
                ve.memset(mark[:], 0.0).then_inc(picked, 1)
                ve.wait_ge(picked, 1)
                ve.wait_ge(set_up, 2)
                with ve.Fori(0, AHEAD) as r:
                    work, last = stages(r)
                    for stage in work:
                        stage()
                    last()
                ve.wait_ge(step, AHEAD * N_STEPS + 1)
                for u in range(2):
                    ve.tensor_copy(icu[:, u, :], idx[:, u * TOPK:(u + 1) * TOPK]).then_inc(icu_ready, 1)
                ve.memset(y[:, 0:2], 0.0).then_inc(dot_done, RU)
                ve.memset(y[:, 2:NT + 1], 0.0).then_inc(y_done, 4)
                ve.wait_ge(dot_done, RU)

                def body(n, u, sel):
                    work, last = stages(n + AHEAD) if sel else ([], None)
                    for j in range(TOPK):
                        ve.wait_ge(u_in[j % RU], n * (16 * (TOPK // RU)) + 16 * (j // RU + 1))
                        if j == 0:
                            ve.wait_ge(gelu_done, n + 1)
                        ve.scalar_tensor_tensor(out=ur[:, j % RU, :].unsqueeze(1), in0=ur[:, j % RU, :].unsqueeze(1), scalar=1.0,
                                                in1=hx[:, bass.ds(n // H + t0, 1), :], op0=ALU.mult, op1=ALU.mult,
                                                accum_out=dots[:, u, j:j + 1]).then_inc(dot_done, 1)
                        for stage in work[j:j + 1] if j < TOPK - 1 else work[j:]:
                            stage()
                    ve.wait_ge(dot_done, n * TOPK + (RU + TOPK))
                    ve.wait_ge(v_used, n * TOPK + TOPK)
                    ve.tensor_copy(icv[:, u, :], idx[:, bass.ds(n * TOPK, TOPK)]).then_inc(icv_ready, 1)
                    if sel:
                        ve.wait_ge(step, n * N_STEPS + (3 * N_STEPS + 1))
                    else:
                        ve.wait_ge(step, NS * N_STEPS + 1)
                    ve.tensor_copy(icu[:, u, :], idx[:, bass.ds(n * TOPK + 2 * TOPK, TOPK)]).then_inc(icu_ready, 1)
                    if sel:
                        last()
                    ve.wait_ge(gelu_done, n + 3)
                    ve.tensor_tensor(out=wt[:, u, :], in0=gl[:, u, :], in1=gate[:, bass.ds(n * TOPK, TOPK)], op=ALU.mult).then_inc(w_ready, 1)
                    ve.wait_ge(v_used, n * TOPK + 2 * TOPK)
                    ve.wait_ge(y_done, n * 2 + 4)
                    for q in range(2):
                        dst = y[:, bass.ds((n + (H - 1)) // H + t0, 1), q * BANK:(q + 1) * BANK]
                        ve.tensor_tensor(out=dst, in0=ps[:, 2 * (1 - u) + q, :].unsqueeze(1), in1=dst, op=ALU.add).then_inc(y_done, 1)

                steps(ve, body)
                ve.wait_ge(v_used, (NS + 2) * TOPK)
                ve.wait_ge(y_done, 2 * NS + 4)
                for q in range(2):
                    dst = y[:, NT, q * BANK:(q + 1) * BANK]
                    ve.tensor_tensor(out=dst, in0=ps[:, 2 + q, :], in1=dst, op=ALU.add).then_inc(y_done, 1)

            @block.scalar
            def _(act):
                def query(r):
                    act.wait_ge(picked, r + 1)
                    act.activation(qb[:], qT[:, bass.ds((r % H) * 2, 2), bass.ds((r // H) * P + t0 * P, P)], ACT.Copy).then_inc(q_ready, 1)

                def exponentials(r):
                    act.wait_ge(step, r * N_STEPS + (N_TO_EXP + 1))
                    act.activation(ex[:], df[:], ACT.Exp).then_inc(exped, 1)

                with act.Fori(0, AHEAD) as r:
                    query(r)
                    exponentials(r)
                act.activation(gl[:, 0, :], self.ones[:, 0:TOPK], ACT.Copy).then_inc(gelu_done, 1)
                act.activation(gl[:, 1, :], self.ones[:, 0:TOPK], ACT.Copy).then_inc(gelu_done, 1)
                act.wait_ge(v_used, TOPK)
                act.wait_ge(gelu_done, 2)

                def diagonals(n, par):
                    act.wait_ge(w_ready, n + 1)
                    for j in range(TOPK):
                        act.wait_ge(v_used, n * TOPK + (j + 1 + TOPK - RD))
                        act.activation(dg[:, j % RD, :], self.ident[:], ACT.Copy, scale=wt[:, par, j:j + 1]).then_inc(dg_ready, 1)

                def body(n, u, sel):
                    if sel:
                        query(n + AHEAD)
                    diagonals(n, 1 - u)
                    if sel:
                        exponentials(n + AHEAD)
                    act.wait_ge(dot_done, n * TOPK + (RU + TOPK))
                    act.activation(gl[:, u, :], dots[:, u, :], ACT.Gelu_apprx_tanh).then_inc(gelu_done, 1)

                steps(act, body)
                diagonals(NS, 1)

            @block.tensor
            def _(pe):
                def scores(r):
                    pe.wait_ge(q_ready, r + 1)
                    pe.wait_ge(picked, r + 1)
                    for g in range(2):
                        mm = pe.matmul(ps[:, 4, g * P:(g + 1) * P], qb[:, g, :], kT[:, bass.ds((r % H) * 2 + g, 1), :], start=True, stop=True)
                    mm.then_inc(scored, 1)

                def head(n, par):
                    pe.wait_ge(y_done, n * 2 + 2)
                    for j in range(TOPK):
                        pe.wait_ge(dg_ready, n * TOPK + (j + 1))
                        pe.wait_ge(v_in[j % RV], n * (16 * (TOPK // RV)) + 16 * (j // RV + 1))
                        for q in range(2):
                            mm = pe.matmul(ps[:, 2 * par + q, :], dg[:, j % RD, :], vr[:, j % RV, q * BANK:(q + 1) * BANK],
                                           start=(j == 0), stop=(j == TOPK - 1))
                        mm.then_inc(v_used, 1)

                with pe.Fori(0, AHEAD) as r:
                    scores(r)

                def body(n, u, sel):
                    if sel:
                        scores(n + AHEAD)
                    head(n, 1 - u)

                steps(pe, body)
                head(NS, 1)

    def build(self):
        nc, a = self.nc, self.a
        ctx = ExitStack()
        with ctx:
            def sb(name, shape, dt=F32):
                return ctx.enter_context(nc.sbuf_tensor(name, shape, dt))

            self.ps = ctx.enter_context(nc.psum_tensor("ps", [P, 8, BANK], F32))
            self.mod_dram = nc.dram_tensor("mod_scratch", (DEPTH, 2, MODW), F32, kind="Internal").ap()
            self.z = sb("z", [P, NT, D])
            self.ident = sb("ident", [P, P])
            self.negident = sb("negident", [P, P])
            self.identb = sb("identb", [P, P], BF16)
            self.mask = sb("mask", [P, 2, 2 * P], BF16)
            self.ones = sb("ones", [P, P])
            self.eps = sb("eps", [P, 1])
            self.cols = sb("cols", [P, DEPTH, K_ALL])
            self.cond = sb("cond", [P, KD, 2])
            self.modc = sb("modc", [P, DEPTH, 2, 6, KD])
            self.setup()
            self.modulation()
            for l in range(DEPTH):
                self.layer(l)
            self.finish_out()

    def layer(self, l):
        nc, a = self.nc, self.a
        t0 = 0 if l < DEPTH - 1 else CT
        tiles = list(range(t0, NT))
        w_l = a["w_in"][l]
        mix, sb, _ = self.scope()
        with mix:
            hT = sb("hT", [P, KD, T])
            hs = sb("hs", [P, NT, D])
            self.modulated_turn(l, 0, hT, 0)
            inner, sb2, _ = self.scope()
            with inner:
                qk = sb2("qk", [P, 2 * KD, T])
                self.project_qk(l, hT, qk)
                v = sb2("v", [P, NT, H, E_H])
                tok = sb2("tok", [P, NT, 4, GR])
                alast = sb2("alast", [P, NT, GR])
                self.m_rows = sb2("m_rows", [GR, T])
                self.ones_column(v)

                def put_v(act, g, t, bank):
                    return act.activation(v[:, t, 4 * g:4 * g + 4, 0:P], bank.rearrange("p (h e) -> p h e", h=4), ACT.Copy)

                self.project_rows([w_l[:, C_V + g * BANK:C_V + (g + 1) * BANK] for g in range(2)], hT, list(range(NT)), put_v)
                self.gates(l, hT, tok, alast)
                self.mlstm(t0, qk, v, tok, alast, hs)
            merged = sb("merged", [P, KD, T])
            brT = sb("brT", [P, KD, T])
            other = sb("other", [P, NT, D])
            self.standardize(hs, tiles, H, P)

            def sig(act, g, t, bank):
                return act.activation(other[:, t, g * BANK:(g + 1) * BANK], bank, ACT.Sigmoid)

            self.project_rows([w_l[:, C_O + g * BANK:C_O + (g + 1) * BANK] for g in range(2)], hT, tiles, sig)
            self.times(hs, other, tiles)
            self.turn(hs, brT, tiles, self.cols[:, l, K_MN:K_MN + KD])
            self.merge_branch(l, a["p_a"][l], C_GA, K_BR, hT, brT, merged, t0, False)

            def gelu_pair(act, g, t, bank):
                dst = hs if g < 2 else other
                return act.activation(dst[:, t, (g % 2) * BANK:(g % 2 + 1) * BANK], bank, ACT.Gelu_apprx_tanh)

            self.project_rows([w_l[:, c0 + g * BANK:c0 + (g + 1) * BANK] for c0 in (C_VG, C_U) for g in range(2)], hT, tiles, gelu_pair)
            self.standardize(hs, tiles, 1, D)
            self.times(hs, None, tiles, a["sgu_norm_w"][l:l + 1, :])
            self.spatial(l, hs, other, tiles)
            self.turn(other, brT, tiles)
            self.merge_branch(l, a["p_b"][l], C_GB, K_BR + KD, hT, brT, merged, t0, True)

            def put_y(act, g, t, bank):
                return act.activation(hs[:, t, g * BANK:(g + 1) * BANK], bank, ACT.Copy)

            self.project_rows([a["w_out"][l][:, g * BANK:(g + 1) * BANK] for g in range(2)], merged, tiles, put_y)
            self.residual_norm(l, 0, 2, hs, tiles)
        peer, sb, _ = self.scope()
        with peer:
            qT = sb("qT", [P, 2 * H, T])
            kT = sb("kT", [P, 2 * H, P])
            inner, sb2, _ = self.scope()
            with inner:
                hT = sb2("hT", [P, KD, T])
                self.modulated_turn(l, 3, hT, t0)
                self.queries(l, hT, qT, kT, t0)
            hx = sb("hx", [P, NT, D])
            y = sb("y", [P, NT + 1, D])
            self.modulate_rows(l, hx, tiles)
            self.experts(l, t0, qT, kT, hx, y)
            self.residual_norm(l, 1, 5, y[:, 1:NT + 1, :], tiles)

    def ones_column(self, v):
        nc = self.nc
        ctx, sb, sem = self.scope()
        with ctx:
            done = sem("done")
            block = ctx.enter_context(nc.Block())

            @block.gpsimd
            def _(gp):
                gp.memset(v[:, :, :, P:E_H], 1.0).then_inc(done, 1)
                gp.memset(self.eps[:], EPS).then_inc(done, 1)

    def finish_out(self):
        nc = self.nc
        ctx, sb, sem = self.scope()
        with ctx:
            stored = sem("stored")
            block = ctx.enter_context(nc.Block())

            @block.sync
            def _(sp):
                sp.dma_start(self.out[0].rearrange("(t p) d -> p t d", p=P), self.z[:, CT:NT, :]).then_inc(stored, 16)
                sp.wait_ge(stored, 16)


def chunk_slice(c, d):
    if d == 0:
        return slice(c * P, (c + 1) * P)
    stop = c * P - 1
    return slice((c + 1) * P - 1, stop if stop >= 0 else None, -1)


def wcols_dyn(w, c0, n):
    return w[:, bass.ds(c0, n)].rearrange("(k p) n -> p k n", p=P)


_INS = ['x', 'c', 'ctx', 'c_ctx', 'w_mod', 'b_mod', 'w_in', 'qk_conv_w', 'qk_conv_b', 'gate_b', 'mlstm_norm_w',
        'sgu_norm_w', 'sgu_w', 'sgu_b', 'branch_b', 'p_a', 'p_b', 'w_out', 'ln_w', 'ln_b', 'peer_wq', 'peer_keys',
        'expert_u', 'expert_v']
_OUTS = [((1, SEQ, D), 'float32')]


def kernel(**inputs):
    import numpy as _np
    import concourse.bacc as _bacc
    from concourse import mybir as _mybir
    from concourse.bass_utils import run_bass_kernel_spmd as _run

    nc = _bacc.Bacc("TRN2", target_bir_lowering=False, num_devices=1)
    arrays, args = {}, {}
    for name in _INS:
        a = _np.ascontiguousarray(inputs[name])
        arrays[f"in_{name}_dram"] = a
        args[name] = nc.dram_tensor(f"in_{name}_dram", a.shape, _mybir.dt.from_np(a.dtype), kind="ExternalInput").ap()
    out = nc.dram_tensor("out_0_dram", _OUTS[0][0], _mybir.dt.from_np(_np.dtype(_OUTS[0][1])), kind="ExternalOutput").ap()
    Kernel(nc, args, out).build()
    r = _run(nc, [arrays], core_ids=[0])
    return r.results[0]["out_0_dram"]
```

```python
from contextlib import ExitStack

import concourse.bass as bass
from concourse import mybir

F32 = mybir.dt.float32
F32R = mybir.dt.float32r
BF16 = mybir.dt.bfloat16
U32 = mybir.dt.uint32
ALU = mybir.AluOpType
ACT = mybir.ActivationFunctionType
AX = mybir.AxisListType.X

P = 128
D = 1024
KD = D // P
DEPTH = 2
CTX, SEQ = 256, 512
T = CTX + SEQ
NT = T // P
CT = CTX // P
H = 8
GRID_W = 64
ROWS = SEQ // GRID_W
TAPS = 9
E_H = P + 1
BANK = 512
TOPK = 16
N_EXPERTS = P * P
NEG = -1e30
ALPHA = float((2 * DEPTH) ** 0.25)
EPS = 1e-5
QSCALE = float(P) ** -0.5
MODW = 6 * D
C_QK, C_V, C_O, C_G, C_U = 0, 2 * D, 3 * D, 4 * D, 4 * D + 32
C_VG, C_GA, C_GB = C_U + D, C_U + 2 * D, C_U + 3 * D
K_TAP, K_CB, K_BR, K_MN, K_SB, K_ALL = 0, 144, 160, 176, 184, 192
ORDER = [[0, 1, 2, 3, 4, 5], [1, 0, 5, 4, 3, 2]]
ROW0 = [0, 32]
GR = 40


def wcols(w, c0, n):
    return w[:, c0:c0 + n].rearrange("(k p) n -> p k n", p=P)


class Kernel:
    def __init__(self, nc, a, out):
        self.nc, self.a, self.out = nc, a, out
        self.count = 0

    def scope(self):
        ctx = ExitStack()
        self.count += 1
        tag = f"_{self.count}"

        def sb(name, shape, dt=F32):
            return ctx.enter_context(self.nc.sbuf_tensor(name + tag, shape, dt))

        sems = []

        def sem(name):
            sems.append(self.nc.alloc_semaphore(name + tag))
            return sems[-1]

        def clear():
            if sems:
                self.nc.clear_and_free_semaphores(sems)
                self.nc.all_engine_barrier()

        ctx.callback(clear)
        return ctx, sb, sem

    def setup(self):
        nc, a = self.nc, self.a
        ctx, sb, sem = self.scope()
        ident, identb, mask, cols, cond = self.ident, self.identb, self.mask, self.cols, self.cond
        with ctx:
            rows_a = sb("rows_a", [P, DEPTH, P])
            rows_b = sb("rows_b", [64, DEPTH, P])
            crow = sb("crow", [2 * KD, P])
            csil = sb("csil", [2 * KD, P])
            rows_in, c_in = sem("rows_in"), sem("c_in")
            zeroed, ident_ready, cond_silu = sem("zeroed"), sem("ident_ready"), sem("cond_silu")
            turned, copied, masks_ready = sem("turned"), sem("copied"), sem("masks_ready")
            block = ctx.enter_context(nc.Block())

            @block.sync
            def _(sp):
                sp.dma_start(crow[0:KD, :], a["c"].rearrange("a (k p) -> (a k) p", p=P)).then_inc(c_in, 16)
                sp.dma_start(crow[KD:2 * KD, :], a["c_ctx"].rearrange("(k p) -> k p", p=P)).then_inc(c_in, 16)
                for l in range(DEPTH):
                    taps = a["qk_conv_w"][l].rearrange("i j (c p) -> (i j c) p", p=P)
                    sp.dma_start(rows_a[:, l, :], taps[0:P]).then_inc(rows_in, 16)
                    sp.dma_start(rows_b[0:16, l, :], taps[P:144]).then_inc(rows_in, 16)
                    sp.dma_start(rows_b[16:32, l, :], a["qk_conv_b"][l].rearrange("(c p) -> c p", p=P)).then_inc(rows_in, 16)
                    sp.dma_start(rows_b[32:48, l, :], a["branch_b"][l].rearrange("(c p) -> c p", p=P)).then_inc(rows_in, 16)
                    sp.dma_start(rows_b[48:56, l, :], a["mlstm_norm_w"][l].rearrange("(c p) -> c p", p=P)).then_inc(rows_in, 16)
                    sp.dma_start(rows_b[56:64, l, :], a["sgu_b"][l]).then_inc(rows_in, 16)

            @block.gpsimd
            def _(gp):
                gp.memset(ident[:], 0.0).then_inc(zeroed, 1)
                gp.memset(mask[:], 0.0).then_inc(zeroed, 1)
                gp.memset(self.ones[:], 1.0).then_inc(zeroed, 1)
                gp.wait_ge(zeroed, 3)
                gp.affine_select(out=ident[:], in_=ident[:], compare_op=ALU.not_equal, fill=1.0, base=0,
                                 pattern=[[-1, P]], channel_multiplier=1).then_inc(ident_ready, 1)
                m0 = mask[:, 0, :].rearrange("p (b t) -> p b t", b=2)
                gp.affine_select(out=m0, in_=m0, compare_op=ALU.is_ge, fill=NEG, base=0,
                                 pattern=[[0, 2], [1, P]], channel_multiplier=-1).then_inc(masks_ready, 1)
                m1 = mask[:, 1, :].rearrange("p (b t) -> p b t", b=2)
                gp.affine_select(out=m1, in_=m1, compare_op=ALU.is_ge, fill=NEG, base=0,
                                 pattern=[[0, 2], [-1, P]], channel_multiplier=1).then_inc(masks_ready, 1)
                gp.wait_ge(ident_ready, 1)
                gp.tensor_scalar(self.negident[:], ident[:], -1.0, None, ALU.mult).then_inc(masks_ready, 1)

            @block.scalar
            def _(act):
                act.wait_ge(c_in, 32)
                act.activation(csil[:], crow[:], ACT.Silu).then_inc(cond_silu, 1)

            @block.tensor
            def _(pe):
                pe.wait_ge(ident_ready, 1)
                pe.wait_ge(cond_silu, 1)
                pe.transpose(self.ps[:, 0, 0:2 * KD], csil[:], ident[0:2 * KD, 0:2 * KD]).then_inc(turned, 1)
                pe.wait_ge(rows_in, 16 * 6 * DEPTH)
                for l in range(DEPTH):
                    pe.transpose(self.ps[:, 1 + l, 0:P], rows_a[:, l, :], ident[:])
                    pe.transpose(self.ps[:, 1 + l, P:P + 64], rows_b[:, l, :], ident[0:64, 0:64]).then_inc(turned, 1)

            @block.vector
            def _(ve):
                ve.wait_ge(ident_ready, 1)
                ve.tensor_copy(identb[:], ident[:]).then_inc(copied, 1)
                ve.wait_ge(turned, 1)
                ve.tensor_copy(cond[:], self.ps[:, 0, 0:2 * KD].rearrange("p (w k) -> p k w", w=2)).then_inc(copied, 1)
                ve.wait_ge(turned, 1 + DEPTH)
                for l in range(DEPTH):
                    ve.tensor_copy(cols[:, l, :], self.ps[:, 1 + l, 0:K_ALL]).then_inc(copied, 1)

    def modulation(self):
        nc, a, ps, cond = self.nc, self.a, self.ps, self.cond
        ctx, sb, sem = self.scope()
        W = BANK
        per_layer = MODW // W
        UN = 4
        ROUNDS = per_layer // UN
        with ctx:
            wt = sb("wt", [P, UN, KD, W])
            w_hi = sb("w_hi", [P, 2, KD, W], F32R)
            w_lo = sb("w_lo", [P, 2, KD, W], F32R)
            c_hi = sb("c_hi", [P, KD, 2], F32R)
            c_lo = sb("c_lo", [P, KD, 2], F32R)
            bias = sb("bias", [2, MODW])
            row = sb("row", [2, MODW])
            rows = sb("rows", [96, DEPTH, P])
            w_in = [sem(f"w_in{u}") for u in range(UN)]
            z_in = sem("z_in")
            b_in, w_used, row_ready, stored, back = sem("b_in"), sem("w_used"), sem("row_ready"), sem("stored"), sem("back")
            c_split, w_hi_ready, w_split, turned, cols_ready = (
                sem(n) for n in ("c_split", "w_hi_ready", "w_split", "turned", "cols_ready"))
            block = ctx.enter_context(nc.Block())

            @block.sync
            def _(sp):
                for l in range(DEPTH):
                    def load(g, u):
                        sp.dma_start(wt[:, u], wcols_dyn(a["w_mod"][l], g * W, W)).then_inc(w_in[u], 16)
                    for u in range(UN):
                        if l:
                            sp.wait_ge(w_split, per_layer * l - UN + u + 1)
                        load(u, u)
                    with sp.Fori(1, ROUNDS) as i:
                        for u in range(UN):
                            sp.wait_ge(w_split, i * UN + (per_layer * l - UN + u + 1))
                            load(i * UN + u, u)
                sp.dma_start(self.z[:, 0:CT, :], a["ctx"][0].rearrange("(t p) d -> p t d", p=P)).then_inc(z_in, 16)
                sp.dma_start(self.z[:, CT:NT, :], a["x"][0].rearrange("(t p) d -> p t d", p=P)).then_inc(z_in, 16)
                sp.wait_ge(z_in, 32)

            @block.scalar
            def _(act):
                with act.Fori(0, DEPTH * ROUNDS) as i:
                    for u in range(UN):
                        act.wait_ge(w_in[u], i * 16 + 16)
                        act.wait_ge(w_used, i * UN + (u + 1))
                        act.activation(w_hi[:, u % 2], wt[:, u], ACT.Copy).then_inc(w_hi_ready, 1)

            @block.tensor
            def _(pe):
                pe.wait_ge(c_split, 2)
                with pe.Fori(0, DEPTH * ROUNDS) as i:
                    for u in range(UN):
                        pe.wait_ge(w_split, i * UN + (u + 1))
                        pe.wait_ge(row_ready, i * UN + (u + 1))
                        mm = split_product(pe, ps[0:2, u, :], c_hi, c_lo, w_hi[:, u % 2], w_lo[:, u % 2])
                        mm.then_inc(w_used, 1)
                pe.wait_ge(back, 32 * DEPTH)
                for l in range(DEPTH):
                    pe.transpose(ps[:, 4 + l, 0:96], rows[:, l, :], self.ident[0:96, 0:96]).then_inc(turned, 1)

            @block.gpsimd
            def _(gp):
                gp.memset(row[:], 0.0).then_inc(row_ready, UN)
                gp.memset(rows[:], 0.0).then_inc(w_used, 2)
                gp.wait_ge(w_used, 2)
                for l in range(DEPTH):
                    if l:
                        gp.wait_ge(stored, 16 * l)
                        gp.wait_ge(row_ready, per_layer * l + UN)
                    gp.dma_start(bias[:], a["b_mod"][l:l + 1, :].broadcast_to((2, MODW))).then_inc(b_in, 16)
                    gp.wait_ge(row_ready, per_layer * (l + 1) + UN)
                    gp.dma_start(self.mod_dram[l], row[:]).then_inc(stored, 16)
                    gp.wait_ge(stored, 16 * (l + 1))
                    for w in range(2):
                        gp.dma_start(rows[48 * w:48 * w + 48, l, :],
                                     self.mod_dram[l, w].rearrange("(r p) -> r p", p=P)).then_inc(back, 16)

            @block.vector
            def _(ve):
                ve.tensor_copy(c_hi[:], cond[:]).then_inc(c_split, 1)
                ve.wait_ge(c_split, 1)
                ve.tensor_tensor(out=c_lo[:], in0=cond[:], in1=c_hi[:].bitcast(F32), op=ALU.subtract).then_inc(c_split, 1)
                ve.wait_ge(row_ready, UN)

                def split(l, i, u):
                    ve.wait_ge(w_hi_ready, i * UN + (per_layer * l + u + 1))
                    ve.tensor_tensor(out=w_lo[:, u % 2], in0=wt[:, u], in1=w_hi[:, u % 2].bitcast(F32), op=ALU.subtract).then_inc(w_split, 1)

                def add(l, i, u):
                    ve.wait_ge(w_used, i * UN + (per_layer * l + u + 3))
                    at = bass.ds(i * (UN * W) + u * W, W)
                    ve.tensor_tensor(out=row[:, at], in0=ps[0:2, u % UN, :], in1=bias[:, at], op=ALU.add).then_inc(row_ready, 1)

                for l in range(DEPTH):
                    for u in range(UN):
                        split(l, 0, u)
                        if u == 2:
                            ve.wait_ge(b_in, 16 * (l + 1))
                        if u >= 2:
                            add(l, 0, u - 2)
                    with ve.Fori(1, ROUNDS) as i:
                        for u in range(UN):
                            split(l, i, u)
                            add(l, i, u - 2)
                    add(l, ROUNDS, -2)
                    add(l, ROUNDS, -1)
                for l in range(DEPTH):
                    ve.wait_ge(turned, l + 1)
                    mc = self.modc[:, l]
                    ve.tensor_copy(mc, ps[:, 4 + l, 0:96].rearrange("p (w m k) -> p w m k", w=2, m=6)).then_inc(cols_ready, 1)
                    ve.wait_ge(cols_ready, 3 * l + 1)
                    for m in (1, 4):
                        ve.tensor_scalar(mc[:, :, m, :], mc[:, :, m, :], 1.0, None, ALU.add).then_inc(cols_ready, 1)

    def modulated_turn(self, l, m_shift, hT, hi, lo, t0):
        nc, ps = self.nc, self.ps
        ctx, sb, sem = self.scope()
        with ctx:
            turned, act_out, dve_out = sem("turned"), sem("act_out"), sem("dve_out")
            hi_ready, lo_ready = sem("hi_ready"), sem("lo_ready")
            block = ctx.enter_context(nc.Block())
            tiles = list(range(t0, NT))

            def col(t, m, k):
                return self.modc[:, l, 1 if t < CT else 0, m, k:k + 1]

            @block.tensor
            def _(pe):
                for n, t in enumerate(tiles):
                    if n >= 4:
                        pe.wait_ge(act_out, 4 * (n - 3))
                        pe.wait_ge(dve_out, 4 * (n - 3))
                    for k in range(KD):
                        mm = pe.transpose(ps[:, 2 * (n % 4) + k // 4, (k % 4) * P:(k % 4) * P + P],
                                          self.z[:, t, k * P:(k + 1) * P], self.ident[:])
                    mm.then_inc(turned, 1)

            @block.scalar
            def _(act):
                for n, t in enumerate(tiles):
                    act.wait_ge(turned, n + 1)
                    for k in range(4):
                        act.activation(hT[:, k, t * P:(t + 1) * P], ps[:, 2 * (n % 4), k * P:(k + 1) * P], ACT.Identity,
                                       bias=col(t, m_shift, k), scale=col(t, m_shift + 1, k)).then_inc(act_out, 1)
                    act.wait_ge(act_out, 4 * (n + 1))
                    act.wait_ge(dve_out, 4 * (n + 1))
                    ts = slice(t * P, (t + 1) * P)
                    act.activation(hi[:, :, ts], hT[:, :, ts], ACT.Copy).then_inc(hi_ready, 1)

            @block.gpsimd
            def _(gp):
                for n, t in enumerate(tiles):
                    gp.wait_ge(hi_ready, n + 1)
                    ts = slice(t * P, (t + 1) * P)
                    gp.tensor_tensor(out=lo[:, :, ts], in0=hT[:, :, ts], in1=hi[:, :, ts].bitcast(F32), op=ALU.subtract).then_inc(lo_ready, 1)

            @block.vector
            def _(ve):
                for n, t in enumerate(tiles):
                    ve.wait_ge(turned, n + 1)
                    for k in range(4):
                        ve.tensor_scalar(hT[:, 4 + k, t * P:(t + 1) * P], ps[:, 2 * (n % 4) + 1, k * P:(k + 1) * P],
                                         col(t, m_shift + 1, 4 + k), col(t, m_shift, 4 + k), ALU.mult, ALU.add).then_inc(dve_out, 1)

    def project_qk(self, l, hi, lo, qk, t0):
        nc, a, ps, cols = self.nc, self.a, self.ps, self.cols
        ctx, sb, sem = self.scope()
        UN = 4
        NC = 2 * D // P
        RH, RW = ROWS + 2, GRID_W + 2
        w_l = a["w_in"][l]
        with ctx:
            wt = sb("wt", [P, UN, KD, P])
            w_hi = sb("w_hi", [P, 2, KD, P], F32R)
            w_lo = sb("w_lo", [P, 2, KD, P], F32R)
            w_hi_ready, w_split, seen = sem("w_hi_ready"), sem("w_split"), sem("seen")
            raw_x = sb("raw_x", [P, 4, RH, RW])
            raw_c = sb("raw_c", [P, 4, CTX + 2])
            acc = sb("acc", [P, 4, T])
            spare = sb("spare", [P, 1])
            w_in = [sem(f"w_in{u}") for u in range(UN)]
            w_used, raw_ready, zeroed, conv_step, silu_done = sem("w_used"), sem("raw_ready"), sem("zeroed"), sem("conv_step"), sem("silu_done")
            HALF = NC // 2
            S0 = TAPS + (3 if t0 == 0 else 0)
            PARTS = [(0, t0 == 0, S0, 0), (HALF, True, TAPS + 3, HALF * S0)]
            block = ctx.enter_context(nc.Block())

            @block.sync
            def _(sp):
                def load(n, u):
                    sp.dma_start(wt[:, u], wcols_dyn(w_l, n * P, P)).then_inc(w_in[u], 16)
                for u in range(UN):
                    load(u, u)
                with sp.Fori(1, NC // UN) as i:
                    for u in range(UN):
                        sp.wait_ge(w_split, i * UN + (u + 1 - UN))
                        load(i * UN + u, u)

            @block.tensor
            def _(pe):
                for first, ctx_in, _, _ in PARTS:
                    with pe.Fori(0, HALF // UN) as i:
                        for u in range(UN):
                            b = 2 * (u % 4)
                            pe.wait_ge(w_split, i * UN + (first + u + 1))
                            pe.wait_ge(raw_ready, i * 8 + 2 * (first + u) + 2)
                            mm = split_product(pe, ps[:, b, :], w_hi[:, u % 2], w_lo[:, u % 2], hi[:, :, CTX:T], lo[:, :, CTX:T])
                            if ctx_in:
                                mm = split_product(pe, ps[:, b + 1, 0:CTX], w_hi[:, u % 2], w_lo[:, u % 2], hi[:, :, 0:CTX], lo[:, :, 0:CTX])
                            mm.then_inc(w_used, 1)

            @block.gpsimd
            def _(gp):
                gp.memset(raw_x[:], 0.0).then_inc(raw_ready, 4)
                gp.memset(raw_c[:], 0.0).then_inc(raw_ready, 4)
                gp.memset(spare[:], 0.0).then_inc(w_used, 2)
                with gp.Fori(0, NC // UN) as i:
                    for u in range(UN):
                        gp.wait_ge(w_in[u], i * 16 + 16)
                        gp.wait_ge(w_used, i * UN + (u + 1))
                        gp.sem_inc(seen, 1)
                        gp.tensor_copy(w_hi[:, u % 2], wt[:, u]).then_inc(w_hi_ready, 1)
                        gp.wait_ge(w_hi_ready, i * UN + (u + 1))
                        gp.tensor_tensor(out=w_lo[:, u % 2], in0=wt[:, u], in1=w_hi[:, u % 2].bitcast(F32), op=ALU.subtract).then_inc(w_split, 1)

            @block.scalar
            def _(act):
                act.wait_ge(raw_ready, 8)
                for n in range(NC + 2):
                    if n < NC:
                        s, ctx_in = n % 4, PARTS[n // HALF][1]
                        act.wait_ge(w_used, n + 3)
                        act.activation(raw_x[:, s, 1:1 + ROWS, 1:1 + GRID_W],
                                       ps[:, 2 * s, :].rearrange("p (r w) -> p r w", r=ROWS), ACT.Copy).then_inc(raw_ready, 1 if ctx_in else 2)
                        if ctx_in:
                            act.activation(raw_c[:, s, 1:1 + CTX], ps[:, 2 * s + 1, 0:CTX], ACT.Copy).then_inc(raw_ready, 1)
                    m = n - 2
                    if m >= 0:
                        first, ctx_in, steps, before = PARTS[m // HALF]
                        c0 = 0 if ctx_in else CTX
                        act.wait_ge(conv_step, before + steps * 2 * ((m - first) // 2 + 1))
                        act.activation(qk[:, m, c0:T], acc[:, m % 4, c0:T], ACT.Silu).then_inc(silu_done, 1)

            @block.vector
            def _(ve):
                for first, ctx_in, steps, before in PARTS:
                    work = []
                    for j in range(TAPS):
                        work += [(j, False, w) for w in range(2)]
                        if j < 3 and ctx_in:
                            work += [(j, True, w) for w in range(2)]
                    place = {x: n for n, x in enumerate(work)}
                    with ve.Fori(0, HALF // UN) as i:
                        for pair in range(UN // 2):
                            ve.wait_ge(raw_ready, i * (2 * UN) + (8 + 2 * (first + 2 * pair + 2)))
                            for j, context, w in work:
                                s = 2 * pair + w

                                def col(c):
                                    return cols[:, l, bass.ds(i * UN + (c + first + s), 1)]
                                if context:
                                    src, dst, tap = raw_c[:, s, j:j + CTX], acc[:, s, 0:CTX], col(K_TAP + 16 * (3 + j))
                                else:
                                    src = raw_x[:, s, j // 3:j // 3 + ROWS, j % 3:j % 3 + GRID_W]
                                    dst, tap = acc[:, s, CTX:T].rearrange("p (r w) -> p r w", r=ROWS), col(K_TAP + 16 * j)
                                if j:
                                    ve.wait_ge(conv_step, i * (UN * steps) + (before + 2 * steps * pair + place[(j - 1, context, w)] + 1))
                                    ve.scalar_tensor_tensor(out=dst, in0=src, scalar=tap, in1=dst, op0=ALU.mult, op1=ALU.add).then_inc(conv_step, 1)
                                else:
                                    ve.tensor_scalar(dst, src, tap, col(K_CB), ALU.mult, ALU.add).then_inc(conv_step, 1)

    def values_and_gates(self, l, hT, v, tok, alast, spare):
        nc, a, ps, ident = self.nc, self.a, self.ps, self.ident
        ctx, sb, sem = self.scope()
        w_l = a["w_in"][l]
        M = self.m_rows
        with ctx:
            wg = sb("wg", [P, KD, 2, GR])
            gb = sb("gb", [GR, 2])
            gi, gf, t1, t2, b_, c_ = (spare[0:GR, n, 0:T] for n in range(6))
            wt = sb("wt", [P, 2, KD, BANK])
            v_in = [sem(f"v_in{s}") for s in range(2)]
            mm_done, v_put, ones_put = sem("mm_done"), sem("v_put"), sem("ones_put")
            V = 2 * NT
            one = sb("one", [GR, P])
            mprev = sb("mprev", [GR, NT])
            nlast = sb("nlast", [GR, NT])
            al = sb("al", [GR, NT])
            ald = sb("ald", [GR, NT, GR])
            av, ev, wv = (sb(n, [GR, T]) for n in ("av", "ev", "wv"))
            zeroed, w_in, g_mm, act_done, dve_done, turned, out_done = (
                sem(n) for n in ("zeroed", "w_in", "g_mm", "act_done", "dve_done", "turned", "out_done"))
            N_ABS = 5
            N_LF = N_ABS + 1
            N_M = N_LF + 2 * NT + 1 + (6 * NT - 2) + NT
            N_DVE = N_M + NT
            block = ctx.enter_context(nc.Block())

            @block.gpsimd
            def _(gp):
                gp.memset(wg[:], 0.0).then_inc(zeroed, 1)
                gp.memset(gb[:], 0.0).then_inc(zeroed, 1)
                gp.memset(one[:], 1.0).then_inc(zeroed, 1)
                for x in (mprev, nlast, al, b_, M):
                    gp.memset(x[:], 0.0).then_inc(zeroed, 1)
                gp.memset(v[:, :, :, P:E_H], 1.0).then_inc(ones_put, 1)
                gp.memset(self.eps[:], EPS).then_inc(ones_put, 1)
                gp.wait_ge(zeroed, 8)
                gp.wait_ge(ones_put, 2)
                for d in range(2):
                    c = ORDER[d][0]
                    gp.memset(mprev[ROW0[d]:ROW0[d] + H, c:c + 1], NEG).then_inc(zeroed, 1)

            @block.sync
            def _(sp):
                sp.wait_ge(zeroed, 2)
                for d in range(2):
                    for kind in range(2):
                        c0 = C_G + 16 * d + 8 * kind
                        sp.dma_start(wg[:, :, kind, ROW0[d]:ROW0[d] + H],
                                     w_l[:, c0:c0 + H].rearrange("(k p) n -> p k n", p=P)).then_inc(w_in, 16)
                        g0 = 16 * d + 8 * kind
                        sp.dma_start(gb[ROW0[d]:ROW0[d] + H, kind:kind + 1],
                                     a["gate_b"][l, g0:g0 + H].rearrange("(n o) -> n o", o=1)).then_inc(w_in, 16)
                self.load_groups(sp, [w_l[:, C_V + g * BANK:C_V + (g + 1) * BANK] for g in range(2)], wt, v_in, mm_done, NT)

            @block.tensor
            def _(pe):
                pe.wait_ge(w_in, 16 * 8)
                for kind in range(2):
                    for k in range(KD):
                        pe.matmul(ps[0:GR, 2 * kind, 0:BANK], wg[:, k, kind, :], hT[:, k, 0:BANK], start=(k == 0), stop=(k == KD - 1))
                    for k in range(KD):
                        mm = pe.matmul(ps[0:GR, 2 * kind + 1, 0:T - BANK], wg[:, k, kind, :], hT[:, k, BANK:T], start=(k == 0), stop=(k == KD - 1))
                    mm.then_inc(g_mm, 1)
                for n in range(V):
                    g, t = n // NT, n % NT
                    if t == 0:
                        pe.wait_ge(v_in[g], 32)
                    if n == 4:
                        pe.wait_ge(dve_done, 4)
                    if n >= 8:
                        pe.wait_ge(v_put, n - 7)
                    for k in range(KD):
                        mm = pe.matmul(ps[:, (n + 4) % 8, :], hT[:, k, t * P:(t + 1) * P], wt[:, g, k, :], start=(k == 0), stop=(k == KD - 1))
                    mm.then_inc(mm_done, 1)
                pe.wait_ge(v_put, V)
                pe.wait_ge(act_done, 2 + 1 + 3 * NT)
                for c in range(NT):
                    for n, x in enumerate((av, ev, wv, c_)):
                        mm = pe.transpose(ps[:, c, n * GR:(n + 1) * GR], x[:, c * P:(c + 1) * P], ident[0:GR, 0:GR])
                    mm.then_inc(turned, 1)
                pe.wait_ge(dve_done, N_DVE)
                pe.matmul(ps[:, 6, 0:NT * GR], self.ones[0:GR, :], ald[:].rearrange("p c r -> p (c r)"), start=True, stop=True).then_inc(turned, 1)

            @block.scalar
            def _(act):
                act.wait_ge(dve_done, N_ABS)
                act.activation(t1[:], t1[:], ACT.Exp, scale=-1.0).then_inc(act_done, 1)
                act.wait_ge(act_done, 1)
                act.activation(t2[:], t1[:], ACT.Ln, bias=1.0).then_inc(act_done, 1)
                for n in range(V):
                    g, t = n // NT, n % NT
                    act.wait_ge(mm_done, n + 1)
                    act.activation(v[:, t, 4 * g:4 * g + 4, 0:P], ps[:, (n + 4) % 8, :].rearrange("p (h e) -> p h e", h=4), ACT.Copy).then_inc(v_put, 1)
                act.wait_ge(dve_done, N_M)
                act.activation(ev[:], t1[:], ACT.Exp, scale=-1.0).then_inc(act_done, 1)
                for c in range(NT):
                    cs = slice(c * P, (c + 1) * P)
                    act.activation(av[:, cs], M[:, cs], ACT.Exp, bias=mprev[:, c:c + 1], scale=-1.0).then_inc(act_done, 1)
                    act.activation(wv[:, cs], c_[:, cs], ACT.Exp, bias=nlast[:, c:c + 1]).then_inc(act_done, 1)
                    act.activation(al[:, c:c + 1], nlast[:, c:c + 1], ACT.Exp, bias=mprev[:, c:c + 1]).then_inc(act_done, 1)

            @block.vector
            def _(ve):
                n = 0

                def after(ins):
                    nonlocal n
                    n += 1
                    ins.then_inc(dve_done, 1)
                    ve.wait_ge(dve_done, n)

                def take(ins):
                    nonlocal n
                    n += 1
                    ins.then_inc(dve_done, 1)

                ve.wait_ge(zeroed, 10)
                ve.wait_ge(g_mm, 2)
                i2 = gi
                take(ve.tensor_scalar(i2[:, 0:BANK], ps[0:GR, 0, :], gb[:, 0:1], None, ALU.add))
                take(ve.tensor_scalar(i2[:, BANK:T], ps[0:GR, 1, 0:T - BANK], gb[:, 0:1], None, ALU.add))
                take(ve.tensor_scalar(gf[:, 0:BANK], ps[0:GR, 2, :], gb[:, 1:2], None, ALU.add))
                after(ve.tensor_scalar(gf[:, BANK:T], ps[0:GR, 3, 0:T - BANK], gb[:, 1:2], None, ALU.add))
                after(ve.scalar_tensor_tensor(out=t1[:], in0=gf[:], scalar=-1.0, in1=gf[:], op0=ALU.mult, op1=ALU.max))
                assert n == N_ABS
                ve.wait_ge(act_done, 2)
                after(ve.scalar_tensor_tensor(out=gf[:], in0=gf[:], scalar=0.0, in1=t2[:], op0=ALU.min, op1=ALU.subtract))
                for d in range(2):
                    r = slice(ROW0[d], ROW0[d] + H)
                    for c in range(NT):
                        cs = chunk_slice(c, d)
                        take(ve.tensor_tensor_scan(b_[r, cs], one[r, :], gf[r, cs], 0.0, ALU.mult, ALU.add))
                ve.wait_ge(dve_done, n)
                after(ve.tensor_tensor(out=c_[:], in0=gi[:], in1=b_[:], op=ALU.subtract))
                for pos in range(NT):
                    for d in range(2):
                        c = ORDER[d][pos]
                        r = slice(ROW0[d], ROW0[d] + H)
                        last = c * P + (P - 1 if d == 0 else 0)
                        cs = chunk_slice(c, d)
                        after(ve.tensor_tensor_scan(M[r, cs], c_[r, cs], c_[r, cs], mprev[r, c:c + 1], ALU.max, ALU.max))
                        take(ve.tensor_scalar(nlast[r, c:c + 1], M[r, last:last + 1], -1.0, None, ALU.mult))
                        if pos < NT - 1:
                            nx = ORDER[d][pos + 1]
                            take(ve.tensor_tensor(out=mprev[r, nx:nx + 1], in0=M[r, last:last + 1], in1=b_[r, last:last + 1], op=ALU.add))
                        ve.wait_ge(dve_done, n)
                for c in range(NT):
                    cs = slice(c * P, (c + 1) * P)
                    take(ve.tensor_tensor(out=t1[:, cs], in0=M[:, cs], in1=b_[:, cs], op=ALU.add))
                ve.wait_ge(act_done, 3 + 3 * NT)
                for c in range(NT):
                    take(ve.tensor_scalar(ald[:, c, :], ident[0:GR, 0:GR], al[:, c:c + 1], None, ALU.mult))
                assert n == N_DVE, (n, N_DVE)
                for c in range(NT):
                    ve.wait_ge(turned, c + 1)
                    ve.tensor_copy(tok[:, c], ps[:, c, 0:4 * GR].rearrange("p (n r) -> p n r", n=4)).then_inc(out_done, 1)
                ve.wait_ge(turned, NT + 1)
                ve.tensor_copy(alast[:], ps[:, 6, 0:NT * GR].rearrange("p (c r) -> p c r", c=NT)).then_inc(out_done, 1)
                ve.wait_ge(out_done, NT)
                ve.tensor_scalar(tok[:, :, 0, :], tok[:, :, 0, :], QSCALE, None, ALU.mult).then_inc(out_done, 1)

    def mlstm(self, t0, qk, v, tok, alast, hsum):
        nc, ps = self.nc, self.ps
        ctx, sb, sem = self.scope()
        M = self.m_rows
        steps = [(d, ORDER[d][pos], ORDER[d][pos] >= t0, pos < NT - 1) for pos in range(NT) for d in range(2)]
        NP_ = H // 2
        hu = []
        uu = []
        for s, (d, c, has_h, has_u) in enumerate(steps):
            for p in range(NP_):
                if has_h:
                    hu.append((s, p))
                if has_u:
                    uu.append((s, p))
        h_at = {x: n for n, x in enumerate(hu)}
        u_at = {x: n for n, x in enumerate(uu)}
        slots = [(s, p) for s in range(len(steps)) for p in range(NP_)]
        h_steps = [s for s in range(len(steps)) if steps[s][2]]
        u_steps = [s for s in range(len(steps)) if steps[s][3]]
        seen = set()
        first_visit = {}
        for s in h_steps:
            first_visit[s] = steps[s][1] not in seen
            seen.add(steps[s][1])
        fin_len = {s: 4 if first_visit[s] else 5 for s in h_steps}
        fin_upto = {}
        total = 0
        for s in h_steps:
            total += fin_len[s]
            fin_upto[s] = total

        def ct_needed(s, p):
            d = steps[s][0]
            before = [x for x in u_steps if x < s and steps[x][0] == d]
            return u_at[(before[-1], p)] + 1 if before else 0

        def after_unit(slot, units_at):
            return units_at.get(slot)

        with ctx:
            state = sb("state", [P, 2, H, E_H])
            ktok = sb("ktok", [P, 2, D])
            vw = sb("vw", [P, 2, H, E_H])
            ex = sb("ex", [P, 2, 2, P])
            pt = sb("pt", [P, 2, 2, P])
            iv = sb("iv", [P, 2, 2, E_H])
            num = sb("num", [P, 2, H, E_H])
            den = sb("den", [P, 3, H])
            hb = sb("hb", [P, H, P])
            zeroed, sb_done, exp_done, p_ready, ii_done, iv_ready, num_ready, upd_done, ct_ready = (
                sem(n) for n in ("zeroed", "sb_done", "exp_done", "p_ready", "ii_done", "iv_ready", "num_ready", "upd_done", "ct_ready"))
            ktr_done, ktok_ready, vw_ready, fin = sem("ktr_done"), sem("ktok_ready"), sem("vw_ready"), sem("fin")
            block = ctx.enter_context(nc.Block())

            @block.gpsimd
            def _(gp):
                for d in range(2):
                    gp.memset(state[:, d], 0.0).then_inc(zeroed, 1)
                for n, s in enumerate(u_steps):
                    d, c = steps[s][:2]
                    if n >= 2:
                        gp.wait_ge(upd_done, NP_ * (n - 1))
                    wl = tok[:, c, 2, ROW0[d]:ROW0[d] + H]
                    gp.tensor_tensor(out=vw[:, n % 2], in0=v[:, c], in1=wl.unsqueeze(2).broadcast_to((P, H, E_H)), op=ALU.mult).then_inc(vw_ready, 1)

            @block.tensor
            def _(pe):
                pe.wait_ge(zeroed, 2)

                def scores(s, p):
                    n = h_at[(s, p)]
                    d, c = steps[s][:2]
                    cs = slice(c * P, (c + 1) * P)
                    if n >= 2:
                        pe.wait_ge(p_ready, n - 1)
                    for j in range(2):
                        h = 2 * p + j
                        pe.matmul(ps[:, n % 2, j * P:(j + 1) * P], qk[:, H + h, cs], qk[:, h, cs], start=True, stop=True)
                    pe.matmul(ps[:, n % 2, 2 * P:4 * P], self.identb[:], self.mask[:, d, :], start=True, stop=False, skip_group_check=True)
                    for j in range(2):
                        r = ROW0[d] + 2 * p + j
                        mm = pe.matmul(ps[:, n % 2, (2 + j) * P:(3 + j) * P], self.negident[0:GR, r:r + 1].broadcast_to((GR, P)),
                                       M[:, cs], start=False, stop=True, skip_group_check=True)
                    mm.then_inc(sb_done, 1)

                def outputs(s, p):
                    n = h_at[(s, p)]
                    d, c = steps[s][:2]
                    cs = slice(c * P, (c + 1) * P)
                    if n >= 2:
                        pe.wait_ge(num_ready, n - 1)
                    need = ct_needed(s, p)
                    if need:
                        pe.wait_ge(ct_ready, 2 * need)
                    for j in range(2):
                        h = 2 * p + j
                        pe.matmul(ps[:, 4 + n % 2, j * E_H:(j + 1) * E_H], qk[:, h, cs], state[:, d, h, :], start=True, stop=True)
                    pe.wait_ge(p_ready, n + 1)
                    for j in range(2):
                        mm = pe.matmul(ps[:, 2 + n % 2, j * E_H:(j + 1) * E_H], pt[:, n % 2, j, :], v[:, c, 2 * p + j, :], start=True, stop=True)
                    mm.then_inc(ii_done, 1)

                def k_rows(s):
                    n = u_steps.index(s)
                    c = steps[s][1]
                    cs = slice(c * P, (c + 1) * P)
                    for half in range(2):
                        if 2 * n + half >= 1:
                            pe.wait_ge(ktok_ready, 2 * n + half)
                        for j in range(4):
                            mm = pe.transpose(ps[:, 7, j * P:(j + 1) * P], qk[:, H + 4 * half + j, cs], self.ident[:])
                        mm.then_inc(ktr_done, 1)

                def update(s, p):
                    n = u_at[(s, p)]
                    us = u_steps.index(s)
                    if n >= 1:
                        pe.wait_ge(ct_ready, 2 * n)
                    pe.wait_ge(ktok_ready, 2 * us + p // 2 + 1)
                    pe.wait_ge(vw_ready, us + 1)
                    for j in range(2):
                        h = 2 * p + j
                        mm = pe.matmul(ps[:, 6, j * E_H:(j + 1) * E_H], ktok[:, us % 2, h * P:(h + 1) * P], vw[:, us % 2, h, :], start=True, stop=True)
                    mm.then_inc(upd_done, 1)

                nxt = {slots[i]: slots[i + 1] for i in range(len(slots) - 1)}
                if slots[0] in h_at:
                    scores(*slots[0])
                for slot in slots:
                    s, p = slot
                    if p == 0 and s in u_steps:
                        k_rows(s)
                    if nxt.get(slot) in h_at:
                        scores(*nxt[slot])
                    if slot in h_at:
                        outputs(s, p)
                    if slot in u_at:
                        update(s, p)

            @block.scalar
            def _(act):
                def exps(s, p):
                    n = h_at[(s, p)]
                    d, c = steps[s][:2]
                    act.wait_ge(sb_done, n + 1)
                    if n >= 2:
                        act.wait_ge(p_ready, n - 1)
                    for j in range(2):
                        r = ROW0[d] + 2 * p + j
                        act.activation(ex[:, n % 2, j, :], ps[:, n % 2, (2 + j) * P:(3 + j) * P], ACT.Exp,
                                       bias=tok[:, c, 3, r:r + 1]).then_inc(exp_done, 1)

                def inter(s, p):
                    n = h_at[(s, p)]
                    d, c = steps[s][:2]
                    act.wait_ge(ii_done, n + 1)
                    if n >= 2:
                        act.wait_ge(num_ready, n - 1)
                    for j in range(2):
                        r = ROW0[d] + 2 * p + j
                        act.activation(iv[:, n % 2, j, :], ps[:, 4 + n % 2, j * E_H:(j + 1) * E_H], ACT.Copy,
                                       scale=tok[:, c, 0, r:r + 1]).then_inc(iv_ready, 1)

                nxt = {slots[i]: slots[i + 1] for i in range(len(slots) - 1)}
                if slots[0] in h_at:
                    exps(*slots[0])
                for slot in slots:
                    s, p = slot
                    if p == 0 and s in u_steps:
                        us = u_steps.index(s)
                        if us >= 2:
                            act.wait_ge(upd_done, NP_ * (us - 1))
                        for half in range(2):
                            act.wait_ge(ktr_done, 2 * us + half + 1)
                            act.activation(ktok[:, us % 2, half * BANK:(half + 1) * BANK], ps[:, 7, :], ACT.Copy).then_inc(ktok_ready, 1)
                    if nxt.get(slot) in h_at:
                        exps(*nxt[slot])
                    if slot in h_at:
                        inter(s, p)

            @block.vector
            def _(ve):
                ve.wait_ge(zeroed, 2)

                def weights(s, p):
                    n = h_at[(s, p)]
                    ve.wait_ge(exp_done, 2 * (n + 1))
                    if n >= 2:
                        ve.wait_ge(ii_done, n - 1)
                    ve.scalar_tensor_tensor(out=pt[:, n % 2], in0=ps[:, n % 2, 0:2 * P].rearrange("p (j t) -> p j t", j=2), scalar=QSCALE,
                                            in1=ex[:, n % 2], op0=ALU.mult, op1=ALU.mult).then_inc(p_ready, 1)

                def sums(s, p):
                    n = h_at[(s, p)]
                    hs = h_steps.index(s)
                    if hs >= 2 and p == 0:
                        ve.wait_ge(fin, fin_upto[h_steps[hs - 2]])
                    ve.wait_ge(iv_ready, 2 * (n + 1))
                    ve.tensor_tensor(out=num[:, hs % 2, 2 * p:2 * p + 2, :], in0=ps[:, 2 + n % 2, 0:2 * E_H].rearrange("p (j t) -> p j t", j=2),
                                     in1=iv[:, n % 2], op=ALU.add).then_inc(num_ready, 1)

                def new_state(s, p):
                    n = u_at[(s, p)]
                    d, c = steps[s][:2]
                    ve.wait_ge(upd_done, n + 1)
                    if (s, p) in h_at:
                        ve.wait_ge(ii_done, h_at[(s, p)] + 1)
                    if ct_needed(s, p):
                        ve.wait_ge(ct_ready, 2 * ct_needed(s, p))
                    for j in range(2):
                        h = 2 * p + j
                        r = ROW0[d] + h
                        ve.scalar_tensor_tensor(out=state[:, d, h, :], in0=state[:, d, h, :], scalar=alast[:, c, r:r + 1],
                                                in1=ps[:, 6, j * E_H:(j + 1) * E_H], op0=ALU.mult, op1=ALU.add).then_inc(ct_ready, 1)

                def finish(s):
                    d, c = steps[s][:2]
                    hs = h_steps.index(s)
                    base = fin_upto[s] - fin_len[s]
                    nb = num[:, hs % 2]
                    ve.wait_ge(num_ready, NP_ * (hs + 1))
                    if base:
                        ve.wait_ge(fin, base)
                    ve.scalar_tensor_tensor(out=den[:, 0], in0=nb[:, :, P], scalar=-1.0, in1=nb[:, :, P], op0=ALU.mult, op1=ALU.max).then_inc(fin, 1)
                    ve.wait_ge(fin, base + 1)
                    ve.tensor_tensor(out=den[:, 1], in0=den[:, 0], in1=tok[:, c, 1, ROW0[d]:ROW0[d] + H], op=ALU.max).then_inc(fin, 1)
                    ve.wait_ge(fin, base + 2)
                    ve.reciprocal(den[:, 2], den[:, 1]).then_inc(fin, 1)
                    ve.wait_ge(fin, base + 3)
                    dst = hsum[:, c].rearrange("p (h e) -> p h e", h=H)
                    first = first_visit[s]
                    ve.tensor_tensor(out=dst if first else hb[:], in0=nb[:, :, 0:P], in1=den[:, 2].unsqueeze(2).broadcast_to((P, H, P)),
                                     op=ALU.mult).then_inc(fin, 1)
                    if not first:
                        ve.wait_ge(fin, base + 4)
                        ve.tensor_tensor(out=dst, in0=dst, in1=hb[:], op=ALU.add).then_inc(fin, 1)

                nxt = {slots[i]: slots[i + 1] for i in range(len(slots) - 1)}
                if slots[0] in h_at:
                    weights(*slots[0])
                for slot in slots:
                    s, p = slot
                    if nxt.get(slot) in h_at:
                        weights(*nxt[slot])
                    if slot in h_at:
                        sums(s, p)
                    if slot in u_at:
                        new_state(s, p)
                    if p == NP_ - 1 and s in h_steps:
                        finish(s)

    def merge_branch(self, l, w_p, c_gate, k_bias, hT, brT, merged, t0, add, h_hi, h_lo, b_lo):
        nc, a, ps = self.nc, self.a, self.ps
        ctx, sb, sem = self.scope()
        UN = 2
        w_l = a["w_in"][l]
        pieces = [(0, CTX), (CTX, T)] if t0 == 0 else [(CTX, T)]
        npc = len(pieces)
        c_in = slice(0 if t0 == 0 else CTX, T)
        with ctx:
            wp = sb("wp", [P, KD, P])
            wg = sb("wg", [P, KD, P])
            wp_hi, wp_lo, wg_hi, wg_lo = (sb(n, [P, KD, P], F32R) for n in ("wp_hi", "wp_lo", "wg_hi", "wg_lo"))
            b_hi = sb("b_hi", [P, KD, T], F32R)
            sg = sb("sg", [P, UN, T])
            pr = sb("pr", [P, T])
            mark = sb("mark", [P, 1])
            g_in, p_in, seen = sem("g_in"), sem("p_in"), sem("seen")
            g_hi_ready, g_split, p_hi_ready, p_split = sem("g_hi_ready"), sem("g_split"), sem("p_hi_ready"), sem("p_split")
            x_hi_ready, x_split = sem("x_hi_ready"), sem("x_split")
            g_done, w_used, gated, merged_up = sem("g_done"), sem("w_used"), sem("gated"), sem("merged_up")
            PER = npc * (2 if add else 1)
            block = ctx.enter_context(nc.Block())

            @block.sync
            def _(sp):
                def load(n):
                    sp.dma_start(wg[:], wcols_dyn(w_l, n * P + c_gate, P)).then_inc(g_in, 16)
                    sp.dma_start(wp[:], wcols_dyn(w_p, n * P, P)).then_inc(p_in, 16)
                load(0)
                with sp.Fori(1, KD) as n:
                    sp.wait_ge(p_split, n)
                    load(n)

            @block.gpsimd
            def _(gp):
                gp.memset(pr[:], 0.0).then_inc(merged_up, UN * PER)
                gp.memset(sg[:], 0.0).then_inc(g_done, 1)
                gp.memset(mark[:], 0.0).then_inc(w_used, 1)
                with gp.Fori(0, KD) as n:
                    for w, hi, lo, w_in, used, hi_ready, split in (
                            (wg, wg_hi, wg_lo, g_in, g_done, g_hi_ready, g_split),
                            (wp, wp_hi, wp_lo, p_in, w_used, p_hi_ready, p_split)):
                        gp.wait_ge(w_in, n * 16 + 16)
                        gp.wait_ge(used, n + 1)
                        gp.sem_inc(seen, 1)
                        gp.tensor_copy(hi[:], w[:]).then_inc(hi_ready, 1)
                        gp.wait_ge(hi_ready, n + 1)
                        gp.tensor_tensor(out=lo[:], in0=w[:], in1=hi[:].bitcast(F32), op=ALU.subtract).then_inc(split, 1)

            @block.tensor
            def _(pe):
                with pe.Fori(0, KD // UN) as i:
                    for u in range(UN):
                        pe.wait_ge(merged_up, i * (UN * PER) + (u + 1) * PER)
                        for hi, lo, x_hi, x_lo, o, split, x_parts, done in (
                                (wg_hi, wg_lo, h_hi, h_lo, 0, g_split, KD, g_done), (wp_hi, wp_lo, b_hi, b_lo, 2, p_split, 2 * KD, w_used)):
                            pe.wait_ge(x_split, x_parts)
                            pe.wait_ge(split, i * UN + (u + 1))
                            for q, (c0, c1) in enumerate(pieces):
                                mm = split_product(pe, ps[:, 4 * u + o + q, 0:c1 - c0], hi, lo, x_hi[:, :, c0:c1], x_lo[:, :, c0:c1])
                            mm.then_inc(done, 1)

            @block.scalar
            def _(act):
                for x, hi in ((hT, h_hi), (brT, b_hi)):
                    for k in range(KD):
                        act.activation(hi[:, k, c_in], x[:, k, c_in], ACT.Copy).then_inc(x_hi_ready, 1)
                with act.Fori(0, KD // UN) as i:
                    for u in range(UN):
                        act.wait_ge(g_done, i * UN + u + 2)
                        act.wait_ge(merged_up, i * (UN * PER) + (u + 1) * PER)
                        for q, (c0, c1) in enumerate(pieces):
                            act.activation(sg[:, u, c0:c1], ps[:, 4 * u + q, 0:c1 - c0], ACT.Sigmoid,
                                           bias=self.cols[:, l, bass.ds(i * UN + (k_bias + u), 1)]).then_inc(gated, 1)

            @block.vector
            def _(ve):
                n = 0
                for x, hi, lo in ((hT, h_hi, h_lo), (brT, b_hi, b_lo)):
                    for k in range(KD):
                        n += 1
                        ve.wait_ge(x_hi_ready, n)
                        ve.tensor_tensor(out=lo[:, k, c_in], in0=x[:, k, c_in], in1=hi[:, k, c_in].bitcast(F32), op=ALU.subtract).then_inc(x_split, 1)
                with ve.Fori(0, KD // UN) as i:
                    for u in range(UN):
                        ve.wait_ge(w_used, i * UN + u + 2)
                        ve.wait_ge(gated, i * (UN * npc) + npc * (u + 1))
                        ve.wait_ge(merged_up, i * (UN * PER) + (u + UN) * PER)
                        for q, (c0, c1) in enumerate(pieces):
                            g, p = sg[:, u, c0:c1].unsqueeze(1), ps[:, 4 * u + 2 + q, 0:c1 - c0].unsqueeze(1)
                            dst = merged[:, bass.ds(i * UN + u, 1), c0:c1]
                            if add:
                                ve.tensor_tensor(out=pr[:, c0:c1].unsqueeze(1), in0=p, in1=g, op=ALU.mult).then_inc(merged_up, 1)
                            else:
                                ve.tensor_tensor(out=dst, in0=p, in1=g, op=ALU.mult).then_inc(merged_up, 1)
                        if add:
                            ve.wait_ge(merged_up, i * (UN * PER) + (UN * PER + u * PER + npc))
                            for q, (c0, c1) in enumerate(pieces):
                                dst = merged[:, bass.ds(i * UN + u, 1), c0:c1]
                                ve.tensor_tensor(out=dst, in0=dst, in1=pr[:, c0:c1].unsqueeze(1), op=ALU.add).then_inc(merged_up, 1)

    def load_groups(self, sp, sources, wt, w_in, mm_done, nt):
        for g, src in enumerate(sources):
            if g >= 2:
                sp.wait_ge(mm_done, (g - 1) * nt)
            for half in range(2):
                k0 = half * KD // 2
                sp.dma_start(wt[:, g % 2, k0:k0 + KD // 2, :],
                             src[k0 * P:(k0 + KD // 2) * P, :].rearrange("(k p) n -> p k n", p=P)).then_inc(w_in[g % 2], 16)

    def output_gate(self, l, hT, hs, other, brT, tiles):
        nc, a, ps = self.nc, self.a, self.ps
        ctx, sb, sem = self.scope()
        nt = len(tiles)
        N = 2 * nt
        gain = self.cols[:, l, K_MN:K_MN + KD]
        with ctx:
            wt = sb("wt", [P, 2, KD, BANK])
            stats = sb("stats", [P, NT, H, 6])
            mv = sb("mv", [P, NT, H, 2])
            sd = sb("sd", [P, NT, H])
            rs = sb("rs", [P, NT, H])
            w_in = [sem(f"w_in{s}") for s in range(2)]
            mm_done, gate_ready, stat_done, rooted, inverted, scaled, gated, turned, turn_out = (
                sem(n) for n in ("mm_done", "gate_ready", "stat_done", "rooted", "inverted", "scaled", "gated", "turned", "turn_out"))
            block = ctx.enter_context(nc.Block())

            @block.sync
            def _(sp):
                w_l = a["w_in"][l]
                self.load_groups(sp, [w_l[:, C_O + g * BANK:C_O + (g + 1) * BANK] for g in range(2)], wt, w_in, mm_done, nt)

            @block.tensor
            def _(pe):
                for n in range(N + 1):
                    if n < N:
                        g, t = n // nt, tiles[n % nt]
                        if n % nt == 0:
                            pe.wait_ge(w_in[g % 2], 32)
                        if n >= 4:
                            pe.wait_ge(gate_ready, n - 3)
                        for k in range(KD):
                            mm = pe.matmul(ps[:, n % 4, :], hT[:, k, t * P:(t + 1) * P], wt[:, g % 2, k, :], start=(k == 0), stop=(k == KD - 1))
                        mm.then_inc(mm_done, 1)
                    if n >= 1:
                        m = n - 1
                        g, t = m // nt, tiles[m % nt]
                        pe.wait_ge(gated, m + 1)
                        if m >= 2:
                            pe.wait_ge(turn_out, 4 * (m - 1))
                        for j in range(4):
                            c0 = g * BANK + j * P
                            mm = pe.transpose(ps[:, 4 + m % 2, j * P:(j + 1) * P], hs[:, t, c0:c0 + P], self.ident[:])
                        mm.then_inc(turned, 1)

            @block.scalar
            def _(act):
                for n in range(N + 1):
                    if n < nt:
                        act.wait_ge(stat_done, (n + 1) * 2 * H)
                        act.activation(sd[:, n], mv[:, n, :, 1], ACT.Sqrt, bias=self.eps[:, 0:1]).then_inc(rooted, 1)
                    if n < N:
                        g, t = n // nt, tiles[n % nt]
                        act.wait_ge(mm_done, n + 1)
                        act.activation(other[:, t, g * BANK:(g + 1) * BANK], ps[:, n % 4, :], ACT.Sigmoid).then_inc(gate_ready, 1)
                    if n >= 1:
                        m = n - 1
                        g, t = m // nt, tiles[m % nt]
                        act.wait_ge(turned, m + 1)
                        for j in range(4):
                            k = 4 * g + j
                            act.activation(brT[:, k, t * P:(t + 1) * P], ps[:, 4 + m % 2, j * P:(j + 1) * P], ACT.Copy,
                                           scale=gain[:, k:k + 1]).then_inc(turn_out, 1)

            @block.vector
            def _(ve):
                for i, t in enumerate(tiles):
                    for h in range(H):
                        ve.bn_stats(stats[:, i, h, :], hs[:, t, h * P:(h + 1) * P]).then_inc(stat_done, 1)
                    ve.wait_ge(stat_done, i * 2 * H + H)
                    for h in range(H):
                        ve.bn_aggr(mv[:, i, h, :], stats[:, i, h]).then_inc(stat_done, 1)
                ve.wait_ge(stat_done, nt * 2 * H)
                for n in range(N):
                    g, i, t = n // nt, n % nt, tiles[n % nt]
                    if g == 0:
                        ve.wait_ge(rooted, i + 1)
                        ve.reciprocal(rs[:, i], sd[:, i]).then_inc(inverted, 1)
                        ve.wait_ge(inverted, i + 1)
                    for h in range(4 * g, 4 * g + 4):
                        xs = hs[:, t, h * P:(h + 1) * P]
                        ve.tensor_scalar(xs, xs, mv[:, i, h, 0:1], rs[:, i, h:h + 1], ALU.subtract, ALU.mult).then_inc(scaled, 1)
                    ve.wait_ge(scaled, 4 * (n + 1))
                    ve.wait_ge(gate_ready, n + 1)
                    xs = hs[:, t, g * BANK:(g + 1) * BANK]
                    ve.tensor_tensor(out=xs, in0=xs, in1=other[:, t, g * BANK:(g + 1) * BANK], op=ALU.mult).then_inc(gated, 1)

    def spatial_branch(self, l, hT, zv, gu, brT, tiles):
        nc, a, ps = self.nc, self.a, self.ps
        ctx, sb, sem = self.scope()
        nt = len(tiles)
        V = 2 * nt
        N = 2 * V
        w_l = a["w_in"][l]
        with ctx:
            wt = sb("wt", [P, 2, KD, BANK])
            ws = sb("ws", [P, H, P])
            wsT = sb("wsT", [P, H, P])
            gain = sb("gain", [P, D])
            stats = sb("stats", [P, NT, 2, 6])
            mv = sb("mv", [P, NT, 2])
            sd = sb("sd", [P, NT])
            rs = sb("rs", [P, NT])
            w_in = [sem(f"w_in{s}") for s in range(2)]
            ws_in, gain_in, ws_turned, ws_ready = sem("ws_in"), sem("gain_in"), sem("ws_turned"), sem("ws_ready")
            mm_done, gelu_done, stat_done, mean_done, rooted, scaled, mixed, gated, turned, turn_out = (
                sem(n) for n in ("mm_done", "gelu_done", "stat_done", "mean_done", "rooted", "scaled", "mixed", "gated", "turned", "turn_out"))
            block = ctx.enter_context(nc.Block())

            @block.sync
            def _(sp):
                self.load_groups(sp, [w_l[:, c0 + g * BANK:c0 + (g + 1) * BANK] for c0 in (C_VG, C_U) for g in range(2)],
                                 wt, w_in, mm_done, nt)

            @block.gpsimd
            def _(gp):
                gp.dma_start(ws[:], a["sgu_w"][l].rearrange("g p q -> p g q")).then_inc(ws_in, 16)
                gp.dma_start(gain[:], a["sgu_norm_w"][l:l + 1, :].broadcast_to((P, D))).then_inc(gain_in, 16)

            @block.tensor
            def _(pe):
                pe.wait_ge(ws_in, 16)
                for g in range(H):
                    mm = pe.transpose(ps[:, 4 + g // 4, (g % 4) * P:(g % 4 + 1) * P], ws[:, g, :], self.ident[:])
                mm.then_inc(ws_turned, 1)
                for n in range(N + 2):
                    if n < N:
                        g, t = n // nt, tiles[n % nt]
                        if n % nt == 0:
                            pe.wait_ge(w_in[g % 2], 32 * (g // 2 + 1))
                        if n >= 4:
                            pe.wait_ge(gelu_done, n - 3)
                        for k in range(KD):
                            mm = pe.matmul(ps[:, n % 4, :], hT[:, k, t * P:(t + 1) * P], wt[:, g % 2, k, :], start=(k == 0), stop=(k == KD - 1))
                        mm.then_inc(mm_done, 1)
                    m = n - V - 1
                    if 0 <= m < V:
                        half, i, t = m // nt, m % nt, tiles[m % nt]
                        if m == 0:
                            pe.wait_ge(ws_ready, 2)
                        pe.wait_ge(scaled, 3 * (i + 1))
                        if m >= 2:
                            pe.wait_ge(gated, 4 * (m - 1))
                        for j in range(4):
                            g = 4 * half + j
                            mm = pe.matmul(ps[:, 4 + m % 2, j * P:(j + 1) * P], wsT[:, g, :], zv[:, t, g * P:(g + 1) * P], start=True, stop=True)
                        mm.then_inc(mixed, 1)
                    m = n - V - 2
                    if 0 <= m < V:
                        half, t = m // nt, tiles[m % nt]
                        pe.wait_ge(gated, 4 * (m + 1))
                        if m >= 2:
                            pe.wait_ge(turn_out, 4 * (m - 1))
                        for j in range(4):
                            c0 = half * BANK + j * P
                            mm = pe.transpose(ps[:, 6 + m % 2, j * P:(j + 1) * P], gu[:, t, c0:c0 + P], self.ident[:])
                        mm.then_inc(turned, 1)

            @block.scalar
            def _(act):
                for n in range(N + 2):
                    i = n - 2 - nt
                    if 0 <= i < nt:
                        act.wait_ge(mean_done, i + 1)
                        act.activation(sd[:, i:i + 1], mv[:, i, 1:2], ACT.Sqrt, bias=self.eps[:, 0:1]).then_inc(rooted, 1)
                    if n < N:
                        half, t = (n // nt) % 2, tiles[n % nt]
                        dst = zv if n < V else gu
                        act.wait_ge(mm_done, n + 1)
                        act.activation(dst[:, t, half * BANK:(half + 1) * BANK], ps[:, n % 4, :], ACT.Gelu_apprx_tanh).then_inc(gelu_done, 1)
                    m = n - V - 2
                    if 0 <= m < V:
                        half, t = m // nt, tiles[m % nt]
                        act.wait_ge(turned, m + 1)
                        for j in range(4):
                            act.activation(brT[:, 4 * half + j, t * P:(t + 1) * P], ps[:, 6 + m % 2, j * P:(j + 1) * P], ACT.Copy).then_inc(turn_out, 1)

            @block.vector
            def _(ve):
                ve.wait_ge(ws_turned, 1)
                for j in range(2):
                    ve.tensor_copy(wsT[:, 4 * j:4 * j + 4, :], ps[:, 4 + j, :].rearrange("p (g q) -> p g q", g=4)).then_inc(ws_ready, 1)
                ve.wait_ge(gain_in, 16)
                for n in range(N + 1):
                    if n < V:
                        half, i, t = n // nt, n % nt, tiles[n % nt]
                        ve.wait_ge(gelu_done, n + 1)
                        if half == 0:
                            ve.bn_stats(stats[:, i, 0, :], zv[:, t, 0:BANK]).then_inc(stat_done, 1)
                        else:
                            ve.bn_stats(stats[:, i, 1, :], zv[:, t, BANK:D]).then_inc(stat_done, 1)
                            ve.wait_ge(stat_done, n + 1)
                            ve.bn_aggr(mv[:, i, :], stats[:, i]).then_inc(mean_done, 1)
                    i = n - 3 - nt
                    if 0 <= i < nt:
                        t = tiles[i]
                        ve.wait_ge(rooted, i + 1)
                        ve.reciprocal(rs[:, i:i + 1], sd[:, i:i + 1]).then_inc(scaled, 1)
                        ve.wait_ge(scaled, 3 * i + 1)
                        ve.tensor_scalar(zv[:, t, :], zv[:, t, :], mv[:, i, 0:1], rs[:, i:i + 1], ALU.subtract, ALU.mult).then_inc(scaled, 1)
                        ve.wait_ge(scaled, 3 * i + 2)
                        ve.tensor_tensor(out=zv[:, t, :], in0=zv[:, t, :], in1=gain[:], op=ALU.mult).then_inc(scaled, 1)
                    m = n - V - 1
                    if 0 <= m < V:
                        half, t = m // nt, tiles[m % nt]
                        ve.wait_ge(mixed, m + 1)
                        ve.wait_ge(gelu_done, V + m + 1)
                        for j in range(4):
                            g = 4 * half + j
                            dst = gu[:, t, g * P:(g + 1) * P]
                            ve.scalar_tensor_tensor(out=dst, in0=ps[:, 4 + m % 2, j * P:(j + 1) * P], scalar=self.cols[:, l, K_SB + g:K_SB + g + 1],
                                                    in1=dst, op0=ALU.add, op1=ALU.mult).then_inc(gated, 1)

    def output_norm(self, l, merged, y, tiles):
        nc, a, ps, z = self.nc, self.a, self.ps, self.z
        ctx, sb, sem = self.scope()
        nt = len(tiles)
        N = 2 * nt
        with ctx:
            wt = sb("wt", [P, 2, KD, BANK])
            gate = sb("gate", [P, 2, D])
            lw = sb("lw", [P, D])
            lb = sb("lb", [P, D])
            stats = sb("stats", [P, NT, 2, 6])
            mv = sb("mv", [P, NT, 2])
            sd = sb("sd", [P, NT])
            rs = sb("rs", [P, NT])
            w_in = [sem(f"w_in{s}") for s in range(2)]
            rows_in, mm_done, gate_used, summed, stat_done, mean_done, rooted, scaled, z_ready = (
                sem(n) for n in ("rows_in", "mm_done", "gate_used", "summed", "stat_done", "mean_done", "rooted", "scaled", "z_ready"))
            block = ctx.enter_context(nc.Block())

            @block.sync
            def _(sp):
                self.load_groups(sp, [a["w_out"][l][:, g * BANK:(g + 1) * BANK] for g in range(2)], wt, w_in, mm_done, nt)
                for w in range(2):
                    sp.dma_start(gate[:, w, :], self.mod_dram[l, w:w + 1, 2 * D:3 * D].broadcast_to((P, D))).then_inc(rows_in, 16)
                sp.dma_start(lw[:], a["ln_w"][l, 0:1, :].broadcast_to((P, D))).then_inc(rows_in, 16)
                sp.dma_start(lb[:], a["ln_b"][l, 0:1, :].broadcast_to((P, D))).then_inc(rows_in, 16)

            @block.tensor
            def _(pe):
                for n in range(N):
                    g, t = n // nt, tiles[n % nt]
                    if n % nt == 0:
                        pe.wait_ge(w_in[g % 2], 32)
                    if n >= 8:
                        pe.wait_ge(gate_used, n - 7)
                    for k in range(KD):
                        mm = pe.matmul(ps[:, n % 8, :], merged[:, k, t * P:(t + 1) * P], wt[:, g % 2, k, :], start=(k == 0), stop=(k == KD - 1))
                    mm.then_inc(mm_done, 1)

            @block.gpsimd
            def _(gp):
                gp.wait_ge(rows_in, 64)
                for n, t in enumerate(tiles):
                    gp.wait_ge(scaled, 2 * (n + 1))
                    gp.tensor_tensor(out=z[:, t, :], in0=z[:, t, :], in1=lw[:], op=ALU.mult).then_inc(z_ready, 1)
                    gp.wait_ge(z_ready, 2 * n + 1)
                    gp.tensor_tensor(out=z[:, t, :], in0=z[:, t, :], in1=lb[:], op=ALU.add).then_inc(z_ready, 1)

            @block.scalar
            def _(act):
                for i in range(nt):
                    act.wait_ge(mean_done, i + 1)
                    act.activation(sd[:, i:i + 1], mv[:, i, 1:2], ACT.Sqrt, bias=self.eps[:, 0:1]).then_inc(rooted, 1)

            @block.vector
            def _(ve):
                ve.wait_ge(rows_in, 64)

                def scale(i):
                    t = tiles[i]
                    ve.wait_ge(rooted, i + 1)
                    ve.reciprocal(rs[:, i:i + 1], sd[:, i:i + 1]).then_inc(scaled, 1)
                    ve.wait_ge(scaled, 2 * i + 1)
                    ve.tensor_scalar(z[:, t, :], z[:, t, :], mv[:, i, 0:1], rs[:, i:i + 1], ALU.subtract, ALU.mult).then_inc(scaled, 1)

                for n in range(N):
                    g, i, t = n // nt, n % nt, tiles[n % nt]
                    half = slice(g * BANK, (g + 1) * BANK)
                    ve.wait_ge(mm_done, n + 1)
                    ve.tensor_tensor(out=y[:, t, half], in0=ps[:, n % 8, :], in1=gate[:, 1 if t < CT else 0, half], op=ALU.mult).then_inc(gate_used, 1)
                    ve.wait_ge(gate_used, n + 1)
                    ve.scalar_tensor_tensor(out=z[:, t, half], in0=z[:, t, half], scalar=ALPHA, in1=y[:, t, half], op0=ALU.mult, op1=ALU.add).then_inc(summed, 1)
                    ve.wait_ge(summed, n + 1)
                    ve.bn_stats(stats[:, i, g, :], z[:, t, half]).then_inc(stat_done, 1)
                    if g:
                        ve.wait_ge(stat_done, n + 1)
                        ve.bn_aggr(mv[:, i, :], stats[:, i]).then_inc(mean_done, 1)
                        if i:
                            scale(i - 1)
                scale(nt - 1)

    def residual_norm(self, l, which, m_gate, y, tiles):
        nc, a, z = self.nc, self.a, self.z
        ctx, sb, sem = self.scope()
        with ctx:
            gate = sb("gate", [P, 2, D])
            lw = sb("lw", [P, D])
            lb = sb("lb", [P, D])
            stats = sb("stats", [P, 2, 2, 6])
            mv = sb("mv", [P, NT, 2])
            sd = sb("sd", [P, NT])
            rs = sb("rs", [P, NT])
            gate_in, rows_in, gated, summed, stat_done, mean_done, rooted, scaled, z_ready, stored = (
                sem(n) for n in ("gate_in", "rows_in", "gated", "summed", "stat_done", "mean_done", "rooted", "scaled", "z_ready", "stored"))
            block = ctx.enter_context(nc.Block())

            @block.sync
            def _(sp):
                for w in range(2):
                    sp.dma_start(gate[:, w, :], self.mod_dram[l, w:w + 1, m_gate * D:(m_gate + 1) * D].broadcast_to((P, D))).then_inc(gate_in, 16)
                sp.dma_start(lw[:], a["ln_w"][l, which:which + 1, :].broadcast_to((P, D))).then_inc(rows_in, 16)
                sp.dma_start(lb[:], a["ln_b"][l, which:which + 1, :].broadcast_to((P, D))).then_inc(rows_in, 16)
                if l == DEPTH - 1:
                    for n, t in enumerate(tiles):
                        sp.wait_ge(z_ready, 2 * (n + 1))
                        sp.dma_start(self.out[0, (t - CT) * P:(t - CT + 1) * P, :], z[:, t, :]).then_inc(stored, 16)
                    sp.wait_ge(stored, 16 * len(tiles))

            @block.gpsimd
            def _(gp):
                gp.wait_ge(rows_in, 32)
                for n, t in enumerate(tiles):
                    gp.wait_ge(scaled, 2 * (n + 1))
                    gp.tensor_tensor(out=z[:, t, :], in0=z[:, t, :], in1=lw[:], op=ALU.mult).then_inc(z_ready, 1)
                    gp.wait_ge(z_ready, 2 * n + 1)
                    gp.tensor_tensor(out=z[:, t, :], in0=z[:, t, :], in1=lb[:], op=ALU.add).then_inc(z_ready, 1)

            @block.scalar
            def _(act):
                for n, t in enumerate(tiles):
                    act.wait_ge(mean_done, n + 1)
                    act.activation(sd[:, t:t + 1], mv[:, t, 1:2], ACT.Sqrt, bias=self.eps[:, 0:1]).then_inc(rooted, 1)

            @block.vector
            def _(ve):
                ve.wait_ge(gate_in, 32)

                def scale(n):
                    t = tiles[n]
                    ve.wait_ge(rooted, n + 1)
                    ve.reciprocal(rs[:, t:t + 1], sd[:, t:t + 1]).then_inc(scaled, 1)
                    ve.wait_ge(scaled, 2 * n + 1)
                    ve.tensor_scalar(z[:, t, :], z[:, t, :], mv[:, t, 0:1], rs[:, t:t + 1], ALU.subtract, ALU.mult).then_inc(scaled, 1)

                def weight(n):
                    t = tiles[n]
                    ve.tensor_tensor(out=y[:, t, :], in0=y[:, t, :], in1=gate[:, 1 if t < CT else 0, :], op=ALU.mult).then_inc(gated, 1)

                weight(0)
                for n, t in enumerate(tiles):
                    if n + 1 < len(tiles):
                        weight(n + 1)
                    ve.wait_ge(gated, n + 1)
                    ve.scalar_tensor_tensor(out=z[:, t, :], in0=z[:, t, :], scalar=ALPHA, in1=y[:, t, :], op0=ALU.mult, op1=ALU.add).then_inc(summed, 1)
                    if n:
                        scale(n - 1)
                    ve.wait_ge(summed, n + 1)
                    for half in range(2):
                        ve.bn_stats(stats[:, n % 2, half, :], z[:, t, half * BANK:(half + 1) * BANK]).then_inc(stat_done, 1)
                    ve.wait_ge(stat_done, 2 * (n + 1))
                    ve.bn_aggr(mv[:, t, :], stats[:, n % 2]).then_inc(mean_done, 1)
                scale(len(tiles) - 1)

    def queries(self, l, hi, lo, qT, kT, t0):
        nc, a, ps = self.nc, self.a, self.ps
        ctx, sb, sem = self.scope()
        UN = 4
        NG = 2 * H
        pieces = [(0, CTX), (CTX, T)] if t0 == 0 else [(CTX, T)]
        npc = len(pieces)
        with ctx:
            wt = sb("wt", [P, UN, KD, P])
            w_hi = sb("w_hi", [P, 2, KD, P], F32R)
            w_lo = sb("w_lo", [P, 2, KD, P], F32R)
            w_hi_ready, w_split = sem("w_hi_ready"), sem("w_split")
            spare = sb("spare", [P, 1])
            keys = sb("keys", [P, NG, P])
            w_in = [sem(f"w_in{u}") for u in range(UN)]
            k_in, k_turned, w_used, q_out = sem("k_in"), sem("k_turned"), sem("w_used"), sem("q_out")
            k_out = sem("k_out")
            block = ctx.enter_context(nc.Block())

            @block.sync
            def _(sp):
                sp.dma_start(keys[:], a["peer_keys"][l].rearrange("h t k d -> k (h t) d")).then_inc(k_in, 16)

                def load(n, u):
                    sp.dma_start(wt[:, u], wcols_dyn(a["peer_wq"][l], n * P, P)).then_inc(w_in[u], 16)
                for u in range(UN):
                    load(u, u)
                with sp.Fori(1, NG // UN) as i:
                    for u in range(UN):
                        sp.wait_ge(w_split, i * UN + (u + 1 - UN))
                        load(i * UN + u, u)

            @block.gpsimd
            def _(gp):
                gp.memset(spare[:], 0.0).then_inc(w_used, 2)

            @block.vector
            def _(ve):
                with ve.Fori(0, NG // UN) as i:
                    for u in range(UN):
                        ve.wait_ge(w_in[u], i * 16 + 16)
                        ve.wait_ge(w_used, i * UN + (u + 1))
                        ve.tensor_copy(w_hi[:, u % 2], wt[:, u]).then_inc(w_hi_ready, 1)
                        ve.wait_ge(w_hi_ready, i * UN + (u + 1))
                        ve.tensor_tensor(out=w_lo[:, u % 2], in0=wt[:, u], in1=w_hi[:, u % 2].bitcast(F32), op=ALU.subtract).then_inc(w_split, 1)

            @block.tensor
            def _(pe):
                pe.wait_ge(k_in, 16)
                for g in range(NG):
                    mm = pe.transpose(ps[:, g // 4, (g % 4) * P:(g % 4 + 1) * P], keys[:, g, :], self.ident[:])
                    if g % 4 == 3:
                        mm.then_inc(k_turned, 1)
                pe.wait_ge(k_out, 4)
                with pe.Fori(0, NG // UN) as i:
                    for u in range(UN):
                        pe.wait_ge(w_split, i * UN + (u + 1))
                        pe.wait_ge(q_out, i * (UN * npc) + npc * (u + 1))
                        for q, (c0, c1) in enumerate(pieces):
                            mm = split_product(pe, ps[:, 2 * u + q, 0:c1 - c0], w_hi[:, u % 2], w_lo[:, u % 2], hi[:, :, c0:c1], lo[:, :, c0:c1])
                        mm.then_inc(w_used, 1)

            @block.scalar
            def _(act):
                for j in range(4):
                    act.wait_ge(k_turned, j + 1)
                    act.activation(kT[:, 4 * j:4 * j + 4, :], ps[:, j, :].rearrange("p (g q) -> p g q", g=4), ACT.Copy).then_inc(k_out, 1)
                act.wait_ge(k_out, 4)
                act.activation(keys[:, 0, :], kT[:, 0, :], ACT.Copy).then_inc(q_out, UN * npc)
                with act.Fori(0, NG // UN) as i:
                    for u in range(UN):
                        act.wait_ge(w_used, i * UN + u + 3)
                        for q, (c0, c1) in enumerate(pieces):
                            act.activation(qT[:, bass.ds(i * UN + u, 1), c0:c1], ps[:, 2 * u + q, 0:c1 - c0].unsqueeze(1), ACT.Copy).then_inc(q_out, 1)

    def modulate_rows(self, l, hx, tiles):
        nc, z = self.nc, self.z
        ctx, sb, sem = self.scope()
        with ctx:
            sh = sb("sh", [P, 2, D])
            sc = sb("sc", [P, 2, D])
            rows_in, done = sem("rows_in"), sem("done")
            block = ctx.enter_context(nc.Block())

            @block.sync
            def _(sp):
                for w in range(2):
                    sp.dma_start(sh[:, w, :], self.mod_dram[l, w:w + 1, 3 * D:4 * D].broadcast_to((P, D))).then_inc(rows_in, 16)
                    sp.dma_start(sc[:, w, :], self.mod_dram[l, w:w + 1, 4 * D:5 * D].broadcast_to((P, D))).then_inc(rows_in, 16)

            @block.vector
            def _(ve):
                ve.wait_ge(rows_in, 64)
                for n, t in enumerate(tiles):
                    w = 1 if t < CT else 0
                    ve.scalar_tensor_tensor(out=hx[:, t, :], in0=sc[:, w, :], scalar=1.0, in1=z[:, t, :], op0=ALU.add, op1=ALU.mult).then_inc(done, 1)
                    ve.wait_ge(done, 2 * n + 1)
                    ve.tensor_tensor(out=hx[:, t, :], in0=hx[:, t, :], in1=sh[:, w, :], op=ALU.add).then_inc(done, 1)

    def experts(self, l, t0, qT, kT, hx, y):
        nc, a, ps = self.nc, self.a, self.ps
        ctx, sb, sem = self.scope()
        NS = (NT - t0) * H
        AHEAD = 2
        RU, RV = 8, 4
        RD = 8
        N_STEPS = 38
        N_SOFTMAX = 3
        N_TO_EXP = 27
        tab_u, tab_v = (a[n].rearrange("l e d -> (l e) d") for n in ("expert_u", "expert_v"))
        with ctx:
            ur = sb("ur", [P, RU, D])
            vr = sb("vr", [P, RV, D])
            dots = sb("dots", [P, 2, TOPK])
            gl = sb("gl", [P, 2, TOPK])
            wt = sb("wt", [P, 2, TOPK])
            dg = sb("dg", [P, RD, P])
            icu = sb("icu", [P, 2, TOPK], U32)
            icv = sb("icv", [P, 2, TOPK], U32)
            idx = sb("idx", [P, (NS + 2) * TOPK], U32)
            gate = sb("gate", [P, NS * TOPK])
            qb = sb("qb", [P, 2, P])
            sc = sb("sc", [P, 2, P])
            sc2 = sb("sc2", [P, 2, P])
            s16 = sb("s16", [P, 2, TOPK])
            i16 = sb("i16", [P, 2, TOPK], U32)
            i16f = sb("i16f", [P, 2, TOPK])
            cand = sb("cand", [P, TOPK * TOPK])
            cand2 = sb("cand2", [P, TOPK * TOPK])
            sf = sb("sf", [P, TOPK])
            pf = sb("pf", [P, TOPK], U32)
            pij = sb("pij", [P, 2, TOPK], U32)
            pijf = sb("pijf", [P, 2, TOPK])
            hot = sb("hot", [P, 2, TOPK, TOPK])
            ids = sb("ids", [P, 2, TOPK])
            df = sb("df", [P, TOPK])
            idf = sb("idf", [P, TOPK])
            iota = sb("iota", [P, TOPK])
            sm = sb("sm", [P, 2])
            ex = sb("ex", [P, TOPK])
            mark = sb("mark", [P, 1])
            u_in = [sem(f"u_in{r}") for r in range(RU)]
            v_in = [sem(f"v_in{r}") for r in range(RV)]
            dot_done, icu_ready, icv_ready, gelu_done, w_ready, dg_ready, v_used, y_done = (
                sem(n) for n in ("dot_done", "icu_ready", "icv_ready", "gelu_done", "w_ready", "dg_ready", "v_used", "y_done"))
            set_up, q_ready, scored, picked, exped, step = (sem(n) for n in ("set_up", "q_ready", "scored", "picked", "exped", "step"))
            gathers = sem("gathers")
            block = ctx.enter_context(nc.Block())
            SEL = (NS - AHEAD) // 2

            def steps(eng, body):
                with eng.Fori(0, SEL) as i:
                    for u in range(2):
                        body(i * 2 + u, u, True)
                with eng.Fori(SEL, NS // 2) as i:
                    for u in range(2):
                        body(i * 2 + u, u, False)

            @block.gpsimd
            def _(gp):
                gp.iota(iota[:], pattern=[[1, TOPK]], base=0, channel_multiplier=0, allow_small_or_imprecise_dtypes=True).then_inc(set_up, 1)
                gp.memset(idx[:, NS * TOPK:(NS + 2) * TOPK], 0).then_inc(set_up, 1)
                gp.memset(icv[:], 0).then_inc(icv_ready, 1)
                gp.memset(wt[:], 0.0).then_inc(w_ready, 1)
                gp.memset(dg[:], 0.0).then_inc(v_used, TOPK)
                gp.wait_ge(icv_ready, 1)

                def rows_v(n, par, j):
                    gp.wait_ge(v_used, n * TOPK + (j + 1 + TOPK - RV))
                    gp.sem_inc(gathers, 1)
                    gp.indirect_dma_start(vr[:, j % RV, :], None, tab_v, bass.IndirectOffsetOnAxis(ap=icv[:, par, j:j + 1], axis=0)).then_inc(v_in[j % RV], 16)

                def body(n, u, _):
                    for j in range(TOPK):
                        if j == 0:
                            gp.wait_ge(icu_ready, n + 1)
                        gp.wait_ge(dot_done, n * TOPK + (j + 1))
                        gp.sem_inc(gathers, 1)
                        gp.indirect_dma_start(ur[:, j % RU, :], None, tab_u, bass.IndirectOffsetOnAxis(ap=icu[:, u, j:j + 1], axis=0)).then_inc(u_in[j % RU], 16)
                        if j == 0:
                            gp.wait_ge(icv_ready, n + 1)
                        rows_v(n, 1 - u, j)

                steps(gp, body)
                gp.wait_ge(icv_ready, NS + 1)
                for j in range(TOPK):
                    rows_v(NS, 1, j)

            @block.vector
            def _(ve):
                def stages(r):
                    n = 0

                    def put(ins):
                        nonlocal n
                        n += 1
                        ins.then_inc(step, 1)

                    def upto():
                        ve.wait_ge(step, r * N_STEPS + (n + 1))

                    def hold():
                        upto()
                        put(ve.memset(mark[:], 0.0))

                    def take_scores():
                        ve.wait_ge(scored, r + 1)
                        upto()
                        put(ve.tensor_copy(sc[:], ps[:, 4, 0:2 * P].rearrange("p (g k) -> p g k", g=2)))

                    def best_keys():
                        upto()
                        ve.memset(mark[:], 0.0).then_inc(picked, 1)
                        ve.wait_ge(picked, r + 2)
                        put(ve.memset(mark[:], 0.0))
                        for g in range(2):
                            put(ve.max(s16[:, g, 0:8], sc[:, g, :]))

                    def their_places():
                        hold()
                        for g in range(2):
                            put(ve.max_index(i16[:, g, 0:8], s16[:, g, 0:8], sc[:, g, :]))
                            put(ve.match_replace(sc2[:, g, :], s16[:, g, 0:8], sc[:, g, :], -3.0e38))

                    def next_keys():
                        hold()
                        for g in range(2):
                            put(ve.max(s16[:, g, 8:16], sc2[:, g, :]))

                    def next_places():
                        hold()
                        for g in range(2):
                            put(ve.max_index(i16[:, g, 8:16], s16[:, g, 8:16], sc2[:, g, :]))

                    def sums_of_halves():
                        upto()
                        put(ve.tensor_copy(i16f[:], i16[:]))
                        put(ve.tensor_tensor(out=cand[:].rearrange("p (i j) -> p i j", i=TOPK),
                                             in0=s16[:, 0, :].unsqueeze(2).broadcast_to((P, TOPK, TOPK)),
                                             in1=s16[:, 1, :].unsqueeze(1).broadcast_to((P, TOPK, TOPK)), op=ALU.add))

                    def best_pairs():
                        hold()
                        put(ve.max(sf[:, 0:8], cand[:]))

                    def their_positions():
                        hold()
                        put(ve.max_index(pf[:, 0:8], sf[:, 0:8], cand[:]))
                        put(ve.match_replace(cand2[:], sf[:, 0:8], cand[:], -3.0e38))

                    def next_pairs():
                        hold()
                        put(ve.max(sf[:, 8:16], cand2[:]))

                    def next_positions():
                        hold()
                        put(ve.max_index(pf[:, 8:16], sf[:, 8:16], cand2[:]))

                    def split_positions():
                        upto()
                        put(ve.tensor_tensor(out=df[:], in0=sf[:], in1=sf[:, 0:1].broadcast_to((P, TOPK)), op=ALU.subtract))
                        assert n == N_TO_EXP, n
                        put(ve.tensor_single_scalar(pij[:, 0, :], pf[:], 4, ALU.logical_shift_right))
                        put(ve.tensor_single_scalar(pij[:, 1, :], pf[:], TOPK - 1, ALU.bitwise_and))

                    def positions_as_floats():
                        upto()
                        put(ve.tensor_copy(pijf[:], pij[:]))

                    def one_hot():
                        upto()
                        put(ve.tensor_tensor(out=hot[:], in0=pijf[:].unsqueeze(3).broadcast_to((P, 2, TOPK, TOPK)),
                                             in1=iota[:].unsqueeze(1).unsqueeze(1).broadcast_to((P, 2, TOPK, TOPK)), op=ALU.is_equal))

                    def keys_there():
                        upto()
                        put(ve.tensor_tensor(out=hot[:], in0=hot[:], in1=i16f[:].unsqueeze(2).broadcast_to((P, 2, TOPK, TOPK)), op=ALU.mult))

                    def keys_summed():
                        upto()
                        put(ve.tensor_reduce(ids[:], hot[:], AX, ALU.add))

                    def expert_numbers():
                        upto()
                        put(ve.scalar_tensor_tensor(out=idf[:], in0=ids[:, 0, :], scalar=float(P), in1=ids[:, 1, :], op0=ALU.mult, op1=ALU.add))

                    def numbers_kept():
                        upto()
                        put(ve.tensor_scalar(idx[:, bass.ds(r * TOPK, TOPK)], idf[:], float(l * N_EXPERTS), None, ALU.add))

                    def softmax():
                        ve.wait_ge(exped, r + 1)
                        put(ve.tensor_reduce(sm[:, 0:1], ex[:], AX, ALU.add))
                        upto()
                        put(ve.reciprocal(sm[:, 1:2], sm[:, 0:1]))
                        upto()
                        put(ve.tensor_scalar(gate[:, bass.ds(r * TOPK, TOPK)], ex[:], sm[:, 1:2], None, ALU.mult))
                        assert n == N_STEPS, n

                    return [take_scores, best_keys, their_places, next_keys, next_places, sums_of_halves, best_pairs,
                            their_positions, next_pairs, next_positions, split_positions, positions_as_floats, one_hot,
                            keys_there, keys_summed, expert_numbers, numbers_kept], softmax

                ve.memset(mark[:], 0.0).then_inc(step, 1)
                ve.wait_ge(step, 1)
                ve.memset(mark[:], 0.0).then_inc(picked, 1)
                ve.wait_ge(picked, 1)
                ve.wait_ge(set_up, 2)
                for r in range(AHEAD):
                    work, last = stages(r)
                    for stage in work:
                        stage()
                    ve.wait_ge(step, (r + 1) * N_STEPS + 1 - N_SOFTMAX)
                    ve.tensor_copy(icu[:, r, :], idx[:, r * TOPK:(r + 1) * TOPK]).then_inc(icu_ready, 1)
                    if r == 0:
                        ve.memset(y[:, 0:2], 0.0).then_inc(dot_done, RU)
                        ve.memset(y[:, 2:NT + 1], 0.0).then_inc(y_done, 4)
                    last()
                ve.wait_ge(dot_done, RU)

                def body(n, u, sel):
                    work, last = stages(n + AHEAD) if sel else ([], None)
                    for j in range(TOPK):
                        ve.wait_ge(u_in[j % RU], n * (16 * (TOPK // RU)) + 16 * (j // RU + 1))
                        if j == 0:
                            ve.wait_ge(gelu_done, n + 1)
                        ve.scalar_tensor_tensor(out=ur[:, j % RU, :].unsqueeze(1), in0=ur[:, j % RU, :].unsqueeze(1), scalar=1.0,
                                                in1=hx[:, bass.ds(n // H + t0, 1), :], op0=ALU.mult, op1=ALU.mult,
                                                accum_out=dots[:, u, j:j + 1]).then_inc(dot_done, 1)
                        for stage in work[j:j + 1] if j < TOPK - 1 else work[j:]:
                            stage()
                    ve.wait_ge(dot_done, n * TOPK + (RU + TOPK))
                    ve.wait_ge(v_used, n * TOPK + TOPK)
                    ve.tensor_copy(icv[:, u, :], idx[:, bass.ds(n * TOPK, TOPK)]).then_inc(icv_ready, 1)
                    if sel:
                        ve.wait_ge(step, n * N_STEPS + (3 * N_STEPS + 1 - N_SOFTMAX))
                    else:
                        ve.wait_ge(step, NS * N_STEPS + 1)
                    ve.tensor_copy(icu[:, u, :], idx[:, bass.ds(n * TOPK + 2 * TOPK, TOPK)]).then_inc(icu_ready, 1)
                    if sel:
                        last()
                    ve.wait_ge(gelu_done, n + 3)
                    ve.tensor_tensor(out=wt[:, u, :], in0=gl[:, u, :], in1=gate[:, bass.ds(n * TOPK, TOPK)], op=ALU.mult).then_inc(w_ready, 1)
                    ve.wait_ge(v_used, n * TOPK + 2 * TOPK)
                    ve.wait_ge(y_done, n * 2 + 4)
                    for q in range(2):
                        dst = y[:, bass.ds((n + (H - 1)) // H + t0, 1), q * BANK:(q + 1) * BANK]
                        ve.tensor_tensor(out=dst, in0=ps[:, 2 * (1 - u) + q, :].unsqueeze(1), in1=dst, op=ALU.add).then_inc(y_done, 1)

                steps(ve, body)
                ve.wait_ge(v_used, (NS + 2) * TOPK)
                ve.wait_ge(y_done, 2 * NS + 4)
                for q in range(2):
                    dst = y[:, NT, q * BANK:(q + 1) * BANK]
                    ve.tensor_tensor(out=dst, in0=ps[:, 2 + q, :], in1=dst, op=ALU.add).then_inc(y_done, 1)

            @block.scalar
            def _(act):
                def query(r):
                    act.wait_ge(picked, r + 1)
                    act.activation(qb[:], qT[:, bass.ds((r % H) * 2, 2), bass.ds((r // H) * P + t0 * P, P)], ACT.Copy).then_inc(q_ready, 1)

                def exponentials(r):
                    act.wait_ge(step, r * N_STEPS + (N_TO_EXP + 1))
                    act.activation(ex[:], df[:], ACT.Exp).then_inc(exped, 1)

                with act.Fori(0, AHEAD) as r:
                    query(r)
                    exponentials(r)
                act.activation(gl[:, 0, :], self.ones[:, 0:TOPK], ACT.Copy).then_inc(gelu_done, 1)
                act.activation(gl[:, 1, :], self.ones[:, 0:TOPK], ACT.Copy).then_inc(gelu_done, 1)
                act.wait_ge(v_used, TOPK)
                act.wait_ge(gelu_done, 2)

                def diagonals(n, par):
                    act.wait_ge(w_ready, n + 1)
                    for j in range(TOPK):
                        act.wait_ge(v_used, n * TOPK + (j + 1 + TOPK - RD))
                        act.activation(dg[:, j % RD, :], self.ident[:], ACT.Copy, scale=wt[:, par, j:j + 1]).then_inc(dg_ready, 1)

                def body(n, u, sel):
                    if sel:
                        query(n + AHEAD)
                    diagonals(n, 1 - u)
                    if sel:
                        exponentials(n + AHEAD)
                    act.wait_ge(dot_done, n * TOPK + (RU + TOPK))
                    act.activation(gl[:, u, :], dots[:, u, :], ACT.Gelu_apprx_tanh).then_inc(gelu_done, 1)

                steps(act, body)
                diagonals(NS, 1)

            @block.tensor
            def _(pe):
                def scores(r):
                    pe.wait_ge(q_ready, r + 1)
                    pe.wait_ge(picked, r + 1)
                    for g in range(2):
                        mm = pe.matmul(ps[:, 4, g * P:(g + 1) * P], qb[:, g, :], kT[:, bass.ds((r % H) * 2 + g, 1), :], start=True, stop=True)
                    mm.then_inc(scored, 1)

                def head(n, par):
                    pe.wait_ge(y_done, n * 2 + 2)
                    for j in range(TOPK):
                        pe.wait_ge(dg_ready, n * TOPK + (j + 1))
                        pe.wait_ge(v_in[j % RV], n * (16 * (TOPK // RV)) + 16 * (j // RV + 1))
                        for q in range(2):
                            mm = pe.matmul(ps[:, 2 * par + q, :], dg[:, j % RD, :], vr[:, j % RV, q * BANK:(q + 1) * BANK],
                                           start=(j == 0), stop=(j == TOPK - 1))
                        mm.then_inc(v_used, 1)

                with pe.Fori(0, AHEAD) as r:
                    scores(r)

                def body(n, u, sel):
                    if sel:
                        scores(n + AHEAD)
                    head(n, 1 - u)

                steps(pe, body)
                head(NS, 1)

    def build(self):
        nc, a = self.nc, self.a
        ctx = ExitStack()
        with ctx:
            def sb(name, shape, dt=F32):
                return ctx.enter_context(nc.sbuf_tensor(name, shape, dt))

            self.ps = ctx.enter_context(nc.psum_tensor("ps", [P, 8, BANK], F32))
            self.mod_dram = nc.dram_tensor("mod_scratch", (DEPTH, 2, MODW), F32, kind="Internal").ap()
            self.z = sb("z", [P, NT, D])
            self.ident = sb("ident", [P, P])
            self.negident = sb("negident", [P, P])
            self.identb = sb("identb", [P, P], BF16)
            self.mask = sb("mask", [P, 2, 2 * P], BF16)
            self.ones = sb("ones", [P, P])
            self.eps = sb("eps", [P, 1])
            self.cols = sb("cols", [P, DEPTH, K_ALL])
            self.cond = sb("cond", [P, KD, 2])
            self.modc = sb("modc", [P, DEPTH, 2, 6, KD])
            self.setup()
            self.modulation()
            for l in range(DEPTH):
                self.layer(l)

    def layer(self, l):
        nc, a = self.nc, self.a
        t0 = 0 if l < DEPTH - 1 else CT
        tiles = list(range(t0, NT))
        w_l = a["w_in"][l]
        mix, sb, _ = self.scope()
        with mix:
            hT = sb("hT", [P, KD, T])
            hs_at = nc.sbuf_base
            hs = sb("hs", [P, NT, D])
            hi = nc.alloc_sbuf_tensor_at(f"hi_{l}", [P, KD, T], F32R, offset=hs_at)
            inner, sb2, _ = self.scope()
            with inner:
                qk = sb2("qk", [P, 2 * KD, T])
                split, sb3, _ = self.scope()
                with split:
                    lo = sb3("lo", [P, KD, T], F32R)
                    self.modulated_turn(l, 0, hT, hi, lo, 0)
                    self.project_qk(l, hi, lo, qk, t0)
                v = sb2("v", [P, NT, H, E_H])
                tok = sb2("tok", [P, NT, 4, GR])
                alast = sb2("alast", [P, NT, GR])
                self.m_rows = sb2("m_rows", [GR, T])
                self.values_and_gates(l, hT, v, tok, alast, hs)
                self.mlstm(t0, qk, v, tok, alast, hs)
            merged = sb("merged", [P, KD, T])
            brT_at = nc.sbuf_base
            brT = sb("brT", [P, KD, T])
            other_at = nc.sbuf_base
            other = sb("other", [P, NT, D])
            h_lo = nc.alloc_sbuf_tensor_at(f"h_lo_{l}", [P, KD, T], F32R, offset=other_at)
            b_lo = nc.alloc_sbuf_tensor_at(f"b_lo_{l}", [P, KD, T], F32R, offset=brT_at)
            self.output_gate(l, hT, hs, other, brT, tiles)
            self.merge_branch(l, a["p_a"][l], C_GA, K_BR, hT, brT, merged, t0, False, hi, h_lo, b_lo)
            self.spatial_branch(l, hT, hs, other, brT, tiles)
            self.merge_branch(l, a["p_b"][l], C_GB, K_BR + KD, hT, brT, merged, t0, True, hi, h_lo, b_lo)
            self.output_norm(l, merged, hs, tiles)
        peer, sb, _ = self.scope()
        with peer:
            qT = sb("qT", [P, 2 * H, T])
            kT = sb("kT", [P, 2 * H, P])
            inner, sb2, _ = self.scope()
            with inner:
                hT = sb2("hT", [P, KD, T])
                hi = sb2("hi", [P, KD, T], F32R)
                lo = sb2("lo", [P, KD, T], F32R)
                self.modulated_turn(l, 3, hT, hi, lo, t0)
                self.queries(l, hi, lo, qT, kT, t0)
            hx = sb("hx", [P, NT, D])
            y = sb("y", [P, NT + 1, D])
            self.modulate_rows(l, hx, tiles)
            self.experts(l, t0, qT, kT, hx, y)
            self.residual_norm(l, 1, 5, y[:, 1:NT + 1, :], tiles)


def split_product(pe, out, w_hi, w_lo, x_hi, x_lo):
    for k in range(KD):
        pe.matmul(out, w_hi[:, k, :], x_hi[:, k, :], start=(k == 0), stop=False)
        pe.matmul(out, w_hi[:, k, :], x_lo[:, k, :], start=False, stop=False)
        mm = pe.matmul(out, w_lo[:, k, :], x_hi[:, k, :], start=False, stop=(k == KD - 1))
    return mm


def chunk_slice(c, d):
    if d == 0:
        return slice(c * P, (c + 1) * P)
    stop = c * P - 1
    return slice((c + 1) * P - 1, stop if stop >= 0 else None, -1)


def wcols_dyn(w, c0, n):
    return w[:, bass.ds(c0, n)].rearrange("(k p) n -> p k n", p=P)


_INS = ['x', 'c', 'ctx', 'c_ctx', 'w_mod', 'b_mod', 'w_in', 'qk_conv_w', 'qk_conv_b', 'gate_b', 'mlstm_norm_w',
        'sgu_norm_w', 'sgu_w', 'sgu_b', 'branch_b', 'p_a', 'p_b', 'w_out', 'ln_w', 'ln_b', 'peer_wq', 'peer_keys',
        'expert_u', 'expert_v']
_OUTS = [((1, SEQ, D), 'float32')]


def kernel(**inputs):
    import numpy as _np
    import concourse.bacc as _bacc
    from concourse import mybir as _mybir
    from concourse.bass_utils import run_bass_kernel_spmd as _run

    nc = _bacc.Bacc("TRN2", target_bir_lowering=False, num_devices=1)
    arrays, args = {}, {}
    for name in _INS:
        a = _np.ascontiguousarray(inputs[name])
        arrays[f"in_{name}_dram"] = a
        args[name] = nc.dram_tensor(f"in_{name}_dram", a.shape, _mybir.dt.from_np(a.dtype), kind="ExternalInput").ap()
    out = nc.dram_tensor("out_0_dram", _OUTS[0][0], _mybir.dt.from_np(_np.dtype(_OUTS[0][1])), kind="ExternalOutput").ap()
    Kernel(nc, args, out).build()
    r = _run(nc, [arrays], core_ids=[0])
    return r.results[0]["out_0_dram"]
```
